# Optimizing a Trainium2 kernel written in Bass

```python
import math
import jax
import jax.numpy as jnp
from jax import lax
import numpy as np

D_MODEL = 1024
BATCH = 1
SEQ = 512
DEPTH = 2
DEC_BATCH = 8
DEC_SEQ = 4
PAST_LEN = 512
PAGE_SIZE = 128

NSA_HEADS = 8
NSA_GROUPS = 2
NSA_HPG = NSA_HEADS // NSA_GROUPS
NSA_DH = 64
NSA_WIDTH = NSA_HEADS * NSA_DH
NSA_SCALE = NSA_DH ** -0.5
CMP_LEN = 32
CMP_STRIDE = 16
CMP_RATIO = CMP_LEN // CMP_STRIDE
CMP_HID = 128
SEL_LEN = 64
SEL_TOP = 16
WINDOW = 512
SEL_QBLOCK = 64
WIN_QBLOCK = 128
HG_HEADS = 4
HG_DK = 128
HG_DV = 128
HG_WIDTH = HG_HEADS * HG_DV
HG_CHUNK = 64
REL_BUCKETS = 32
REL_MAX_DIST = 128
D_FF = 2816
N_ADA = 9
EPS = 1e-6
IN_SIZES = (NSA_WIDTH, 6 * NSA_GROUPS * NSA_DH, 3 * NSA_HEADS, HG_HEADS * HG_DK, HG_HEADS * HG_DK, HG_WIDTH, HG_WIDTH, D_MODEL, D_MODEL)
D_IN = NSA_WIDTH + 6 * NSA_GROUPS * NSA_DH + 3 * NSA_HEADS + 2 * HG_HEADS * HG_DK + 2 * HG_WIDTH + 2 * D_MODEL

kernel_name = 'nsa_hgrn2_macaron_adaln_step'

def rmsnorm(x, g):
    xf = x.astype(jnp.float32)
    y = xf * lax.rsqrt(jnp.mean(xf * xf, axis=-1, keepdims=True) + EPS)
    return (y * g.astype(jnp.float32)).astype(x.dtype)

def modulate(x, shift, scale):
    return x * (1 + scale) + shift

def swiglu(x, w_in, w_out):
    a, b = jnp.split(x @ w_in, 2, axis=-1)
    return (jax.nn.silu(a) * b) @ w_out

def rel_bucket(dist):
    n = jnp.maximum(dist, 0)
    exact = REL_BUCKETS // 2
    large = exact + (jnp.log(jnp.maximum(n, 1).astype(jnp.float32) / exact)
                     / math.log(REL_MAX_DIST / exact) * (REL_BUCKETS - exact)).astype(jnp.int32)
    return jnp.where(n < exact, n, jnp.minimum(large, REL_BUCKETS - 1))

def masked_softmax(logits, mask):
    logits = jnp.where(mask, logits, -jnp.inf)
    m = jnp.max(logits, axis=-1, keepdims=True)
    m = jnp.where(jnp.isfinite(m), m, 0.0)
    e = jnp.exp(logits - m)
    s = jnp.sum(e, axis=-1, keepdims=True)
    return e / jnp.where(s > 0, s, 1.0)

def gqa_probs(q, k, mask, bias):
    B, Lq = q.shape[:2]
    qg = q.reshape(B, Lq, NSA_GROUPS, NSA_HPG, NSA_DH)
    logits = jnp.einsum('bqgrd,bkgd->bgrqk', qg, k, preferred_element_type=jnp.float32) * NSA_SCALE
    logits = logits + bias.reshape(NSA_GROUPS, NSA_HPG, Lq, -1).astype(jnp.float32)
    return masked_softmax(logits, mask)

def gqa_apply(p, v):
    B, _, _, Lq, _ = p.shape
    o = jnp.einsum('bgrqk,bkgd->bqgrd', p.astype(v.dtype), v)
    return o.reshape(B, Lq, NSA_HEADS, NSA_DH)

def compress(kv, w1, b1, w2, b2, n_cmp):
    B = kv.shape[0]
    n_sub = n_cmp + CMP_RATIO - 1
    sub = kv[:, :n_sub * CMP_STRIDE].reshape(B, n_sub, CMP_STRIDE, NSA_GROUPS, NSA_DH)
    h = b1
    for r in range(CMP_RATIO):
        h = h + jnp.einsum('bnjgd,jde->bnge', sub[:, r:r + n_cmp], w1[r])
    return jnp.einsum('bnge,ed->bngd', jax.nn.silu(h), w2) + b2

def block_overlap(n_cmp, n_sel):
    c0 = np.arange(n_cmp) * CMP_STRIDE
    s0 = np.arange(n_sel) * SEL_LEN
    return ((c0[:, None] <= s0[None] + SEL_LEN - 1) & (c0[:, None] + CMP_LEN - 1 >= s0[None])).astype(np.float32)

def sel_attend(q, idx, q_pos, ksb, vsb, table_g):
    B, Lq = q.shape[:2]
    n = idx.shape[-1]
    pick = jax.vmap(jax.vmap(lambda blocks, i: blocks[i]))
    kg = pick(ksb, idx).reshape(B, NSA_GROUPS, Lq, n * SEL_LEN, NSA_DH)
    vg = pick(vsb, idx).reshape(B, NSA_GROUPS, Lq, n * SEL_LEN, NSA_DH)
    kpos = (idx[..., None] * SEL_LEN + jnp.arange(SEL_LEN)).reshape(B, NSA_GROUPS, Lq, n * SEL_LEN)
    dist = q_pos[:, None] - kpos
    bias = table_g[jnp.arange(NSA_GROUPS)[None, :, None, None], rel_bucket(dist)]
    qg = q.reshape(B, Lq, NSA_GROUPS, NSA_HPG, NSA_DH)
    logits = jnp.einsum('bqgrd,bgqkd->bgrqk', qg, kg, preferred_element_type=jnp.float32) * NSA_SCALE
    logits = logits + jnp.moveaxis(bias, -1, 2).astype(jnp.float32)
    p = masked_softmax(logits, (dist >= 0)[:, :, None])
    o = jnp.einsum('bgrqk,bgqkd->bqgrd', p.astype(vg.dtype), vg)
    return o.reshape(B, Lq, NSA_HEADS, NSA_DH)

def nsa_mixer(q, kv_new, gates, past_kv, win_buf, w1, b1, w2, b2, rel_table):
    B, L = q.shape[:2]
    q_pos0 = 0 if past_kv is None else past_kv.shape[1]
    q_pos = q_pos0 + jnp.arange(L)
    full = kv_new[:, :, :4] if past_kv is None else jnp.concatenate([past_kv, kv_new[:, :, :4]], axis=1)
    T = full.shape[1]
    n_cmp = (T - CMP_LEN) // CMP_STRIDE + 1
    k_cmp = compress(full[:, :, 0], w1[0], b1[0], w2[0], b2[0], n_cmp)
    v_cmp = compress(full[:, :, 1], w1[1], b1[1], w2[1], b2[1], n_cmp)
    dist_c = q_pos[:, None] - (jnp.arange(n_cmp) * CMP_STRIDE + (CMP_LEN - 1))[None, :]
    p_cmp = gqa_probs(q, k_cmp, dist_c >= 0, jnp.moveaxis(rel_table[rel_bucket(dist_c)], -1, 0))
    o_cmp = gqa_apply(p_cmp, v_cmp)
    n_sel = -(-T // SEL_LEN)
    overlap = jnp.asarray(block_overlap(n_cmp, n_sel), dtype=p_cmp.dtype)
    score = jnp.einsum('bgrqc,cs->bgqs', p_cmp, overlap)
    blk = jnp.arange(n_sel)[None, :]
    cur = (q_pos // SEL_LEN)[:, None]
    forced = (blk == 0) | (blk == cur) | (blk == cur - 1)
    score = jnp.where(forced, jnp.inf, jnp.where(blk <= cur, score, -jnp.inf))
    _, idx = lax.top_k(score, min(SEL_TOP, n_sel))
    pad = n_sel * SEL_LEN - T

    def to_blocks(a):
        a = jnp.pad(a, ((0, 0), (0, pad), (0, 0), (0, 0)))
        return a.reshape(B, n_sel, SEL_LEN, NSA_GROUPS, NSA_DH).transpose(0, 3, 1, 2, 4)

    ksb, vsb = to_blocks(full[:, :, 2]), to_blocks(full[:, :, 3])
    table_g = rel_table.reshape(REL_BUCKETS, NSA_GROUPS, NSA_HPG).transpose(1, 0, 2)
    if L > SEL_QBLOCK and L % SEL_QBLOCK == 0:
        nb = L // SEL_QBLOCK
        qs = q.reshape(B, nb, SEL_QBLOCK, NSA_HEADS, NSA_DH).transpose(1, 0, 2, 3, 4)
        ids = idx.reshape(B, NSA_GROUPS, nb, SEL_QBLOCK, -1).transpose(2, 0, 1, 3, 4)
        ps = q_pos.reshape(nb, SEL_QBLOCK)

        def sel_block(args):
            qb, ib, pb = args
            return sel_attend(qb, ib, pb, ksb, vsb, table_g)

        o_sel = lax.map(sel_block, (qs, ids, ps)).transpose(1, 0, 2, 3, 4).reshape(B, L, NSA_HEADS, NSA_DH)
    else:
        o_sel = sel_attend(q, idx, q_pos, ksb, vsb, table_g)
    if win_buf is None:
        nb = L // WIN_QBLOCK
        kw_len = WIN_QBLOCK + WINDOW
        rows = (jnp.arange(nb) * WIN_QBLOCK)[:, None] + jnp.arange(kw_len)[None, :]
        kpos = rows - WINDOW
        wkv = jnp.pad(kv_new[:, :, 4:], ((0, 0), (WINDOW, 0), (0, 0), (0, 0), (0, 0)))[:, rows]
        dist = q_pos.reshape(nb, WIN_QBLOCK)[:, :, None] - kpos[:, None, :]
        mask = (dist >= 0) & (dist < WINDOW) & (kpos[:, None, :] >= 0)
        bias = jnp.moveaxis(rel_table[rel_bucket(dist)], -1, 1)
        qb = q.reshape(B, nb, WIN_QBLOCK, NSA_HEADS, NSA_DH)
        band = jax.vmap(lambda qq, kk, vv, mm, bb: gqa_apply(gqa_probs(qq, kk, mm, bb), vv),
                        in_axes=(1, 1, 1, 0, 0), out_axes=1)
        o_win = band(qb, wkv[:, :, :, 0], wkv[:, :, :, 1], mask, bias).reshape(B, L, NSA_HEADS, NSA_DH)
        new_win = kv_new[:, -min(WINDOW, L):, 4:]
    else:
        wkv = jnp.concatenate([win_buf, kv_new[:, :, 4:]], axis=1)
        kpos = q_pos0 - win_buf.shape[1] + jnp.arange(wkv.shape[1])
        dist = q_pos[:, None] - kpos[None, :]
        mask = (dist >= 0) & (dist < WINDOW)
        p_win = gqa_probs(q, wkv[:, :, 0], mask, jnp.moveaxis(rel_table[rel_bucket(dist)], -1, 0))
        o_win = gqa_apply(p_win, wkv[:, :, 1])
        new_win = wkv[:, -win_buf.shape[1]:]
    o = gates[:, :, 0, :, None] * o_cmp + gates[:, :, 1, :, None] * o_sel + gates[:, :, 2, :, None] * o_win
    return o.reshape(B, L, NSA_WIDTH), new_win

def hgrn_scan(q, k, v, logf, s0):
    B, L, H, _ = q.shape
    DV = v.shape[-1]
    C = math.gcd(L, HG_CHUNK)
    nc = L // C

    def chunks(a):
        return a.astype(jnp.float32).reshape(B, nc, C, H, a.shape[-1]).transpose(1, 0, 3, 2, 4)

    causal = jnp.tril(jnp.ones((C, C), dtype=bool))[:, :, None]

    def step(s, inp):
        qc, kc, vc, lc = inp
        b = jnp.cumsum(lc, axis=2)
        decay = jnp.exp(jnp.where(causal, b[:, :, :, None, :] - b[:, :, None, :, :], -jnp.inf))
        a = jnp.einsum('bhtk,bhsk,bhtsk->bhts', qc, kc, decay)
        o = jnp.einsum('bhtk,bhkv->bhtv', qc * jnp.exp(b), s) + jnp.einsum('bhts,bhsv->bhtv', a, vc)
        b_last = b[:, :, -1:, :]
        s = jnp.exp(b_last[:, :, 0, :, None]) * s + jnp.einsum('bhsk,bhsv->bhkv', kc * jnp.exp(b_last - b), vc)
        return s, o

    s, o = lax.scan(step, s0.astype(jnp.float32), (chunks(q), chunks(k), chunks(v), chunks(logf)))
    return o.transpose(1, 0, 3, 2, 4).reshape(B, L, H, DV), s

def hgrn2_mixer(q_raw, f_raw, i_raw, g_raw, lb, s0, gain):
    B, L = q_raw.shape[:2]
    q = jax.nn.silu(q_raw.reshape(B, L, HG_HEADS, HG_DK))
    fz = f_raw.reshape(B, L, HG_HEADS, HG_DK).astype(jnp.float32)
    logf = jnp.log(lb + (1 - lb) * jax.nn.sigmoid(fz))
    k = (1 - lb) * jax.nn.sigmoid(-fz)
    o, s = hgrn_scan(q, k, i_raw.reshape(B, L, HG_HEADS, HG_DV), logf, s0)
    o = rmsnorm(o.astype(q_raw.dtype), gain) * jax.nn.silu(g_raw.reshape(B, L, HG_HEADS, HG_DV))
    return o.reshape(B, L, HG_WIDTH), s

def setup_inputs(seed: int = 0) -> dict:
    key = jax.random.key(seed)
    ks = jax.random.split(key, 25)
    f32 = jnp.float32

    def nrm(k, shape, scale):
        return jax.random.normal(k, shape, f32) * scale

    n_pages = PAST_LEN // PAGE_SIZE
    n_used = DEC_BATCH * n_pages
    n_pool = n_used + (n_used + 3) // 4
    page_table = jax.random.permutation(ks[0], n_pool)[:n_used].reshape(DEC_BATCH, n_pages).astype(jnp.int32)
    w_buf = min(WINDOW, PAST_LEN)
    return {
        'x_prompt': nrm(ks[1], (BATCH, SEQ, D_MODEL), 1.0),
        'x_sample': nrm(ks[2], (DEC_BATCH, DEC_SEQ, D_MODEL), 1.0),
        'cache_nsa_kv': nrm(ks[3], (DEPTH, n_pool, PAGE_SIZE, 4, NSA_GROUPS, NSA_DH), 1.0),
        'state_win_kv': nrm(ks[4], (DEPTH, DEC_BATCH, w_buf, 2, NSA_GROUPS, NSA_DH), 1.0),
        'state_hgrn': nrm(ks[5], (DEPTH, DEC_BATCH, HG_HEADS, HG_DK, HG_DV), 0.5),
        'page_table': page_table,
        'c_prompt': nrm(ks[6], (BATCH, D_MODEL), 1.0),
        'c_sample': nrm(ks[7], (DEC_BATCH, D_MODEL), 1.0),
        'norm_g': 1.0 + nrm(ks[8], (DEPTH, 3, D_MODEL), 0.02),
        'ada_w': nrm(ks[9], (DEPTH, D_MODEL, N_ADA * D_MODEL), 0.5 * D_MODEL ** -0.5),
        'ada_b': nrm(ks[10], (DEPTH, N_ADA * D_MODEL), 0.02),
        'ffn_w_in': nrm(ks[11], (DEPTH, 2, D_MODEL, 2 * D_FF), D_MODEL ** -0.5),
        'ffn_w_out': nrm(ks[12], (DEPTH, 2, D_FF, D_MODEL), D_FF ** -0.5),
        'w_in': nrm(ks[13], (DEPTH, D_MODEL, D_IN), D_MODEL ** -0.5),
        'cmp_w1': nrm(ks[14], (DEPTH, 2, CMP_RATIO, CMP_STRIDE, NSA_DH, CMP_HID), (CMP_LEN * NSA_DH) ** -0.5),
        'cmp_b1': nrm(ks[15], (DEPTH, 2, CMP_HID), 0.02),
        'cmp_w2': nrm(ks[16], (DEPTH, 2, CMP_HID, NSA_DH), CMP_HID ** -0.5),
        'cmp_b2': nrm(ks[17], (DEPTH, 2, NSA_DH), 0.02),
        'rel_table': nrm(ks[18], (REL_BUCKETS, NSA_HEADS), 0.5),
        'hgrn_lb_logits': nrm(ks[19], (DEPTH, HG_HEADS * HG_DK), 1.0),
        'hgrn_norm_g': 1.0 + nrm(ks[20], (DEPTH, HG_DV), 0.02),
        'w_branch_nsa': nrm(ks[21], (DEPTH, NSA_WIDTH, D_MODEL), NSA_WIDTH ** -0.5),
        'w_branch_hgrn': nrm(ks[22], (DEPTH, HG_WIDTH, D_MODEL), HG_WIDTH ** -0.5),
        'w_out': nrm(ks[23], (DEPTH, D_MODEL, D_MODEL), D_MODEL ** -0.5),
        'final_g': 1.0 + nrm(ks[24], (D_MODEL,), 0.02),
    }

def reference(x_prompt, x_sample, cache_nsa_kv, state_win_kv, state_hgrn, page_table,
              c_prompt, c_sample, norm_g, ada_w, ada_b, ffn_w_in, ffn_w_out, w_in,
              cmp_w1, cmp_b1, cmp_w2, cmp_b2, rel_table, hgrn_lb_logits, hgrn_norm_g,
              w_branch_nsa, w_branch_hgrn, w_out, final_g):
    lb = jnp.cumsum(jax.nn.softmax(hgrn_lb_logits.astype(jnp.float32), axis=0), axis=0)
    lb = (lb - lb[:1]).reshape(DEPTH, HG_HEADS, HG_DK)
    splits = [int(s) for s in np.cumsum(IN_SIZES)[:-1]]

    def trunk(x, c, past_fn):
        B, L, _ = x.shape
        kv_rows, win_bufs, hg_states = [], [], []
        for l in range(DEPTH):
            past_kv, win_buf, s0 = past_fn(l)
            mods = (jax.nn.silu(c) @ ada_w[l] + ada_b[l]).reshape(B, N_ADA, 1, D_MODEL)
            shift, scale, gate = mods[:, 0::3], mods[:, 1::3], mods[:, 2::3]
            n = modulate(rmsnorm(x, norm_g[l, 0]), shift[:, 0], scale[:, 0])
            x = x + 0.5 * gate[:, 0] * swiglu(n, ffn_w_in[l, 0], ffn_w_out[l, 0])
            n = modulate(rmsnorm(x, norm_g[l, 1]), shift[:, 1], scale[:, 1])
            qa, kva, ga, qb, fb, ib, gb, ma, mb = jnp.split(n @ w_in[l], splits, axis=-1)
            kv_new = kva.reshape(B, L, 6, NSA_GROUPS, NSA_DH)
            o_a, new_win = nsa_mixer(qa.reshape(B, L, NSA_HEADS, NSA_DH), kv_new,
                                     jax.nn.sigmoid(ga.reshape(B, L, 3, NSA_HEADS)), past_kv, win_buf,
                                     cmp_w1[l], cmp_b1[l], cmp_w2[l], cmp_b2[l], rel_table)
            o_b, s_new = hgrn2_mixer(qb, fb, ib, gb, lb[l], s0, hgrn_norm_g[l])
            merged = jax.nn.sigmoid(ma) * (o_a @ w_branch_nsa[l]) + jax.nn.sigmoid(mb) * (o_b @ w_branch_hgrn[l])
            x = x + gate[:, 1] * (merged @ w_out[l])
            n = modulate(rmsnorm(x, norm_g[l, 2]), shift[:, 2], scale[:, 2])
            x = x + 0.5 * gate[:, 2] * swiglu(n, ffn_w_in[l, 1], ffn_w_out[l, 1])
            kv_rows.append(kv_new[:, :, :4])
            win_bufs.append(new_win)
            hg_states.append(s_new)
        return rmsnorm(x, final_g), jnp.stack(kv_rows), jnp.stack(win_bufs), jnp.stack(hg_states)

    n_seq, n_pages = page_table.shape

    def prompt_past(l):
        return None, None, jnp.zeros((x_prompt.shape[0], HG_HEADS, HG_DK, HG_DV), jnp.float32)

    def sample_past(l):
        past = cache_nsa_kv[l][page_table].reshape(n_seq, n_pages * PAGE_SIZE, 4, NSA_GROUPS, NSA_DH)
        return past, state_win_kv[l], state_hgrn[l]

    y_prompt, kv_p, win_p, hg_p = trunk(x_prompt, c_prompt, prompt_past)
    y_sample, kv_s, win_s, hg_s = trunk(x_sample, c_sample, sample_past)
    return (y_prompt, y_sample, kv_p, kv_s, win_p, win_s, hg_p, hg_s)


_drawn_inputs = setup_inputs


def setup_inputs(seed=0):
    import zlib

    import numpy as np

    out = dict(_drawn_inputs(seed))
    spreads = {}
    factors = {'cache_nsa_kv': 2.777,
     'norm_g': 2.896,
     'cmp_b1': 48.447,
     'cmp_b2': 49.258,
     'rel_table': 3.831,
     'hgrn_norm_g': 8.0,
     'final_g': 8.129}
    for name, (base, spread) in spreads.items():
        noise = np.random.default_rng([zlib.crc32(name.encode()), seed]).standard_normal(out[name].shape)
        drawn = base * np.exp(spread * noise) if base else spread * noise
        out[name] = jnp.asarray(drawn.astype(out[name].dtype))
    for name, factor in factors.items():
        out[name] = (out[name] * factor).astype(out[name].dtype)
    return out
```

```python
from contextlib import ExitStack, contextmanager
import math

import numpy as np
import concourse.bass as bass
from concourse import mybir

F32, F32R, I32, U32 = mybir.dt.float32, mybir.dt.float32r, mybir.dt.int32, mybir.dt.uint32
ALU, ACT = mybir.AluOpType, mybir.ActivationFunctionType

P = 128
D, DEPTH, D_FF = 1024, 2, 2816
SEQ, NB, NI, PAST, PAGE = 512, 8, 4, 512, 128
NSMP = NB * NI
T = SEQ + NSMP
HALF = T // 2
DC = D // P
NSEQ = 1 + NB
HEADS, GROUPS, R, DH = 8, 2, 4, 64
HG = 4
NKV = 6
CMP_STRIDE = 16
NPAGE = PAST // PAGE
NCMP = (PAST - 32) // 16 + 1
NSUB = NCMP + 1
BUCKETS, MAXDIST = 32, 128
EPS = 1e-6
NEG = -1e30
FLOOR = -1e29
FFN_PARTS = (12, 10)
KMAX = max(FFN_PARTS)
PIECES = 3
TOKT = [(t * P, P) for t in range(SEQ // P)] + [(SEQ, NSMP)]
LEVELS = [64, 32, 16, 8, 4, 2, 1, 0]
Q0, KV0, HQ0, HF0, HI0, HO0, GATE0 = 0, 4, 10, 14, 18, 22, 26
NPC = 27
NPOOL = NB * PAST // PAGE * 5 // 4
C_KV, C_GATE = 512, 1280
C_HG = C_GATE + 3 * HEADS
C_MA = C_HG + 4 * 512
C_MB = C_MA + D


def bucket(dist):
    exact = BUCKETS // 2
    if dist < exact:
        return dist
    return min(exact + int(math.log(dist / exact) / math.log(MAXDIST / exact) * exact), BUCKETS - 1)


def shape_constants():
    rev = np.zeros((BUCKETS + 1, 640), np.float32)
    for m in range(640):
        dist = 511 - m
        if dist >= 0:
            rev[bucket(dist), m] = 1.0
        else:
            rev[BUCKETS, m] = NEG
    old = np.zeros((BUCKETS + 1, 2, NI, PAST), np.float32)
    for i in range(NI):
        for c in range(PAST):
            tok = 4 * (c % P) + c // P
            old[bucket(PAST + i - tok), :, i, c] = 1.0
            if tok <= i:
                old[BUCKETS, 1, i, c] = NEG
    cmp = np.zeros((BUCKETS + 1, NI, NCMP), np.float32)
    for i in range(NI):
        for n in range(NCMP):
            cmp[bucket(PAST + i - 16 * n - 31), i, n] = 1.0
    new = np.zeros((BUCKETS + 1, 4, NI, 2, NSMP), np.float32)
    for j in range(4):
        for i in range(NI):
            for half in range(2):
                for key in range(NSMP):
                    b, k = key // NI, key % NI
                    if b == 4 * half + j and k <= i:
                        new[bucket(i - k), j, i, half, key] = 1.0
                    else:
                        new[BUCKETS, j, i, half, key] = NEG
    level = np.zeros((P, len(LEVELS), P), np.float32)
    for n, size in enumerate(LEVELS):
        for s in range(P):
            for t in range(P):
                if size == 0:
                    level[s, n, t] = s == t
                else:
                    level[s, n, t] = s // (2 * size) == t // (2 * size) and s % (2 * size) < size <= t % (2 * size)
    own = np.zeros((NSMP, NB), np.float32)
    for t in range(NSMP):
        own[t, t // NI] = 1.0
    return {
        "c_rev": rev, "c_old": old.reshape(BUCKETS + 1, -1), "c_cmp": cmp.reshape(BUCKETS + 1, -1),
        "c_new": new.reshape(BUCKETS + 1, -1), "c_level": level, "c_own": own, "c_ident": np.eye(P, dtype=np.float32),
    }


def strided(ap, *dims):
    return bass.AP(ap.tensor, ap.offset, [list(ap.ap[0])] + [list(d) for d in dims])


@contextmanager
def stage(nc, *names):
    with ExitStack() as ctx:
        sems = [ctx.enter_context(nc.semaphore(f"{n}_{nc.next_id()}")) for n in names]
        yield sems
        for s in sems:
            nc.sync.sem_clear(s)
        nc.all_engine_barrier(sem_only=True)


class Weights:

    NAMES = ("raw_full0", "raw_full1", "hi_done", "lo_done", "mm_done")

    def __init__(self, nc, ctx, sems, k):
        self.raw_full, (self.hi_done, self.lo_done, self.mm_done) = sems[0:2], sems[2:5]
        sb = lambda n, dt: ctx.enter_context(nc.sbuf_tensor(f"{n}_{nc.next_id()}", [P, k, P], dt))
        self.raw = [sb("w_raw", F32) for _ in range(2)]
        self.hi = [sb("w_hi", F32R) for _ in range(2)]
        self.lo = [sb("w_lo", F32R) for _ in range(2)]

    def credit_vector(self, dve):
        dve.sem_inc(self.lo_done, 2)

    def credit_tensor(self, pe):
        pe.sem_inc(self.mm_done, 2)

    def load(self, sp, u, slot, pieces):
        assert len(pieces) == PIECES
        sp.wait_ge(self.lo_done, 2 * u + slot + 1)
        for dst, src in pieces:
            sp.dma_start(dst, src).then_inc(self.raw_full[slot], 16)

    def columns(self, slot, k, src):
        v = src.rearrange("(k p) n -> p k n", p=P)
        cut = [0, (k + 2) // 3, (2 * k + 2) // 3, k]
        return [(self.raw[slot][:, a:b, :], v[:, a:b, :]) for a, b in zip(cut, cut[1:])]

    def split_hi(self, act, u, slot, k):
        act.wait_ge(self.raw_full[slot], 16 * PIECES * (u + 1))
        act.wait_ge(self.mm_done, 2 * u + slot + 1)
        act.activation(self.hi[slot][:, 0:k, :], self.raw[slot][:, 0:k, :], ACT.Copy).then_inc(self.hi_done, 1)

    def split_lo(self, dve, u, slot, k):
        dve.wait_ge(self.hi_done, 2 * u + slot + 1)
        dve.tensor_tensor(self.lo[slot][:, 0:k, :], self.raw[slot][:, 0:k, :],
                          self.hi[slot][:, 0:k, :].bitcast(F32), ALU.subtract).then_inc(self.lo_done, 1)

    def product(self, pe, u, slot, out, hi, lo, ks, k0=0, last=True):
        pe.wait_ge(self.lo_done, 2 * u + slot + 3)
        for n in range(ks):
            for w, x, end in ((self.hi, hi, 0), (self.hi, lo, 0), (self.lo, hi, 1)):
                for half in range(2):
                    mm = pe.matmul(out[:, half, 0:HALF], w[slot][:, k0 + n, :], x[:, n, half * HALF:(half + 1) * HALF],
                                   start=(n == 0 and w is self.hi and x is hi), stop=(n == ks - 1 and end == 1))
        if last:
            mm.then_inc(self.mm_done, 1)
        return mm


    def first_products(self, pe, outs, hi, lo, ks, landed):
        pe.wait_ge(self.lo_done, 4)
        for n in range(ks):
            pe.wait_ge(landed, n + 1)
            for slot in range(2):
                for w, x, end in ((self.hi, hi, 0), (self.hi, lo, 0), (self.lo, hi, 1)):
                    for half in range(2):
                        mm = pe.matmul(outs[slot][:, half, 0:HALF], w[slot][:, n, :], x[:, n, half * HALF:(half + 1) * HALF],
                                       start=(n == 0 and w is self.hi and x is hi), stop=(n == ks - 1 and end == 1))
                if n == ks - 1:
                    mm.then_inc(self.mm_done, 1)


def norm_vector(dve, s, x, tmp, nf, rs, mods, w, nhi, nlo):
    dve.wait_ge(s.sd_done, 1)
    dve.reciprocal(rs[:, :], rs[:, :]).then_inc(s.rs_done, 1)
    dve.wait_ge(s.rs_done, 1)

    def lo(c):
        dve.wait_ge(s.nh_done, c + 1)
        dve.tensor_tensor(nlo[:, c, :], nf[:, c % 2, :], nhi[:, c, :].bitcast(F32), ALU.subtract).then_inc(s.nl_done, 1)

    for c in range(DC):
        if c >= 2:
            dve.wait_ge(s.af_done, c - 1)
        dve.tensor_tensor(tmp[:, c % 2, :], x[:, c, :], rs[:, :], ALU.mult).then_inc(s.xr_done, 1)
        if c >= 1:
            lo(c - 1)
        dve.wait_ge(s.xr_done, c + 1)
        smp = tmp[:, c % 2, SEQ:T]
        dve.tensor_tensor(strided(smp, [NI, NB], [1, NI]), strided(smp, [NI, NB], [1, NI]),
                          strided(mods[:, 3 * w + 1, c, 1:NSEQ], [1, NB], [0, NI]), ALU.mult).then_inc(s.sm_done, 1)
        dve.wait_ge(s.sm_done, c + 1)
        if c >= 2:
            dve.wait_ge(s.nl_done, c - 1)
        dve.tensor_tensor(strided(nf[:, c % 2, SEQ:T], [NI, NB], [1, NI]), strided(smp, [NI, NB], [1, NI]),
                          strided(mods[:, 3 * w, c, 1:NSEQ], [1, NB], [0, NI]), ALU.add).then_inc(s.sa_done, 1)
    lo(DC - 1)


def norm_scalar(act, s, wt, x, sq, st, eps, tmp, nf, rs, mods, w, nhi):
    for c in range(DC):
        if c >= 2:
            act.wait_ge(s.st_done, c - 1)
        act.activation(sq[:, c % 2, :], x[:, c, :], ACT.Square).then_inc(s.sq_done, 1)
    for slot in range(2):
        wt.split_hi(act, 0, slot, DC)
    act.wait_ge(s.st_done, DC)
    act.activation(strided(rs[:, :], [HALF, 2], [1, HALF]), st[:, :, 0:HALF], ACT.Sqrt, bias=eps[:, 0:1],
                   scale=1.0 / D).then_inc(s.sd_done, 1)

    def hi(c):
        act.wait_ge(s.af_done, c + 1)
        act.wait_ge(s.sa_done, c + 1)
        act.activation(nhi[:, c, :], nf[:, c % 2, :], ACT.Copy).then_inc(s.nh_done, 1)

    for c in range(DC):
        act.wait_ge(s.xr_done, c + 1)
        if c >= 2:
            act.wait_ge(s.nl_done, c - 1)
        act.activation(nf[:, c % 2, 0:SEQ], tmp[:, c % 2, 0:SEQ], ACT.Identity, bias=mods[:, 3 * w, c, 0:1],
                       scale=mods[:, 3 * w + 1, c, 0:1]).then_inc(s.af_done, 1)
        if c >= 1:
            hi(c - 1)
    hi(DC - 1)


def norm_tensor(pe, s, sq, st, ones):
    for c in range(DC):
        pe.wait_ge(s.sq_done, c + 1)
        for half in range(2):
            mm = pe.matmul(st[:, half, 0:HALF], ones[:, :], sq[:, c % 2, half * HALF:(half + 1) * HALF],
                           start=(c == 0), stop=(c == DC - 1))
        mm.then_inc(s.st_done, 1)


class NormSems:
    NAMES = ("sq_done", "st_done", "sd_done", "rs_done", "xr_done", "sm_done", "sa_done", "af_done", "nh_done",
             "nl_done")

    def __init__(self, sems):
        (self.sq_done, self.st_done, self.sd_done, self.rs_done, self.xr_done, self.sm_done, self.sa_done,
         self.af_done, self.nh_done, self.nl_done) = sems


def peeled(engine, n, step, body):
    if n > step:
        with engine.Fori(0, n - step, step) as i:
            body(i, False)
    body(n - step, True)


def trunk(nc, a, o):
    ctx = ExitStack()
    with ctx:
        def sb(name, shape, dt=F32, at=ctx):
            return at.enter_context(nc.sbuf_tensor(f"{name}_{nc.next_id()}", shape, dt))

        def ps(name, banks, at):
            return at.enter_context(nc.psum_tensor(f"{name}_{nc.next_id()}", [P, banks, 512], F32))

        rv_dram = nc.dram_tensor("rel_rev", (HEADS, P, 640), F32, kind="Internal").ap()
        gate_dram = nc.dram_tensor("gate_rows", (NB, 3 * HEADS, NI), F32, kind="Internal").ap()

        x = sb("x", [P, DC, T])
        mods = sb("mods", [P, 9, DC, NSEQ])
        cT = sb("cT", [P, DC, NSEQ])
        ident = sb("ident", [P, P])
        ones = sb("ones", [P, P])
        eps = sb("eps", [P, 1])
        vecs = sb("vecs", [P, 74])
        adab = sb("adab", [P, DEPTH, 72])
        lb = sb("lb", [P, DEPTH, HG])
        oml = sb("oml", [P, DEPTH, HG])
        own = sb("own", [NSMP, NB])
        b2row = sb("b2row", [32, DEPTH, DH])
        bias_old = sb("bias_old", [P, 2, PAST])
        bias_cmp = sb("bias_cmp", [P, NCMP])
        bias_new = sb("bias_new", [P, 2, NSMP])
        pages = sb("pages", [1, NB * PAST // PAGE], I32)

        with stage(nc, "loaded", "set_done", "dve_done", "tr_done", "ev_done", "sil_done", "la_done",
                                      "rev_done", "rev_ev", "rev_out", "bi_done", "bi_ev", "lb_done", "lbe_done") as (
                loaded, set_done, dve_done, tr_done, ev_done, sil_done, la_done, rev_done, rev_ev, rev_out, bi_done,
                bi_ev, lb_done, lbe_done), ExitStack() as st:
            xn = sb("xn", [P, 4, D], at=st)
            xs = sb("xs", [NSMP, D], at=st)
            cn = sb("cn", [NSEQ, D], at=st)
            vn = sb("vn", [74, P], at=st)
            an = sb("an", [72, DEPTH, P], at=st)
            rev = sb("rev", [33, 640], at=st)
            old = sb("old", [33, 2, NI, PAST], at=st)
            cmpc = sb("cmpc", [33, NI, NCMP], at=st)
            newc = sb("newc", [33, 16, 2 * NSMP], at=st)
            table = sb("table", [33, HEADS], at=st)
            la = sb("la", [33, NI, P], at=st)
            lj = sb("lj", [33, 16, P], at=st)
            revs = sb("revs", [HEADS, 640], at=st)
            sm = sb("sm", [P, 6, HG], at=st)
            pt = [ps(f"pt{i}", 1, st) for i in range(2)]
            pr = ps("pr", 2, st)
            pb = ps("pb", 4, st)
            block = st.enter_context(nc.Block())
            n_loads = 20
            jobs = []
            for c in range(DC):
                jobs.append(("x", c))
            for c in range(DC):
                jobs.append(("xs", c))
            jobs += [("c", 0), ("v", 0), ("a", 0)]

            @block.sync
            def _(sp):
                sp.wait_ge(set_done, 1)
                loads = [
                    (xn[:, :, :], a["x_prompt"][0].rearrange("(t p) d -> p t d", p=P)),
                    (xs[:, :], a["x_sample"].rearrange("b i d -> (b i) d")),
                    (cn[0:1, :], a["c_prompt"]), (cn[1:NSEQ, :], a["c_sample"]),
                    (vn[0:48, :], a["norm_g"].rearrange("l w (c p) -> (l w c) p", p=P)),
                    (vn[48:56, :], a["final_g"].rearrange("(c p) -> c p", p=P)),
                    (vn[56:60, :], a["cmp_b1"].rearrange("l k e -> (l k) e")),
                    (vn[60:64, 0:DH], a["cmp_b2"].rearrange("l k e -> (l k) e")),
                    (vn[60:64, DH:P], a["cmp_b2"].rearrange("l k e -> (l k) e")),
                    (vn[64:72, :], a["hgrn_lb_logits"].rearrange("l (h p) -> (l h) p", p=P)),
                    (vn[72:74, :], a["hgrn_norm_g"]),
                    (an[:, :, :], a["ada_b"].rearrange("l (n p) -> n l p", p=P)),
                    (rev[:, :], a["c_rev"]), (old[:, :, :, :], a["c_old"].rearrange("b (m i k) -> b m i k", m=2, i=NI)),
                    (cmpc[:, :, :], a["c_cmp"].rearrange("b (i k) -> b i k", i=NI)),
                    (newc[:, :, :], a["c_new"].rearrange("b (i k) -> b i k", i=16)),
                    (table[0:BUCKETS, :], a["rel_table"]), (own[:, :], a["c_own"]), (ident[:, :], a["c_ident"]),
                    (pages[:, :], a["page_table"].rearrange("(o b) n -> o (b n)", o=1)),
                ]
                assert len(loads) == n_loads
                for dst, src in loads:
                    sp.dma_start(dst, src).then_inc(loaded, 16)
                for l in range(DEPTH):
                    sp.dma_start(b2row[:, l, :], a["cmp_b2"][l, 1].partition_broadcast(32)).then_inc(loaded, 16)
                sp.wait_ge(rev_ev, 2)
                sp.dma_start(rv_dram, strided(revs[:, :], [0, P], [1, 640])).then_inc(rev_out, 16)
                sp.wait_ge(rev_out, 16)
                sp.wait_ge(loaded, 16 * (n_loads + DEPTH))

            @block.vector
            def _(dve):
                dve.memset(table[:, :], 1.0).then_inc(set_done, 1)
                dve.memset(ones[:, :], 1.0)
                dve.memset(eps[:, :], EPS)
                dve.memset(la[:, :, :], 0.0).then_inc(dve_done, 1)
                dve.memset(lj[:, :, :], 0.0).then_inc(dve_done, 1)
                dve.wait_ge(dve_done, 2)
                dve.wait_ge(loaded, 16 * (n_loads + DEPTH))
                for i in range(NI):
                    dve.tensor_copy(strided(la[:, i, i:], [32, 4], [NI, HEADS]),
                                    strided(table[:, :], [0, 4], [1, HEADS])).then_inc(la_done, 1)
                    dve.tensor_copy(strided(lj[:, i, i:], [NI * P + 32, 4], [NI, HEADS]),
                                    strided(table[:, :], [0, 4], [1, HEADS])).then_inc(la_done, 1)
                for n, (kind, c) in enumerate(jobs):
                    dve.wait_ge(tr_done, n + 1)
                    src = pt[n % 2][:, 0, :]
                    if kind == "x":
                        ins = dve.tensor_copy(x[:, c, 0:SEQ], src)
                    elif kind == "xs":
                        ins = dve.tensor_copy(x[:, c, SEQ:T], src[:, 0:NSMP])
                    elif kind == "c":
                        ins = dve.tensor_copy(strided(cT[:, :, :], [1, DC * NSEQ]), src[:, 0:DC * NSEQ])
                    elif kind == "v":
                        ins = dve.tensor_copy(vecs[:, :], src[:, 0:74])
                    else:
                        ins = dve.tensor_copy(strided(adab[:, :, :], [1, 144]), src[:, 0:144])
                    ins.then_inc(ev_done, 1)
                dve.wait_ge(ev_done, len(jobs))
                lg = vecs[:, 64:72]
                dve.tensor_tensor(sm[:, 0, :], lg[:, 0:4], lg[:, 4:8], ALU.max).then_inc(lb_done, 1)
                dve.wait_ge(lb_done, 1)
                dve.tensor_tensor(sm[:, 1, :], lg[:, 0:4], sm[:, 0, :], ALU.subtract).then_inc(lb_done, 1)
                dve.tensor_tensor(sm[:, 2, :], lg[:, 4:8], sm[:, 0, :], ALU.subtract).then_inc(lb_done, 1)
                dve.wait_ge(lbe_done, 1)
                dve.tensor_tensor(sm[:, 5, :], sm[:, 3, :], sm[:, 4, :], ALU.add).then_inc(lb_done, 1)
                dve.wait_ge(lb_done, 4)
                dve.reciprocal(sm[:, 5, :], sm[:, 5, :]).then_inc(lb_done, 1)
                dve.wait_ge(lb_done, 5)
                dve.tensor_tensor(sm[:, 3, :], sm[:, 3, :], sm[:, 5, :], ALU.mult).then_inc(lb_done, 1)
                dve.tensor_tensor(sm[:, 4, :], sm[:, 4, :], sm[:, 5, :], ALU.mult).then_inc(lb_done, 1)
                dve.wait_ge(lb_done, 7)
                dve.tensor_tensor(sm[:, 4, :], sm[:, 3, :], sm[:, 4, :], ALU.add).then_inc(lb_done, 1)
                dve.tensor_tensor(lb[:, 0, :], sm[:, 3, :], sm[:, 3, :], ALU.subtract).then_inc(lb_done, 1)
                dve.wait_ge(lb_done, 8)
                dve.tensor_tensor(lb[:, 1, :], sm[:, 4, :], sm[:, 3, :], ALU.subtract).then_inc(lb_done, 1)
                dve.wait_ge(lb_done, 10)
                dve.tensor_scalar(oml[:, :, :], lb[:, :, :], -1.0, 1.0, ALU.mult, ALU.add)
                dve.wait_ge(rev_done, 1)
                for h in range(2):
                    dve.tensor_copy(revs[:, 320 * h:320 * h + 320], pr[0:HEADS, h, 0:320]).then_inc(rev_ev, 1)
                dve.wait_ge(bi_done, 1)
                dve.tensor_copy(bias_old[:, :, :], pb[:, 0:2, :])
                dve.tensor_copy(bias_cmp[:, :], pb[:, 2, 0:NCMP])
                dve.tensor_copy(strided(bias_new[:, :, :], [1, 2 * NSMP]), pb[:, 3, 0:2 * NSMP]).then_inc(bi_ev, 1)

            @block.scalar
            def _(act):
                act.wait_ge(loaded, 16 * (n_loads + DEPTH))
                act.activation(cn[:, :], cn[:, :], ACT.Silu).then_inc(sil_done, 1)
                act.wait_ge(lb_done, 3)
                act.activation(strided(sm[:, 3:5, :], [1, 8]), strided(sm[:, 1:3, :], [1, 8]), ACT.Exp).then_inc(lbe_done, 1)

            @block.tensor
            def _(pe):
                pe.wait_ge(loaded, 16 * (n_loads + DEPTH))
                pe.wait_ge(sil_done, 1)
                for n, (kind, c) in enumerate(jobs):
                    out = pt[n % 2][:, 0, :]
                    if n >= 2:
                        pe.wait_ge(ev_done, n - 1)
                    if kind == "x":
                        for t in range(4):
                            mm = pe.transpose(out[:, t * P:(t + 1) * P], xn[:, t, c * P:(c + 1) * P], ident[:, :])
                    elif kind == "xs":
                        mm = pe.transpose(out[:, 0:NSMP], xs[:, c * P:(c + 1) * P], ident[0:NSMP, 0:NSMP])
                    elif kind == "c":
                        for k in range(DC):
                            mm = pe.transpose(out[:, k * NSEQ:(k + 1) * NSEQ], cn[:, k * P:(k + 1) * P],
                                              ident[0:NSEQ, 0:NSEQ])
                    elif kind == "v":
                        mm = pe.transpose(out[:, 0:74], vn[:, :], ident[0:74, 0:74])
                    else:
                        for l in range(DEPTH):
                            mm = pe.transpose(out[:, 72 * l:72 * l + 72], an[:, l, :], ident[0:72, 0:72])
                    mm.then_inc(tr_done, 1)
                for h in range(2):
                    mm = pe.matmul(pr[0:HEADS, h, 0:320], table[:, :], rev[:, 320 * h:320 * h + 320], start=True, stop=True)
                mm.then_inc(rev_done, 1)
                pe.wait_ge(la_done, 2 * NI)
                for m in range(2):
                    for i in range(NI):
                        pe.matmul(pb[:, m, :], la[:, i, :], old[:, m, i, :], start=(i == 0), stop=(i == NI - 1))
                for i in range(NI):
                    pe.matmul(pb[:, 2, 0:NCMP], la[:, i, :], cmpc[:, i, :], start=(i == 0), stop=(i == NI - 1))
                for i in range(16):
                    mm = pe.matmul(pb[:, 3, 0:2 * NSMP], lj[:, i, :], newc[:, i, :], start=(i == 0), stop=(i == 15))
                mm.then_inc(bi_done, 1)

        def ada_stage(l):
            NP = 4
            LO = 32
            with stage(nc, "full0", "full1", "full2", "full3", "c_done", "hi_done", "lo_done", "mm_done", "md_done",
                       "tp_done", "add_done", "mod_done") as (full0, full1, full2, full3, c_done, hi_done, lo_done,
                                                              mm_done, md_done, tp_done, add_done, mod_done), ExitStack() as st:
                full = [full0, full1, full2, full3]
                raw = [sb(f"ada_raw{i}", [P, DC // 2, 512], at=st) for i in range(NP)]
                hi = [sb(f"ada_hi{i}", [P, DC // 2, 512], F32R, at=st) for i in range(NP)]
                lo = [sb(f"ada_lo{i}", [P, DC // 2, 512], F32R, at=st) for i in range(NP)]
                cp = sb("cp", [P, DC, P], at=st)
                cs = sb("cs", [P, DC, P], F32R, at=st)
                ch = sb("ch", [P, DC, NSEQ], F32R, at=st)
                sel = sb("sel", [LO + NSEQ, NSEQ], at=st)
                md = sb("md", [LO + NSEQ, 2, 512], at=st)
                pm = [ps(f"pm{i}", 1, st) for i in range(2)]
                pt = [ps(f"pt{i}", 1, st) for i in range(2)]
                block = st.enter_context(nc.Block())
                src = a["ada_w"][l].rearrange("(k p) n -> p k n", p=P)

                @block.sync
                def _(sp):
                    with sp.Fori(0, 9) as u:
                        for i in range(NP):
                            s, h = divmod(i, 2)
                            sp.wait_ge(lo_done, NP * u + i + 1)
                            sp.dma_start(raw[i][:, :, :], src[:, 4 * h:4 * h + 4, bass.ds(u * 1024 + s * 512, 512)]).then_inc(full[i], 16)

                @block.scalar
                def _(act):
                    act.activation(ch[:, :, :], cT[:, :, :], ACT.Copy).then_inc(c_done, 1)
                    act.wait_ge(c_done, 4)
                    act.activation(cs[:, :, :], cp[:, :, :], ACT.Copy).then_inc(c_done, 1)

                    def split(u, i):
                        act.wait_ge(full[i], 16 * (u + 1))
                        act.wait_ge(mm_done, NP * u + i + 1)
                        act.activation(hi[i][:, :, :], raw[i][:, :, :], ACT.Copy).then_inc(hi_done, 1)

                    def evacuate(u, s):
                        act.wait_ge(mm_done, NP * u + (2 * s + 2 + NP))
                        act.wait_ge(tp_done, 2 * u + s + 1)
                        act.activation(md[:, s, :], pm[s][0:LO + NSEQ, 0, :], ACT.Copy).then_inc(md_done, 1)

                    split(0, 0)
                    split(0, 1)
                    with act.Fori(0, 8) as u:
                        split(u, 2)
                        split(u, 3)
                        evacuate(u, 0)
                        split(u + 1, 0)
                        split(u + 1, 1)
                        evacuate(u, 1)
                    split(8, 2)
                    split(8, 3)
                    evacuate(8, 0)
                    evacuate(8, 1)

                @block.tensor
                def _(pe):
                    pe.sem_inc(mm_done, NP)
                    pe.sem_inc(tp_done, 2)
                    pe.wait_ge(c_done, 5)

                    def products(u, i):
                        s, h = divmod(i, 2)
                        pe.wait_ge(lo_done, NP * u + (i + 1 + NP))
                        if h == 0:
                            pe.wait_ge(md_done, 2 * u + s + 1)
                        for n in range(DC // 2):
                            for w in (hi, lo):
                                mm = pe.matmul(pm[s][:, 0, :], cs[:, 4 * h + n, :], w[i][:, n, :],
                                               start=(h == 0 and n == 0 and w is hi), stop=(h == 1 and n == DC // 2 - 1 and w is lo))
                        mm.then_inc(mm_done, 1)

                    def turn(u, s):
                        pe.wait_ge(md_done, 2 * u + s + 3)
                        pe.wait_ge(add_done, 2 * u + s + 1)
                        for m in range(4):
                            mm = pe.matmul(pt[s][:, 0, m * NSEQ:(m + 1) * NSEQ], md[:, s, m * P:(m + 1) * P], sel[:, :],
                                           start=True, stop=True)
                        mm.then_inc(tp_done, 1)

                    products(0, 0)
                    products(0, 1)
                    with pe.Fori(0, 8) as u:
                        products(u, 2)
                        products(u, 3)
                        turn(u, 0)
                        products(u + 1, 0)
                        products(u + 1, 1)
                        turn(u, 1)
                    products(8, 2)
                    products(8, 3)
                    turn(8, 0)
                    turn(8, 1)

                @block.vector
                def _(dve):
                    dve.sem_inc(md_done, 2)
                    dve.sem_inc(add_done, 2)
                    dve.sem_inc(lo_done, NP)
                    dve.memset(cp[:, :, :], 0.0).then_inc(c_done, 1)
                    dve.tensor_tensor(sel[:, :], ident[0:LO + NSEQ, 0:NSEQ], ident[0:LO + NSEQ, LO:LO + NSEQ], ALU.add).then_inc(c_done, 1)
                    dve.wait_ge(c_done, 3)
                    dve.tensor_copy(cp[:, :, 0:NSEQ], cT[:, :, :])
                    dve.tensor_tensor(cp[:, :, LO:LO + NSEQ], cT[:, :, :], ch[:, :, :].bitcast(F32), ALU.subtract).then_inc(c_done, 1)
                    flat = mods[:, :, :, :].rearrange("p a c s -> p (a c s)")

                    def split(u, i):
                        dve.wait_ge(hi_done, NP * u + i + 1)
                        dve.tensor_tensor(lo[i][:, :, :], raw[i][:, :, :], hi[i][:, :, :].bitcast(F32), ALU.subtract).then_inc(lo_done, 1)

                    def add_bias(u, s):
                        dve.wait_ge(tp_done, 2 * u + s + 3)
                        dve.tensor_tensor(flat[:, bass.ds(u * 72 + s * 36, 36)].rearrange("p (m s) -> p m s", m=4),
                                          pt[s][:, 0, 0:36].rearrange("p (m s) -> p m s", m=4),
                                          bias_view(adab, l, u, s), ALU.add).then_inc(add_done, 1)

                    for i in range(3):
                        split(0, i)
                    with dve.Fori(0, 8) as u:
                        split(u, 3)
                        split(u + 1, 0)
                        add_bias(u, 0)
                        split(u + 1, 1)
                        split(u + 1, 2)
                        add_bias(u, 1)
                    split(8, 3)
                    add_bias(8, 0)
                    add_bias(8, 1)
                    dve.wait_ge(add_done, 20)
                    for w3 in range(3):
                        g = vecs[:, bass.ds(l * 24 + w3 * 8, 8)]
                        sc = mods[:, 3 * w3 + 1, :, :]
                        dve.scalar_tensor_tensor(sc, sc, 1.0, strided(g, [1, DC], [0, NSEQ]), ALU.add, ALU.mult).then_inc(mod_done, 1)
                        if w3 != 1:
                            gt = mods[:, 3 * w3 + 2, :, :]
                            dve.tensor_scalar(gt, gt, 0.5, None, ALU.mult).then_inc(mod_done, 1)

        def bias_view(t, l, u, s):
            v = t[:, :, :].rearrange("p l n -> p (l n)")[:, bass.ds(l * 72 + u * 8 + s * 4, 4)]
            return strided(v, [1, 4], [0, NSEQ])

        def norm_buffers(at):
            return (sb("sq", [P, 2, T], at=at), sb("tmp", [P, 2, T], at=at), sb("nf", [P, 2, T], at=at),
                    sb("rs", [P, T], at=at))

        def residual(dve, psum, c, comp, tmp, x_done, res_done, count):
            xc = x[:, bass.ds(c, 1), :]
            mc = mods[:, comp, bass.ds(c, 1), :]
            gate = mc[:, 0, 0:1]
            w = SEQ - HALF
            dve.tensor_tensor(strided(tmp, [NI, NB], [1, NI]), strided(psum[:, 1, w:w + NSMP], [NI, NB], [1, NI]),
                              strided(mc[:, 0, 1:NSEQ], [1, NB], [0, NI]), ALU.mult).then_inc(x_done, 1)
            dve.scalar_tensor_tensor(xc[:, 0, 0:HALF], psum[:, 0, 0:HALF], gate, xc[:, 0, 0:HALF], ALU.mult, ALU.add)
            dve.scalar_tensor_tensor(xc[:, 0, HALF:SEQ], psum[:, 1, 0:w], gate, xc[:, 0, HALF:SEQ], ALU.mult, ALU.add)
            dve.wait_ge(x_done, count)
            dve.tensor_tensor(xc[:, 0, SEQ:T], xc[:, 0, SEQ:T], tmp, ALU.add).then_inc(res_done, 1)

        def ffn_stage(l, which, w3):
            names = Weights.NAMES + NormSems.NAMES + ("silu_done", "prod_done", "gh_done", "gl_done", "res_done", "x_done")
            with stage(nc, *names) as sems, ExitStack() as st:
                s = NormSems(sems[5:15])
                silu_done, prod_done, gh_done, gl_done, res_done, x_done = sems[15:]
                wt = Weights(nc, st, sems[0:5], KMAX)
                nhi, nlo = (sb(n, [P, DC, T], F32R, at=st) for n in ("nhi", "nlo"))
                ghi, glo = (sb(n, [P, KMAX, T], F32R, at=st) for n in ("ghi", "glo"))
                sq, tmp, nf, rs = norm_buffers(st)
                sa, g32 = sq, tmp
                rt = sb("rt", [P, 2, NSMP], at=st)
                pa = [ps(f"pa{i}", 2, st) for i in range(2)]
                pg = [ps(f"pg{i}", 2, st) for i in range(2)]
                block = st.enter_context(nc.Block())
                w_in = a["ffn_w_in"][l, which]
                w_out = a["ffn_w_out"][l, which]
                n0, n1 = FFN_PARTS
                parts = [(n0, 0, 0, n0, DC), (n1, n0 + DC // 2, n0, n0 + DC // 2 + n1, None)]

                @block.sync
                def _(sp):
                    for n, u0, j0, uo, _ in parts:
                        with sp.Fori(0, n) as j:
                            for slot in range(2):
                                wt.load(sp, j + u0, slot, wt.columns(slot, DC, w_in[:, bass.ds((j + j0) * P + slot * D_FF, P)]))
                        rows = w_out[j0 * P:(j0 + n) * P, :]
                        with sp.Fori(0, DC // 2) as c:
                            for slot in range(2):
                                wt.load(sp, c + uo, slot, wt.columns(slot, n, rows[:, bass.ds((2 * c + slot) * P, P)]))

                @block.scalar
                def _(act):
                    norm_scalar(act, s, wt, x, sq, pg[1], eps, tmp, nf, rs, mods, w3, nhi)
                    for n, u0, j0, uo, k_after in parts:
                        def pair(j, last):
                            for q in range(2):
                                k = n if last and q == 1 else DC
                                wt.split_hi(act, j + (u0 + q + 1), 0, k)
                                act.wait_ge(prod_done, j + (j0 + q + 1))
                                act.activation(strided(sa[:, q, :], [HALF, 2], [1, HALF]), pa[q][:, :, 0:HALF],
                                               ACT.Silu).then_inc(silu_done, 1)
                                wt.split_hi(act, j + (u0 + q + 1), 1, k)
                                act.wait_ge(prod_done, j + (j0 + q + 3))
                                act.activation(ghi[:, bass.ds(j + q, 1), :], g32[:, q, :].unsqueeze(1), ACT.Copy).then_inc(gh_done, 1)

                        def chunks(c, last):
                            for slot in range(2):
                                if not last:
                                    wt.split_hi(act, c + (uo + 1), slot, n)
                                elif k_after:
                                    wt.split_hi(act, c + (uo + 1), slot, k_after)

                        peeled(act, n, 2, pair)
                        peeled(act, DC // 2, 1, chunks)

                @block.vector
                def _(dve):
                    dve.sem_inc(prod_done, 2)
                    dve.sem_inc(res_done, 2)
                    wt.credit_vector(dve)
                    for slot in range(2):
                        wt.split_lo(dve, 0, slot, DC)
                    norm_vector(dve, s, x, tmp, nf, rs, mods, w3, nhi, nlo)
                    for c0, (n, u0, j0, uo, k_after) in enumerate(parts):
                        def pair(j, last):
                            for q in range(2):
                                k = n if last and q == 1 else DC
                                for slot in range(2):
                                    wt.split_lo(dve, j + (u0 + q + 1), slot, k)
                                dve.wait_ge(silu_done, j + (j0 + q + 1))
                                dve.wait_ge(wt.mm_done, 2 * (j + (u0 + q)) + 4)
                                dve.tensor_tensor(strided(g32[:, q, :], [HALF, 2], [1, HALF]),
                                                  strided(sa[:, q, :], [HALF, 2], [1, HALF]), pg[q][:, :, 0:HALF],
                                                  ALU.mult).then_inc(prod_done, 1)
                                dve.wait_ge(gh_done, j + (j0 + q + 1))
                                dve.tensor_tensor(glo[:, bass.ds(j + q, 1), :], g32[:, q, :].unsqueeze(1),
                                                  ghi[:, bass.ds(j + q, 1), :].bitcast(F32), ALU.subtract).then_inc(gl_done, 1)

                        def chunks(c, last):
                            for slot in range(2):
                                if not last:
                                    wt.split_lo(dve, c + (uo + 1), slot, n)
                                elif k_after:
                                    wt.split_lo(dve, c + (uo + 1), slot, k_after)
                                dve.wait_ge(wt.mm_done, 2 * (c + uo) + (slot + 3))
                                residual(dve, pa[slot], 2 * c + slot, 3 * w3 + 2, rt[:, slot, :], x_done, res_done,
                                         2 * c + (DC * c0 + slot + 1))

                        peeled(dve, n, 2, pair)
                        peeled(dve, DC // 2, 1, chunks)

                @block.tensor
                def _(pe):
                    wt.credit_tensor(pe)
                    norm_tensor(pe, s, sq, pg[1], ones)

                    def pair(j, u0, j0, q):
                        pe.wait_ge(prod_done, j + (j0 + q + 1))
                        for slot in range(2):
                            wt.product(pe, j + (u0 + q), slot, (pa, pg)[slot][q], nhi, nlo, DC)

                    wt.first_products(pe, (pa[0], pg[0]), nhi, nlo, DC, s.nl_done)
                    pair(0, 0, 0, 1)
                    for c0, (n, u0, j0, uo, _) in enumerate(parts):
                        with pe.Fori(2 if c0 == 0 else 0, n, 2) as j:
                            for q in range(2):
                                pair(j, u0, j0, q)
                        pe.wait_ge(gl_done, j0 + n)
                        with pe.Fori(0, DC // 2) as c:
                            for slot in range(2):
                                pe.wait_ge(res_done, 2 * c + (DC * c0 + slot + 1))
                                wt.product(pe, c + uo, slot, pa[slot], ghi, glo, n)
                        pe.wait_ge(res_done, DC * (c0 + 1) + 2)

        def final_stage():
            with stage(nc, *NormSems.NAMES, "tr_done", "ya_done", "out_done") as sems, ExitStack() as st:
                s = NormSems(sems[0:10])
                tr_done, ya_done, out_done = sems[10:]
                sq, tmp, nf, rs = norm_buffers(st)
                y = sb("y", [P, 5, D], at=st)
                pst = ps("pst", 2, st)
                pt = [ps(f"pt{i}", 2, st) for i in range(2)]
                block = st.enter_context(nc.Block())

                @block.sync
                def _(sp):
                    sp.wait_ge(ya_done, 10)
                    sp.dma_start(o["y_p"][0].rearrange("(t p) d -> p t d", p=P), y[:, 0:4, :]).then_inc(out_done, 16)
                    sp.dma_start(o["y_s"].rearrange("b i d -> (b i) d"), y[0:NSMP, 4, :]).then_inc(out_done, 16)
                    sp.wait_ge(out_done, 32)

                @block.scalar
                def _(act):
                    for c in range(DC):
                        if c >= 2:
                            act.wait_ge(s.st_done, c - 1)
                        act.activation(sq[:, c % 2, :], x[:, c, :], ACT.Square).then_inc(s.sq_done, 1)
                    act.wait_ge(s.st_done, DC)
                    act.activation(strided(rs[:, :], [HALF, 2], [1, HALF]), pst[:, :, 0:HALF], ACT.Sqrt,
                                   bias=eps[:, 0:1], scale=1.0 / D).then_inc(s.sd_done, 1)

                @block.vector
                def _(dve):
                    dve.wait_ge(s.sd_done, 1)
                    dve.reciprocal(rs[:, :], rs[:, :]).then_inc(s.rs_done, 1)
                    dve.wait_ge(s.rs_done, 1)
                    for c in range(DC):
                        dve.scalar_tensor_tensor(x[:, c, :], x[:, c, :], vecs[:, 48 + c:49 + c], rs[:, :], ALU.mult,
                                                 ALU.mult).then_inc(s.xr_done, 1)
                    for n in range(10):
                        t, h = divmod(n, 2)
                        r = TOKT[t][1]
                        dve.wait_ge(tr_done, n + 1)
                        dve.tensor_copy(y[0:r, t, h * 512:(h + 1) * 512], pt[n % 2][0:r, 0, :]).then_inc(ya_done, 1)

                @block.tensor
                def _(pe):
                    norm_tensor(pe, s, sq, pst, ones)
                    pe.wait_ge(s.xr_done, DC)
                    for n in range(10):
                        t, h = divmod(n, 2)
                        t0, r = TOKT[t]
                        if n >= 2:
                            pe.wait_ge(ya_done, n - 1)
                        for k in range(4):
                            mm = pe.transpose(pt[n % 2][0:r, 0, k * P:(k + 1) * P], x[:, 4 * h + k, t0:t0 + r], ident[:, :])
                        mm.then_inc(tr_done, 1)

        def proj_stage(l, nhi, nlo, pj):
            names = Weights.NAMES + NormSems.NAMES + ("ev_done",)
            with stage(nc, *names) as sems, ExitStack() as st:
                s = NormSems(sems[5:15])
                ev_done = sems[15]
                wt = Weights(nc, st, sems[0:5], DC)
                sq, tmp, nf, rs = norm_buffers(st)
                pp = [ps(f"pp{i}", 2, st) for i in range(2)]
                pst = ps("pst", 2, st)
                block = st.enter_context(nc.Block())
                w = a["w_in"][l]
                UQ, UK, UH, UG = 0, R // 2, (R + NKV) // 2, (R + NKV) // 2 + 8

                @block.sync
                def _(sp):
                    with sp.Fori(0, R // 2) as u:
                        for slot in range(2):
                            src = [w[:, bass.ds(u * 2 * DH + slot * DH + g * R * DH, DH)].rearrange("(k p) n -> p k n", p=P)
                                   for g in range(GROUPS)]
                            raw = wt.raw[slot]
                            wt.load(sp, u + UQ, slot, [(raw[:, :, 0:DH], src[0]), (raw[:, 0:4, DH:P], src[1][:, 0:4, :]),
                                                       (raw[:, 4:8, DH:P], src[1][:, 4:8, :])])
                    for n, u0, col in ((NKV // 2, UK, C_KV), (8, UH, C_HG)):
                        with sp.Fori(0, n) as u:
                            for slot in range(2):
                                wt.load(sp, u + u0, slot, wt.columns(slot, DC, w[:, bass.ds(u * 256 + (slot * P + col), P)]))
                    wt.load(sp, UG, 0, wt.columns(0, DC, w[:, C_GATE:C_GATE + P]))

                @block.scalar
                def _(act):
                    norm_scalar(act, s, wt, x, sq, pst, eps, tmp, nf, rs, mods, 1, nhi)
                    with act.Fori(1, UG) as u:
                        for slot in range(2):
                            wt.split_hi(act, u, slot, DC)
                    wt.split_hi(act, UG, 0, DC)

                @block.vector
                def _(dve):
                    dve.sem_inc(ev_done, 2)
                    wt.credit_vector(dve)
                    for slot in range(2):
                        wt.split_lo(dve, 0, slot, DC)
                    norm_vector(dve, s, x, tmp, nf, rs, mods, 1, nhi, nlo)

                    def evacuate(u, slot, chunk, scale):
                        dve.wait_ge(wt.mm_done, 2 * u + (slot + 3))
                        dve.tensor_scalar(pj[:, bass.ds(chunk, 1), :].rearrange("p o (h t) -> p (o h) t", h=2),
                                          pp[slot][:, :, 0:HALF], scale, None, ALU.mult).then_inc(ev_done, 1)

                    for n, u0, chunk, scale in ((R // 2, UQ, Q0, DH ** -0.5), (NKV // 2, UK, KV0, 1.0), (8, UH, HQ0, 1.0)):
                        def pair(u, last):
                            for slot in range(2):
                                if not (last and u0 == UH and slot == 1):
                                    wt.split_lo(dve, u + (u0 + 1), slot, DC)
                                evacuate(u + u0, slot, 2 * u + (chunk + slot), scale)
                        peeled(dve, n, 1, pair)
                    evacuate(UG, 0, GATE0, 1.0)

                @block.tensor
                def _(pe):
                    wt.credit_tensor(pe)
                    norm_tensor(pe, s, sq, pst, ones)
                    wt.first_products(pe, pp, nhi, nlo, DC, s.nl_done)
                    with pe.Fori(1, UG) as u:
                        for slot in range(2):
                            pe.wait_ge(ev_done, 2 * u + (slot + 1))
                            wt.product(pe, u, slot, pp[slot], nhi, nlo, DC)
                    pe.wait_ge(ev_done, 2 * UG + 1)
                    wt.product(pe, UG, 0, pp[0], nhi, nlo, DC)

        def rows_stage(l, pj, kvn, gn):
            with stage(nc, "sig_done", "tr_done", "va_done", "sc_done", "out_done", "gate_out") as (
                    sig_done, tr_done, va_done, sc_done, out_done, gate_out), ExitStack() as st:
                pa = [ps(f"pa{i}", 1, st) for i in range(2)]
                pb = [ps(f"pb{i}", 1, st) for i in range(2)]
                block = st.enter_context(nc.Block())

                @block.scalar
                def _(act):
                    g = pj[0:24, GATE0, :]
                    act.activation(g, g, ACT.Sigmoid).then_inc(sig_done, 1)
                    for t, (t0, r) in enumerate(TOKT):
                        act.wait_ge(tr_done, t + 1)
                        act.activation(kvn[0:r, t, 512:768], pb[t % 2][0:r, 0, 0:256], ACT.Copy).then_inc(sc_done, 1)
                        if t < 4:
                            act.activation(gn[0:r, t, :], pb[t % 2][0:r, 0, 256:280], ACT.Copy)

                @block.vector
                def _(dve):
                    for t, (t0, r) in enumerate(TOKT):
                        dve.wait_ge(tr_done, t + 1)
                        dve.tensor_copy(kvn[0:r, t, 0:512], pa[t % 2][0:r, 0, :]).then_inc(va_done, 1)

                @block.tensor
                def _(pe):
                    pe.wait_ge(sig_done, 1)
                    for t, (t0, r) in enumerate(TOKT):
                        if t >= 2:
                            pe.wait_ge(va_done, t - 1)
                            pe.wait_ge(sc_done, t)
                        for c in range(4):
                            pe.transpose(pa[t % 2][0:r, 0, c * P:(c + 1) * P], pj[:, KV0 + c, t0:t0 + r], ident[:, :])
                        for c in range(2):
                            mm = pe.transpose(pb[t % 2][0:r, 0, c * P:(c + 1) * P], pj[:, KV0 + 4 + c, t0:t0 + r], ident[:, :])
                        if t < 4:
                            mm = pe.transpose(pb[t % 2][0:r, 0, 256:280], pj[0:24, GATE0, t0:t0 + r], ident[0:24, 0:24])
                        mm.then_inc(tr_done, 1)

                @block.sync
                def _(sp):
                    sp.wait_ge(sig_done, 1)
                    sp.dma_start(gate_dram.rearrange("b g i -> g b i"), pj[0:3 * HEADS, GATE0, SEQ:T].rearrange("g (b i) -> g b i", i=NI)).then_inc(gate_out, 16)
                    sp.wait_ge(va_done, 5)
                    sp.wait_ge(sc_done, 5)
                    sp.dma_start(o["kv_p"][l, 0].rearrange("(t p) k g d -> p t (k g d)", p=P), kvn[:, 0:4, 0:512]).then_inc(out_done, 16)
                    sp.dma_start(o["win_p"][l, 0].rearrange("(t p) k g d -> p t (k g d)", p=P), kvn[:, 0:4, 512:768]).then_inc(out_done, 16)
                    sp.dma_start(o["kv_s"][l].rearrange("b i k g d -> (b i) (k g d)"), kvn[0:NSMP, 4, 0:512]).then_inc(out_done, 16)
                    for b in range(NB):
                        sp.dma_start(o["win_s"][l, b, PAST - NI:PAST].rearrange("i k g d -> i (k g d)"),
                                     kvn[NI * b:NI * b + NI, 4, 512:768]).then_inc(out_done, 16)
                    sp.wait_ge(out_done, 16 * (3 + NB))
                    sp.wait_ge(gate_out, 16)

        def compress_stage(l, pj, kct, vcn):
            NM = CMP_STRIDE // 2
            with stage(nc, "rows0", "rows1", "rows2", "rows3", "w_in", "tr_done", "ca_done", "cb_done", "silu_done", "o_done",
                       "oe_done", "x_done") as (rows0, rows1, rows2, rows3, w_in, tr_done, ca_done, cb_done, silu_done,
                                                o_done, oe_done, x_done), ExitStack() as st:
                rows_in = [rows0, rows1, rows2, rows3]
                cn = [sb(f"cn{i}", [P, NPAGE, P], at=st) for i in range(4)]
                ct = sb("ct", [P, GROUPS, NM, NSEQ, NSUB], at=st)
                w1 = sb("w1", [P, 2, 2, NM, P], at=st)
                w2 = sb("w2", [P, 2, DH], at=st)
                sh = sb("sh", [P, 2, NSEQ * NCMP], at=st)
                pt = [ps(f"pt{i}", 1, st) for i in range(2)]
                ph = [ps(f"ph{i}", 1, st) for i in range(2)]
                po = [ps(f"po{i}", 2, st) for i in range(2)]
                block = st.enter_context(nc.Block())

                @block.sync
                def _(sp):
                    for kv in range(2):
                        for b in range(NB):
                            if NB * kv + b >= 4:
                                sp.wait_ge(tr_done, NB * kv + b - 3)
                            for n in range(NPAGE):
                                page = sp.value_load(pages[0:1, NPAGE * b + n:NPAGE * b + n + 1], min_val=0, max_val=NPOOL - 1)
                                sp.dma_start(cn[b % 4][:, n, :], a["cache_nsa_kv"][l][bass.ds(page, 1), :, kv].rearrange(
                                    "o p g d -> (o p) (g d)")).then_inc(rows_in[b % 4], 16)
                            if kv == 0 and b < 2:
                                for j in range(2):
                                    sp.dma_start(w1[j * DH:(j + 1) * DH, b, :, :, :],
                                                 a["cmp_w1"][l, b, :, j::2].rearrange("r m d e -> d r m e")).then_inc(w_in, 16)
                                sp.dma_start(w2[:, b, :], a["cmp_w2"][l, b]).then_inc(w_in, 16)

                def gather(engine, g, kv, done):
                    if kv:
                        engine.wait_ge(x_done, g + 1)
                    for s in (NSEQ - 1, *range(NB)):
                        rows = slice(g * DH, (g + 1) * DH)
                        if s < NB:
                            engine.wait_ge(tr_done, NB * kv + s + 1)
                            src = pt[s % 2][rows, 0, :]
                        else:
                            src = pj[rows, KV0 + kv, 0:SEQ]
                        for parity in range(2):
                            dst, v = ct[parity * DH:(parity + 1) * DH, g, :, s, :], strided(src[:, parity:], [2, NM], [CMP_STRIDE, NSUB])
                            if g == 0:
                                ins = engine.activation(dst, v, ACT.Copy)
                            else:
                                ins = engine.tensor_copy(dst, v)
                        ins.then_inc(done, 1)

                @block.tensor
                def _(pe):
                    def hidden(q):
                        kv, g = divmod(q, 2)
                        if q >= 2:
                            pe.wait_ge(silu_done, q - 1)
                        pe.wait_ge((ca_done, cb_done)[g], NSEQ * (kv + 1))
                        for m in range(NM):
                            for r in range(2):
                                mm = pe.matmul(ph[q % 2][:, 0, 0:NSEQ * NCMP].rearrange("p (s n) -> p s n", n=NCMP),
                                               w1[:, kv, r, m, :], ct[:, g, m, :, r:r + NCMP], start=(m == 0 and r == 0),
                                               stop=(m == NM - 1 and r == 1))
                        mm.then_inc(x_done, 1)

                    def output(q):
                        kv, g = divmod(q, 2)
                        pe.wait_ge(silu_done, q + 1)
                        if q >= 2:
                            pe.wait_ge(oe_done, q - 1)
                        if kv == 0:
                            mm = pe.matmul(po[q % 2][g * DH:(g + 1) * DH, 0, 0:NSEQ * NCMP], w2[:, 0, :], sh[:, q % 2, :],
                                           start=True, stop=True)
                        else:
                            for b in range(NSEQ):
                                mm = pe.matmul(po[q % 2][0:NCMP, b // NB, (b % NB) * DH:(b % NB) * DH + DH],
                                               sh[:, q % 2, b * NCMP:(b + 1) * NCMP], w2[:, 1, :], start=True, stop=True)
                        mm.then_inc(o_done, 1)

                    for kv in range(2):
                        for b in range(NB):
                            pe.wait_ge(rows_in[b % 4], 64 * (2 * kv + b // 4 + 1))
                            if NB * kv + b >= 2:
                                before = NB * kv + b - 2
                                pe.wait_ge(ca_done, before + before // NB + 2)
                                pe.wait_ge(cb_done, before + before // NB + 2)
                            for n in range(NPAGE):
                                mm = pe.transpose(pt[b % 2][:, 0, n * P:(n + 1) * P], cn[b % 4][:, n, :], ident[:, :])
                            mm.then_inc(tr_done, 1)
                        if kv == 0:
                            pe.wait_ge(w_in, 16 * 6)
                        for g in range(GROUPS):
                            hidden(2 * kv + g)
                        for g in range(GROUPS):
                            output(2 * kv + g)

                @block.vector
                def _(dve):
                    for q in range(4):
                        kv, g = divmod(q, 2)
                        if g == 0:
                            gather(dve, 1, kv, cb_done)
                        dve.wait_ge(o_done, q + 1)
                        if kv == 0:
                            src = po[q % 2][g * DH:(g + 1) * DH, 0, 0:NSEQ * NCMP]
                            b2 = vecs[g * DH:(g + 1) * DH, bass.ds(60 + l * 2, 1)]
                            dve.tensor_scalar(kct[g * DH:(g + 1) * DH, :], src, b2, None, ALU.add).then_inc(oe_done, 1)
                        else:
                            row = b2row[0:NCMP, bass.ds(l, 1), :]
                            dve.tensor_tensor(vcn[:, 0:NB, g * DH:(g + 1) * DH],
                                              po[q % 2][0:NCMP, 0, :].rearrange("p (b d) -> p b d", d=DH),
                                              strided(row, [0, NB], [1, DH]), ALU.add)
                            dve.tensor_tensor(vcn[:, NB, g * DH:(g + 1) * DH], po[q % 2][0:NCMP, 1, 0:DH], row[:, 0, :],
                                              ALU.add).then_inc(oe_done, 1)

                @block.scalar
                def _(act):
                    for q in range(4):
                        kv, g = divmod(q, 2)
                        if g == 0:
                            gather(act, 0, kv, ca_done)
                        act.wait_ge(x_done, q + 1)
                        if q >= 2:
                            act.wait_ge(o_done, q - 1)
                        act.activation(sh[:, q % 2, :], ph[q % 2][:, 0, 0:NSEQ * NCMP], ACT.Silu,
                                       bias=vecs[:, bass.ds(56 + l * 2 + kv, 1)]).then_inc(silu_done, 1)

        def attention_stage(l, pj, kvn, gn, kct, vcn, oa):
            NU = 8
            with stage(nc, "q_done", "tz_in", "s_done", "max_done", "neg_done", "exp_done", "w_done", "p_done", "t_done", "pt_act",
                       "pt_dve", "pv_done", "o_done") as (q_done, tz_in, s_done, max_done, neg_done, exp_done, w_done, p_done,
                                                          t_done, pt_act, pt_dve, pv_done, o_done), ExitStack() as st:
                tz = sb("tz", [P, HEADS, SEQ], at=st)
                qs = sb("qs", [P, 2, P], at=st)
                bs = sb("bs", [P, 2, SEQ], at=st)
                sc = sb("sc", [P, 2, 2 * SEQ + 32], at=st)
                pT = sb("pT", [P, 2, 2 * SEQ + P], at=st)
                mx = sb("mx", [P, 2, 3], at=st)
                start = sb("start", [P, 2], at=st)
                begun = sb("begun", [P, 2], at=st)
                neg = sb("neg", [P, 2, 3], at=st)
                rsum = sb("rsum", [P, 2, 3], at=st)
                wgt = sb("wgt", [P, 2, 3], at=st)
                ps_sel, ps_win, ps_cmp, pt_sel, pt_win, pt_cmp = (ps(n, 1, st) for n in ("ss", "sw", "sc", "ts", "tw", "tc"))
                po = [ps(f"po{i}", 1, st) for i in range(2)]
                block = st.enter_context(nc.Block())

                def unit(k):
                    g, qi = divmod(k % NU, 4)
                    return g, qi, P * (qi + 1), 7 + 8 * qi

                @block.sync
                def _(sp):
                    sp.dma_start(tz[:, :, :], bass.AP(rv_dram.tensor, rv_dram.offset + P - 1, [[639, P], [640 * P, HEADS], [1, SEQ]])).then_inc(tz_in, 16)

                @block.tensor
                def _(pe):
                    def scores(r, k):
                        g, qi, w, nc_ = unit(k)
                        rows = slice(g * DH, (g + 1) * DH)
                        q = qs[rows, k % 2, :]
                        pe.wait_ge(q_done, 2 * (NU * r + k) + 1)
                        pe.wait_ge(max_done, 3 * (NU * r + k) + 3)
                        pe.matmul(ps_cmp[:, 0, 0:nc_], q, kct[rows, NB * NCMP:NB * NCMP + nc_], start=True, stop=True)
                        pe.matmul(ps_sel[:, 0, 0:w], q, pj[rows, KV0 + 2, 0:w], start=True, stop=True)
                        pe.matmul(ps_win[:, 0, 0:w], q, pj[rows, KV0 + 4, 0:w], start=True, stop=True).then_inc(s_done, 1)

                    def turn(r, k):
                        g, qi, w, nc_ = unit(k)
                        u = NU * r + k
                        pe.wait_ge(p_done, 3 * u + 3)
                        pe.wait_ge(pt_act, u + 1)
                        pe.wait_ge(pt_dve, 2 * u + 2)
                        pe.transpose(pt_cmp[0:nc_, 0, 0:P], sc[:, k % 2, 2 * SEQ:2 * SEQ + nc_], ident[:, :])
                        for half, out in ((0, pt_sel), (1, pt_win)):
                            for t in range(qi + 1):
                                mm = pe.transpose(out[:, 0, t * P:(t + 1) * P], sc[:, k % 2, half * SEQ + t * P:half * SEQ + (t + 1) * P], ident[:, :])
                        mm.then_inc(t_done, 1)

                    def values(r, k):
                        g, qi, w, nc_ = unit(k)
                        u = NU * r + k
                        pe.wait_ge(pt_act, u + 2)
                        pe.wait_ge(pt_dve, 2 * u + 4)
                        pe.wait_ge(o_done, u + 1)
                        out = po[k % 2][g * DH:(g + 1) * DH, 0, 0:P]
                        pe.matmul(out, vcn[0:nc_, NB, g * DH:(g + 1) * DH], pT[0:nc_, k % 2, 2 * SEQ:], start=True, stop=False)
                        for half, col in ((0, 3 * P), (1, 5 * P)):
                            for t in range(qi + 1):
                                mm = pe.matmul(out, kvn[:, t, col + g * DH:col + (g + 1) * DH], pT[:, k % 2, half * SEQ + t * P:half * SEQ + (t + 1) * P],
                                               start=False, stop=(half == 1 and t == qi))
                        mm.then_inc(pv_done, 1)

                    def head(r, last):
                        for k in range(NU):
                            if k + 1 < NU or not last:
                                scores(r, k + 1)
                            if k >= 1:
                                values(r, k - 1)
                            turn(r, k)
                        values(r, NU - 1)

                    scores(0, 0)
                    peeled(pe, R, 1, head)

                @block.vector
                def _(dve):
                    dve.sem_inc(max_done, 3)
                    dve.sem_inc(pt_dve, 2)
                    dve.sem_inc(w_done, 6)

                    def maxima(r, k):
                        g, qi, w, nc_ = unit(k)
                        u = NU * r + k
                        i = k % 2
                        dve.wait_ge(q_done, 2 * u + 2)
                        dve.wait_ge(s_done, u + 1)
                        dve.wait_ge(t_done, u + 1)
                        dve.memset(start[:, i:i + 1], 0.0)
                        for n, (dst, src, b, lo, width) in enumerate((
                                (2 * SEQ, ps_cmp, bs[:, i, 31:w:16], 2, nc_),
                                (0, ps_sel, bs[:, i, 0:w], 0, w),
                                (SEQ, ps_win, bs[:, i, 0:w], 1, w))):
                            dve.tensor_tensor_reduce(sc[:, i, dst:dst + width], src[:, 0, 0:width], b, 1.0, 3 * FLOOR, ALU.add,
                                                     ALU.max, mx[:, i, lo:lo + 1]).then_inc(max_done, 1)
                        dve.wait_ge(max_done, 3 * u + 6)
                        dve.tensor_scalar(neg[:, i, :], mx[:, i, :], FLOOR, -1.0, ALU.max, ALU.mult).then_inc(neg_done, 1)

                    def weigh(r, k):
                        g, qi, w, nc_ = unit(k)
                        u = NU * r + k
                        i = k % 2
                        dve.wait_ge(exp_done, 3 * u + 3)
                        dve.tensor_scalar(wgt[:, i, :], rsum[:, i, :], 1e-30, None, ALU.max).then_inc(w_done, 1)
                        dve.wait_ge(w_done, 3 * u + 7)
                        dve.reciprocal(wgt[:, i, :], wgt[:, i, :]).then_inc(w_done, 1)
                        dve.wait_ge(w_done, 3 * u + 8)
                        gate = gn[:, qi, bass.ds(r + g * R, 17)]
                        dve.tensor_tensor(wgt[:, i, :], wgt[:, i, :], strided(gate, [HEADS, 3]), ALU.mult).then_inc(w_done, 1)
                        dve.wait_ge(w_done, 3 * u + 9)
                        for dst, br, width in ((2 * SEQ, 0, nc_), (0, 1, w), (SEQ, 2, w)):
                            v = sc[:, i, dst:dst + width]
                            dve.tensor_scalar(v, v, wgt[:, i, br:br + 1], None, ALU.mult).then_inc(p_done, 1)

                    def copy_turned(r, k):
                        g, qi, w, nc_ = unit(k)
                        u = NU * r + k
                        dve.wait_ge(t_done, u + 3)
                        dve.wait_ge(pv_done, u + 1)
                        dve.tensor_copy(pT[0:nc_, k % 2, 2 * SEQ:], pt_cmp[0:nc_, 0, 0:P]).then_inc(pt_dve, 1)
                        dve.tensor_copy(pT[:, k % 2, SEQ:SEQ + w], pt_win[:, 0, 0:w]).then_inc(pt_dve, 1)

                    def head(r, last):
                        for k in range(NU):
                            weigh(r, k)
                            if k + 1 < NU or not last:
                                maxima(r, k + 1)
                            copy_turned(r, k)

                    maxima(0, 0)
                    peeled(dve, R, 1, head)

                @block.scalar
                def _(act):
                    act.sem_inc(pt_act, 1)
                    act.sem_inc(o_done, 2)

                    def exps(r, k):
                        g, qi, w, nc_ = unit(k)
                        u = NU * r + k
                        i = k % 2
                        act.wait_ge(neg_done, u + 1)
                        act.wait_ge(w_done, 3 * u + 1)
                        for dst, n, br, width in ((2 * SEQ, 2, 0, nc_), (0, 0, 1, w), (SEQ, 1, 2, w)):
                            v = sc[:, i, dst:dst + width]
                            act.activation(v, v, ACT.Exp, bias=neg[:, i, n:n + 1], accum_out=rsum[:, i, br:br + 1]).then_inc(exp_done, 1)

                    def copy_turned(r, k):
                        g, qi, w, nc_ = unit(k)
                        u = NU * r + k
                        act.wait_ge(t_done, u + 3)
                        act.wait_ge(pv_done, u + 1)
                        act.activation(pT[:, k % 2, 0:w], pt_sel[:, 0, 0:w], ACT.Copy).then_inc(pt_act, 1)

                    def outputs(r, k):
                        g, qi, w, nc_ = unit(k)
                        u = NU * r + k
                        rows = slice(g * DH, (g + 1) * DH)
                        act.wait_ge(pv_done, u + 3)
                        act.activation(oa[rows, bass.ds(r, 1), qi * P:(qi + 1) * P], po[k % 2][rows, 0, 0:P].unsqueeze(1),
                                       ACT.Copy).then_inc(o_done, 1)

                    def head(r, last):
                        for k in range(NU):
                            if k >= 1:
                                outputs(r, k - 1)
                            if k + 1 < NU or not last:
                                exps(r, k + 1)
                            copy_turned(r, k)
                        outputs(r, NU - 1)

                    exps(0, 0)
                    peeled(act, R, 1, head)

                @block.gpsimd
                def _(pool):
                    pool.sem_inc(t_done, 2)
                    pool.sem_inc(pv_done, 2)
                    pool.wait_ge(tz_in, 16)
                    with pool.Fori(0, R) as r:
                        for k in range(NU):
                            g, qi, w, nc_ = unit(k)
                            pool.wait_ge(max_done, 3 * (NU * r + k) + 1)
                            pool.tensor_tensor(begun[:, k % 2:k % 2 + 1], ones[:, 0:1], ones[:, 0:1], ALU.mult)
                            pool.tensor_copy(qs[:, k % 2, :].unsqueeze(1), pj[:, bass.ds(r, 1), qi * P:(qi + 1) * P]).then_inc(q_done, 1)
                            pool.tensor_copy(bs[:, k % 2, 0:w].unsqueeze(1), tz[:, bass.ds(r + g * R, 1), SEQ - w:SEQ]).then_inc(q_done, 1)

        def sample_stage(l, pj, kvn, kct, vcn, oa):
            with stage(nc, "in0", "in1", "in2", "in3", "gs_in", "win_out", "qbd_done", "kt_done", "ka_done", "kb_done",
                       "s_done", "sa_done", "mx_done", "neg_done", "exp_done", "w_done", "p_done", "t_done", "ta_done",
                       "tb_done", "pv_done", "o_done", "sq_done") as (
                    in0, in1, in2, in3, gs_in, win_out, qbd_done, kt_done, ka_done, kb_done, s_done, sa_done, mx_done,
                    neg_done, exp_done, w_done, p_done, t_done, ta_done, tb_done, pv_done, o_done, sq_done), ExitStack() as st:
                rows_in = [in0, in1, in2, in3]
                kv = sb("kv", [P, 4, 2, 4, 2 * P], at=st)
                kT = sb("kT", [P, 2, 2, PAST], at=st)
                qbd = sb("qbd", [P, NB, GROUPS, R, NI], at=st)
                gs = sb("gs", [P, 2, 3], at=st)
                sc = sb("sc", [P, 2, PAST + NSMP], at=st)
                scc = sb("scc", [P, 32], at=st)
                pT = sb("pT", [P, 2, 5, P], at=st)
                pTc = sb("pTc", [32, P], at=st)
                mx = sb("mx", [P, 2, 5], at=st)
                m3 = sb("m3", [P, 2, 3], at=st)
                rsum = sb("rsum", [P, 2, 3], at=st)
                wgt = sb("wgt", [P, 2, 3], at=st)
                pk = [ps(f"pk{i}", 1, st) for i in range(2)]
                pss = [ps(f"pss{i}", 1, st) for i in range(2)]
                psn = ps("psn", 1, st)
                ptn = ps("ptn", 1, st)
                po = ps("po", 1, st)
                block = st.enter_context(nc.Block())
                BRANCH = (scc[:, 0:NCMP], sc[:, 0, :], sc[:, 1, :])

                def write_window(sp, b):
                    sp.wait_ge(rows_in[b % 4], 80 * (b // 4 + 1))
                    sp.dma_start(o["win_s"][l, b, 0:PAST - NI].rearrange("(p t) k g d -> p t (k g d)", t=4),
                                 kv[1:P, b % 4, 1, :, :]).then_inc(win_out, 16)

                @block.sync
                def _(sp):
                    for b in range(NB):
                        sp.dma_start(gs[32 * (b % 4):32 * (b % 4) + 32, b // 4, :],
                                     gate_dram[b].rearrange("(r h) i -> (h i) r", r=3),
                                     allow_slow_non_contiguous=True).then_inc(gs_in, 16)
                    for b in range(NB):
                        j = b % 4
                        if b >= 4:
                            sp.wait_ge(pv_done, 1)
                            sp.wait_ge(win_out, 16 * (b - 3))
                        for n in range(4):
                            page = sp.value_load(pages[0:1, 4 * b + n:4 * b + n + 1], min_val=0, max_val=NPOOL - 1)
                            src = a["cache_nsa_kv"][l][bass.ds(page, 1)].rearrange("o (p t) k g d -> (o p) t (k g d)", t=4)
                            sp.dma_start(kv[32 * n:32 * n + 32, j, 0, :, :], src[:, :, 2 * P:4 * P]).then_inc(rows_in[j], 16)
                        sp.dma_start(kv[:, j, 1, :, :], a["state_win_kv"][l, b].rearrange("(p t) k g d -> p t (k g d)", t=4)).then_inc(rows_in[j], 16)
                        if b >= 3:
                            write_window(sp, b - 3)
                    for b in range(NB - 3, NB):
                        write_window(sp, b)
                    sp.wait_ge(win_out, 16 * NB)

                @block.tensor
                def _(pe):
                    for half in range(2):
                        for j in range(4):
                            b = 4 * half + j
                            pe.wait_ge(rows_in[j], 80 * (half + 1))
                            if half or j:
                                pe.wait_ge(ka_done, b)
                                pe.wait_ge(kb_done, b)
                            if half and j == 0:
                                pe.wait_ge(ta_done, 1)
                                pe.wait_ge(tb_done, 1)
                            for br in range(2):
                                for t in range(4):
                                    mm = pe.transpose(pk[br][:, 0, t * P:(t + 1) * P], kv[:, j, br, t, 0:P], ident[:, :])
                            mm.then_inc(kt_done, 1)
                            pe.wait_ge(ka_done, b + 1)
                            pe.wait_ge(kb_done, b + 1)
                            pe.wait_ge(qbd_done, 2)
                            if half and j == 0:
                                pe.wait_ge(sa_done, 5)
                            rows = slice(32 * j, 32 * j + 32)
                            q = qbd[:, b, :, :, :]
                            for br in range(2):
                                pe.matmul(pss[br][rows, 0, :], q, kT[:, b % 2, br, :], start=True, stop=True)
                            for br in range(2):
                                pe.matmul(psn[rows, 0, br * NSMP:(br + 1) * NSMP], q, pj[:, KV0 + 2 + 2 * br, SEQ:T], start=True, stop=True)
                            mm = pe.matmul(psn[rows, 0, 64:64 + NCMP], q, kct[:, b * NCMP:(b + 1) * NCMP], start=True, stop=True)
                            mm.then_inc(s_done, 1)
                        pe.wait_ge(p_done, 3 * (half + 1))
                        for br in range(2):
                            for t in range(4):
                                pe.transpose(pk[br][:, 0, t * P:(t + 1) * P], sc[:, br, t * P:(t + 1) * P], ident[:, :])
                        for br in range(2):
                            pe.transpose(ptn[0:NSMP, 0, br * P:(br + 1) * P], sc[:, br, PAST:PAST + NSMP], ident[:, :])
                        mm = pe.transpose(ptn[0:NCMP, 0, 2 * P:3 * P], scc[:, 0:NCMP], ident[:, :])
                        mm.then_inc(t_done, 1)
                        pe.wait_ge(ta_done, half + 1)
                        pe.wait_ge(tb_done, half + 1)
                        if half:
                            pe.wait_ge(o_done, 2)
                        for j in range(4):
                            b = 4 * half + j
                            cols = slice(32 * j, 32 * j + 32)
                            out = po[:, 0, cols]
                            pe.matmul(out, vcn[0:NCMP, b, :], pTc[0:NCMP, cols], start=True, stop=False)
                            for br in range(2):
                                for t in range(4):
                                    pe.matmul(out, kv[:, j, br, t, P:2 * P], pT[:, br, t, cols], start=False, stop=False)
                                mm = pe.matmul(out, kvn[0:NSMP, 4, (3 + 2 * br) * P:(4 + 2 * br) * P], pT[0:NSMP, br, 4, cols],
                                               start=False, stop=(br == 1))
                        mm.then_inc(pv_done, 1)

                @block.vector
                def _(dve):
                    dve.memset(qbd[:, :, :, :, :], 0.0).then_inc(sq_done, 1)
                    dve.wait_ge(sq_done, 1)
                    for g in range(GROUPS):
                        rows = slice(g * DH, (g + 1) * DH)
                        dve.tensor_copy(qbd[rows, :, g, :, :], pj[rows, Q0:Q0 + R, SEQ:T].rearrange("p r (b i) -> p b r i", i=NI)).then_inc(qbd_done, 1)
                    dve.wait_ge(gs_in, 16 * NB)
                    for half in range(2):
                        for j in range(4):
                            b = 4 * half + j
                            dve.wait_ge(kt_done, b + 1)
                            if b >= 2:
                                dve.wait_ge(s_done, b - 1)
                            dve.tensor_copy(kT[:, b % 2, 1, :], pk[1][:, 0, :]).then_inc(kb_done, 1)
                        dve.wait_ge(s_done, 4 * half + 4)
                        if half:
                            dve.wait_ge(t_done, 1)
                        for n, (out, src, bias) in enumerate((
                                (scc[:, 0:NCMP], psn[:, 0, 64:64 + NCMP], bias_cmp[:, :]),
                                (sc[:, 0, 0:PAST], pss[0][:, 0, :], bias_old[:, 0, :]),
                                (sc[:, 1, 0:PAST], pss[1][:, 0, :], bias_old[:, 1, :]),
                                (sc[:, 0, PAST:PAST + NSMP], psn[:, 0, 0:NSMP], bias_new[:, half, :]),
                                (sc[:, 1, PAST:PAST + NSMP], psn[:, 0, NSMP:2 * NSMP], bias_new[:, half, :]))):
                            dve.tensor_tensor_reduce(out, src, bias, 1.0, 3 * FLOOR, ALU.add, ALU.max, mx[:, half, n:n + 1]).then_inc(sa_done, 1)
                        dve.wait_ge(sa_done, 5 * half + 5)
                        dve.tensor_copy(m3[:, half, 0:1], mx[:, half, 0:1]).then_inc(mx_done, 1)
                        dve.tensor_tensor(m3[:, half, 1:3], mx[:, half, 1:3], mx[:, half, 3:5], ALU.max).then_inc(mx_done, 1)
                        dve.wait_ge(mx_done, 2 * half + 2)
                        dve.tensor_scalar(m3[:, half, :], m3[:, half, :], FLOOR, -1.0, ALU.max, ALU.mult).then_inc(neg_done, 1)
                        dve.wait_ge(exp_done, 3 * half + 3)
                        dve.tensor_scalar(wgt[:, half, :], rsum[:, half, :], 1e-30, None, ALU.max).then_inc(w_done, 1)
                        dve.wait_ge(w_done, 3 * half + 1)
                        dve.reciprocal(wgt[:, half, :], wgt[:, half, :]).then_inc(w_done, 1)
                        dve.wait_ge(w_done, 3 * half + 2)
                        dve.tensor_tensor(wgt[:, half, :], wgt[:, half, :], gs[:, half, :], ALU.mult).then_inc(w_done, 1)
                        dve.wait_ge(w_done, 3 * half + 3)
                        for br in range(3):
                            v = BRANCH[br]
                            dve.tensor_scalar(v, v, wgt[:, half, br:br + 1], None, ALU.mult).then_inc(p_done, 1)
                        dve.wait_ge(t_done, half + 1)
                        dve.tensor_copy(pT[0:NSMP, :, 4, :], ptn[0:NSMP, 0, 0:2 * P].rearrange("p (b q) -> p b q", b=2))
                        dve.tensor_copy(pTc[0:NCMP, :], ptn[0:NCMP, 0, 2 * P:3 * P])
                        dve.tensor_copy(pT[:, 1, 0:4, :], pk[1][:, 0, :].rearrange("p (t q) -> p t q", t=4)).then_inc(tb_done, 1)
                        dve.wait_ge(pv_done, half + 1)
                        for g in range(GROUPS):
                            rows = slice(g * DH, (g + 1) * DH)
                            for j in range(4):
                                b = 4 * half + j
                                ins = dve.tensor_copy(oa[rows, 0:R, SEQ + NI * b:SEQ + NI * b + NI],
                                                      po[rows, 0, 32 * j + 16 * g:32 * j + 16 * g + 16].rearrange("p (r i) -> p r i", i=NI))
                            ins.then_inc(o_done, 1)

                @block.scalar
                def _(act):
                    for half in range(2):
                        for j in range(4):
                            b = 4 * half + j
                            act.wait_ge(kt_done, b + 1)
                            if b >= 2:
                                act.wait_ge(s_done, b - 1)
                            act.activation(kT[:, b % 2, 0, :], pk[0][:, 0, :], ACT.Copy).then_inc(ka_done, 1)
                        act.wait_ge(neg_done, half + 1)
                        for br in range(3):
                            v = BRANCH[br]
                            act.activation(v, v, ACT.Exp, bias=m3[:, half, br:br + 1], accum_out=rsum[:, half, br:br + 1]).then_inc(exp_done, 1)
                        act.wait_ge(t_done, half + 1)
                        act.activation(pT[:, 0, 0:4, :], pk[0][:, 0, :].rearrange("p (t q) -> p t q", t=4), ACT.Copy).then_inc(ta_done, 1)

        def hgrn_stage(l, pj, ob):
            NL = len(LEVELS) - 1
            W = HG * T
            with stage(nc, "sin", "mask_in", "sig_done", "aff_done", "ln_done", "set_done", "b_done", "d_done", "e_done",
                       "g_done", "a_done", "cp_done", "tr_done", "ie_done", "qe_done", "kt_done", "ke_done", "po_done",
                       "oe_done", "st_done", "su_done", "kd_done", "sp_done", "ss_done", "out_done", "sq_done", "n_done",
                       "r_done", "f_done", "mul_done", "hv_done") as (
                    sin, mask_in, sig_done, aff_done, ln_done, set_done, b_done, d_done, e_done, g_done, a_done, cp_done,
                    tr_done, ie_done, qe_done, kt_done, ke_done, po_done, oe_done, st_done, su_done, kd_done, sp_done,
                    ss_done, out_done, sq_done, n_done, r_done, f_done, mul_done, hv_done), ExitStack() as st:
                q, k, g = (pj[:, c:c + HG, :] for c in (HQ0, HF0, HO0))
                f1 = sb("f1", [P, HG, T], at=st)
                bc = sb("bc", [P, HG, T], at=st)
                g1 = sb("g1", [P, HG, T], at=st)
                dd = [f1[:, :, :], pj[:, 0:4, :]]
                gg = [pj[:, 4:8, :], g1[:, :, :]]
                rows = sb("rows", [P, 5, HG * P], at=st)
                at = sb("at", [P, 4, HG, P], at=st)
                ats = sb("ats", [NSMP, HG, NSMP], at=st)
                keep = sb("keep", [P, T], at=st)
                state = sb("state", [P, HG, P], at=st)
                ss = sb("ss", [P, NB, HG, P], at=st)
                level = sb("level", [P, len(LEVELS), P], at=st)
                flat = pj[:, :, :].rearrange("p c t -> p (c t)")
                kn = [flat[:, t * HG * P:(t + 1) * HG * P] for t in range(4)] + [flat[0:NSMP, 8 * T:8 * T + HG * P]]
                kd = [flat[0:NSMP, 8 * T - (i + 1) * 512:8 * T - i * 512] for i in range(2)]
                rt = pj[:, HI0:HI0 + HG, :]
                bank = [ps(f"b{i}", 1, st) for i in range(8)]
                block = st.enter_context(nc.Block())

                def tiles(n):
                    return 4 if n < NL and LEVELS[n] > 2 else 5

                def before(n, t=0):
                    return sum(tiles(i) for i in range(n)) + t

                def halves(n):
                    size = LEVELS[n]
                    blocks = (SEQ if size > 2 else T) // (2 * size)
                    return size, [T, HG], [2 * size, blocks], [1, size]

                @block.sync
                def _(sp):
                    sp.dma_start(level[:, :, :], a["c_level"]).then_inc(mask_in, 16)
                    for rows_ in (slice(0, P // 2), slice(P // 2, P)):
                        sp.dma_start(ss[rows_, :, :, :], a["state_hgrn"][l, :, :, rows_].rearrange("b h k v -> k b h v")).then_inc(sin, 16)
                    sp.wait_ge(su_done, 16)
                    sp.dma_start(o["hg_p"][l, 0].rearrange("h k v -> k h v"), state[:, :, :]).then_inc(out_done, 16)
                    sp.wait_ge(ss_done, 2 * NB)
                    sp.dma_start(o["hg_s"][l].rearrange("b h k v -> k b h v"), ss[:, :, :, :]).then_inc(out_done, 16)
                    sp.wait_ge(out_done, 32)

                @block.scalar
                def _(act):
                    act.activation(f1[:, :, :], k, ACT.Sigmoid).then_inc(sig_done, 1)
                    act.wait_ge(sig_done, 1)
                    act.activation(k, k, ACT.Sigmoid, scale=-1.0).then_inc(sig_done, 1)
                    act.activation(q, q, ACT.Silu).then_inc(sig_done, 1)
                    act.activation(g, g, ACT.Silu).then_inc(sig_done, 1)
                    for t in range(5):
                        r = TOKT[t][1]
                        act.wait_ge(tr_done, t + 1)
                        act.activation(rows[0:r, t, :], bank[5 + t % 2][0:r, 0, :], ACT.Copy).then_inc(ie_done, 1)
                    act.wait_ge(aff_done, 9)
                    act.activation(f1[:, :, :], f1[:, :, :], ACT.Ln).then_inc(ln_done, 1)
                    for n in range(NL + 2):
                        if n == NL:
                            act.wait_ge(g_done, 2 * NL)
                        else:
                            act.wait_ge(d_done, 2 * min(n, NL) + 2)
                        d = dd[n % 2] if n <= NL else pj[:, 0:4, :]
                        d = f1[:, :, :] if n == NL else d
                        if n < NL and LEVELS[n] > 2:
                            d = d[:, :, 0:SEQ]
                        act.activation(d, bc[:, :, :] if n == NL else d, ACT.Exp).then_inc(e_done, 1)
                    for t in range(5):
                        t0, r = TOKT[t]
                        act.wait_ge(po_done, t + 1)
                        act.activation(ob[:, :, t0:t0 + r], bank[t % 2][:, 0, 0:HG * r].rearrange("p (h t) -> p h t", h=HG),
                                       ACT.Copy).then_inc(oe_done, 1)
                    act.wait_ge(oe_done, 5)
                    act.activation(g1[:, :, :], ob[:, :, :], ACT.Square).then_inc(sq_done, 1)
                    rf = rt.rearrange("p h t -> p (h t)")
                    for c in range(5):
                        w = min(512, W - 512 * c)
                        act.wait_ge(n_done, c + 1)
                        act.activation(rf[:, 512 * c:512 * c + w], bank[(0, 1, 5, 6, 7)[c]][:, 0, 0:w], ACT.Sqrt,
                                       bias=eps[:, 0:1], scale=1.0 / P).then_inc(r_done, 1)

                @block.vector
                def _(dve):
                    dve.memset(at[:, :, :, :], 0.0).then_inc(set_done, 1)
                    dve.memset(ats[:, :, :], 0.0).then_inc(set_done, 1)
                    dve.memset(keep[:, :], 1.0).then_inc(set_done, 1)
                    dve.wait_ge(set_done, 3)
                    dve.memset(keep[:, 0:SEQ:P], 0.0).then_inc(set_done, 1)
                    dve.memset(keep[:, SEQ:T:NI], 0.0).then_inc(set_done, 1)
                    dve.wait_ge(sig_done, 2)
                    lbl = lb[:, bass.ds(l, 1), :]
                    oml_l = oml[:, bass.ds(l, 1), :]
                    for h in range(HG):
                        dve.tensor_scalar(f1[:, h, :], f1[:, h, :], oml_l[:, 0, h:h + 1], lbl[:, 0, h:h + 1], ALU.mult, ALU.add).then_inc(aff_done, 1)
                        dve.tensor_scalar(k[:, h, :], k[:, h, :], oml_l[:, 0, h:h + 1], None, ALU.mult).then_inc(aff_done, 1)
                    dve.wait_ge(aff_done, 8)
                    dve.tensor_scalar(f1[:, :, :], f1[:, :, :], 2.0 ** -64, None, ALU.max).then_inc(aff_done, 1)
                    dve.wait_ge(ln_done, 1)
                    dve.wait_ge(set_done, 5)
                    for h in range(HG):
                        dve.tensor_tensor_scan(bc[:, h, :], keep[:, :], f1[:, h, :], 0.0, ALU.mult, ALU.add).then_inc(b_done, 1)
                    dve.wait_ge(b_done, HG)
                    dve.wait_ge(mask_in, 16)

                    def differences(n):
                        size, hd, bd, td = halves(n)
                        d = dd[n % 2]
                        last = strided(bc[:, 0, size - 1:], hd, bd, [0, size])
                        if n >= 2:
                            dve.wait_ge(g_done, 2 * n - 2)
                        dve.tensor_tensor(strided(d, hd, bd, td), last, strided(bc[:, :, :], hd, bd, td), ALU.subtract).then_inc(d_done, 1)
                        dve.tensor_tensor(strided(d[:, 0, size:], hd, bd, td), strided(bc[:, 0, size:], hd, bd, td), last, ALU.subtract).then_inc(d_done, 1)

                    def operands(n):
                        size, hd, bd, td = halves(n)
                        d, out = dd[n % 2], gg[n % 2]
                        dve.wait_ge(e_done, n + 1)
                        if n >= 2:
                            dve.wait_ge(a_done, before(n - 1))
                        dve.tensor_tensor(strided(out, hd, bd, td), strided(d, hd, bd, td), strided(k, hd, bd, td), ALU.mult).then_inc(g_done, 1)
                        dve.wait_ge(sig_done, 4)
                        dve.tensor_tensor(strided(out[:, 0, size:], hd, bd, td), strided(d[:, 0, size:], hd, bd, td),
                                          strided(q[:, 0, size:], hd, bd, td), ALU.mult).then_inc(g_done, 1)

                    def select(n):
                        for t in range(tiles(n)):
                            t0, r = TOKT[t]
                            dve.wait_ge(a_done, before(n, t) + 1)
                            dst = at[:, t, :, :] if t < 4 else ats[:, :, :]
                            dve.copy_predicated(dst, strided(level[0:r, n, :].bitcast(U32), [0, HG], [1, r]),
                                                bank[t][0:r, 0, 0:HG * r].rearrange("p (h t) -> p h t", h=HG)).then_inc(cp_done, 1)

                    differences(0)
                    for n in range(NL):
                        if n + 1 < NL:
                            differences(n + 1)
                        operands(n)
                        if n >= 1:
                            select(n - 1)
                    select(NL - 1)
                    dve.wait_ge(g_done, 2 * NL)
                    for t0, n, c in ((0, SEQ // P, P), (SEQ, NB, NI)):
                        hd, bd, td = [T, HG], [c, n], [1, c]
                        dve.tensor_tensor(strided(pj[:, 0, t0:], hd, bd, td), strided(bc[:, 0, t0 + c - 1:], hd, bd, [0, c]),
                                          strided(bc[:, 0, t0:], hd, bd, td), ALU.subtract).then_inc(d_done, 1)
                    select(NL)
                    dve.wait_ge(e_done, NL + 1)
                    dve.tensor_tensor(g1[:, :, :], q, f1[:, :, :], ALU.mult).then_inc(qe_done, 1)
                    dve.wait_ge(e_done, NL + 2)
                    dve.tensor_tensor(pj[:, 4:8, :], k, pj[:, 0:4, :], ALU.mult).then_inc(qe_done, 1)
                    dve.wait_ge(qe_done, 2)
                    for t in range(5):
                        r = TOKT[t][1]
                        dve.wait_ge(kt_done, t + 1)
                        dve.tensor_copy(kn[t], bank[2 + t % 2][0:r, 0, :]).then_inc(ke_done, 1)
                    for t in range(4):
                        dve.wait_ge(st_done, t + 1)
                        dve.wait_ge(po_done, t + 1)
                        for h in range(HG):
                            new = bank[2 + t % 2][:, 0, h * P:(h + 1) * P]
                            if t == 0:
                                dve.tensor_copy(state[:, h, :], new).then_inc(su_done, 1)
                            else:
                                dve.scalar_tensor_tensor(state[:, h, :], state[:, h, :], f1[:, h, t * P + P - 1:t * P + P], new,
                                                         ALU.mult, ALU.add).then_inc(su_done, 1)
                    dve.wait_ge(sin, 32)
                    dve.wait_ge(po_done, 5)
                    dve.wait_ge(ke_done, 5)

                    def own_rows(b):
                        if b >= 2:
                            dve.wait_ge(sp_done, b - 1)
                        dve.tensor_scalar(kd[b % 2], kn[4], own[:, b:b + 1], None, ALU.mult).then_inc(kd_done, 1)

                    own_rows(0)
                    for b in range(NB):
                        if b + 1 < NB:
                            own_rows(b + 1)
                        decay = strided(f1[:, 0, SEQ + NI * b + NI - 1:], [T, HG], [0, P])
                        dve.tensor_tensor(ss[:, b, :, :], ss[:, b, :, :], decay, ALU.mult).then_inc(ss_done, 1)
                        dve.wait_ge(ss_done, 2 * b + 1)
                        dve.wait_ge(sp_done, b + 1)
                        dve.tensor_tensor(ss[:, b, :, :], ss[:, b, :, :], bank[5 + b % 2][:, 0, :].rearrange("p (h v) -> p h v", h=HG),
                                          ALU.add).then_inc(ss_done, 1)
                    dve.wait_ge(r_done, 5)
                    dve.reciprocal(rt, rt).then_inc(f_done, 1)
                    dve.wait_ge(f_done, 1)
                    dve.tensor_tensor(ob[:, :, :], ob[:, :, :], rt, ALU.mult).then_inc(mul_done, 1)
                    dve.wait_ge(mul_done, 1)
                    dve.scalar_tensor_tensor(ob[:, :, :], ob[:, :, :], vecs[:, bass.ds(72 + l, 1)], g, ALU.mult, ALU.mult).then_inc(hv_done, 1)

                @block.tensor
                def _(pe):
                    for t in range(5):
                        t0, r = TOKT[t]
                        if t >= 2:
                            pe.wait_ge(ie_done, t - 1)
                        for h in range(HG):
                            mm = pe.transpose(bank[5 + t % 2][0:r, 0, h * P:(h + 1) * P], pj[:, HI0 + h, t0:t0 + r], ident[:, :])
                        mm.then_inc(tr_done, 1)
                    for n in range(NL + 1):
                        if n < NL:
                            pe.wait_ge(g_done, 2 * n + 2)
                            ks, qs = gg[n % 2], gg[n % 2]
                        else:
                            ks, qs = k, q
                        for t in range(tiles(n)):
                            t0, r = TOKT[t]
                            if n >= 1 and t < tiles(n - 1):
                                pe.wait_ge(cp_done, before(n - 1, t) + 1)
                            for h in range(HG):
                                mm = pe.matmul(bank[t][0:r, 0, h * r:(h + 1) * r], ks[:, h, t0:t0 + r], qs[:, h, t0:t0 + r],
                                               start=True, stop=True)
                            mm.then_inc(a_done, 1)
                    pe.wait_ge(qe_done, 2)
                    pe.wait_ge(cp_done, before(NL + 1))
                    for t in range(5):
                        t0, r = TOKT[t]
                        if t >= 2:
                            pe.wait_ge(ke_done, t - 1)
                        for h in range(HG):
                            mm = pe.transpose(bank[2 + t % 2][0:r, 0, h * P:(h + 1) * P], pj[:, 4 + h, t0:t0 + r], ident[:, :])
                        mm.then_inc(kt_done, 1)
                    pe.wait_ge(ie_done, 5)
                    pe.wait_ge(ke_done, 5)
                    pe.wait_ge(sin, 32)
                    for t in range(5):
                        t0, r = TOKT[t]
                        if t >= 2:
                            pe.wait_ge(oe_done, t - 1)
                        if 1 <= t < 4:
                            pe.wait_ge(su_done, 4 * t)
                        for h in range(HG):
                            out = bank[t % 2][:, 0, h * r:(h + 1) * r]
                            if 1 <= t < 4:
                                pe.matmul(out, state[:, h, :], g1[:, h, t0:t0 + r], start=True, stop=False)
                            w = at[:, t, h, :] if t < 4 else ats[:, h, :]
                            mm = pe.matmul(out, rows[0:r, t, h * P:(h + 1) * P], w, start=(t in (0, 4)), stop=(t < 4))
                            if t == 4:
                                for b in range(NB):
                                    mm = pe.matmul(out[:, NI * b:NI * b + NI], ss[:, b, h, :], g1[:, h, SEQ + NI * b:SEQ + NI * b + NI],
                                                   start=False, stop=(b == NB - 1))
                        mm.then_inc(po_done, 1)
                        if t < 4:
                            if t >= 2:
                                pe.wait_ge(su_done, 4 * (t - 1))
                            for h in range(HG):
                                mm = pe.matmul(bank[2 + t % 2][:, 0, h * P:(h + 1) * P], kn[t][:, h * P:(h + 1) * P],
                                               rows[:, t, h * P:(h + 1) * P], start=True, stop=True)
                            mm.then_inc(st_done, 1)
                    for b in range(NB):
                        pe.wait_ge(kd_done, b + 1)
                        if b >= 2:
                            pe.wait_ge(ss_done, 2 * b - 2)
                        for h in range(HG):
                            mm = pe.matmul(bank[5 + b % 2][:, 0, h * P:(h + 1) * P], kd[b % 2][:, h * P:(h + 1) * P],
                                           rows[0:NSMP, 4, h * P:(h + 1) * P], start=True, stop=True)
                        mm.then_inc(sp_done, 1)
                    pe.wait_ge(sq_done, 1)
                    pe.wait_ge(ss_done, 2 * NB)
                    gf = g1[:, :, :].rearrange("p h t -> p (h t)")
                    for c in range(5):
                        w = min(512, W - 512 * c)
                        pe.matmul(bank[(0, 1, 5, 6, 7)[c]][:, 0, 0:w], ones[:, :], gf[:, 512 * c:512 * c + w], start=True, stop=True).then_inc(n_done, 1)

        def merge_stage(l, nhi, nlo, oa, ob):
            names = Weights.NAMES + ("oh_done", "ol_done", "sg_done", "ta_done", "m_done", "mh_done", "ml_done", "x_done", "res_done")
            with stage(nc, *names) as sems, ExitStack() as st:
                oh_done, ol_done, sg_done, ta_done, m_done, mh_done, ml_done, x_done, res_done = sems[5:]
                wt = Weights(nc, st, sems[0:5], DC)
                ohi, olo, mhi, mlo = (sb(n, [P, DC, T], F32R, at=st) for n in ("ohi", "olo", "mhi", "mlo"))
                sg = sb("sg", [P, 2, T], at=st)
                tt = sb("tt", [P, 2, T], at=st)
                m32 = sb("m32", [P, T], at=st)
                rt = sb("rt", [P, 2, NSMP], at=st)
                pma, pmb, ppa, ppb = (ps(n, 2, st) for n in ("pma", "pmb", "ppa", "ppb"))
                block = st.enter_context(nc.Block())
                two = lambda v: v.rearrange("p (h t) -> p h t", h=2)
                UO = 3 * DC // 2

                @block.sync
                def _(sp):
                    w = a["w_in"][l]
                    with sp.Fori(0, DC // 2) as m:
                        for q in range(2):
                            for kind in range(3):
                                tile = 3 * q + kind
                                u, slot = 3 * m + tile // 2, tile % 2
                                if kind < 2:
                                    col = bass.ds(m * 256 + (q * P + (C_MA, C_MB)[kind]), P)
                                    wt.load(sp, u, slot, wt.columns(slot, DC, w[:, col]))
                                else:
                                    col = bass.ds(m * 256 + q * P, P)
                                    nsa = a["w_branch_nsa"][l].rearrange("(g r d) n -> g d r n", g=GROUPS, r=R)
                                    raw = wt.raw[slot]
                                    wt.load(sp, u, slot, [(raw[g * DH:(g + 1) * DH, 0:R, :], nsa[g][:, :, col]) for g in range(GROUPS)]
                                            + [(raw[:, 4:8, :], a["w_branch_hgrn"][l].rearrange("(k p) n -> p k n", p=P)[:, :, col])])
                    with sp.Fori(0, DC // 2) as c:
                        for slot in range(2):
                            wt.load(sp, c + UO, slot, wt.columns(slot, DC, a["w_out"][l][:, bass.ds(c * 256 + slot * P, P)]))

                @block.scalar
                def _(act):
                    for slot in range(2):
                        wt.split_hi(act, 0, slot, DC)
                    for c, v in ((0, oa), (4, ob)):
                        act.activation(ohi[:, c:c + 4, :], v[:, :, :], ACT.Copy).then_inc(oh_done, 1)
                    with act.Fori(0, DC // 2) as m:
                        for q in range(2):
                            for kind in range(3):
                                tile = 3 * q + kind
                                wt.split_hi(act, 3 * m + tile // 2 + 1, tile % 2, DC)
                                if kind < 2:
                                    act.wait_ge(ta_done, 4 * m + (2 * q + kind + 1))
                                    act.activation(two(sg[:, kind, :]), (pma, pmb)[kind][:, :, 0:HALF], ACT.Sigmoid).then_inc(sg_done, 1)
                            act.wait_ge(m_done, 2 * m + (q + 1))
                            act.activation(mhi[:, bass.ds(2 * m + q, 1), :], m32[:, :].unsqueeze(1), ACT.Copy).then_inc(mh_done, 1)
                    with act.Fori(1, DC // 2) as c:
                        for slot in range(2):
                            wt.split_hi(act, c + UO, slot, DC)

                @block.vector
                def _(dve):
                    dve.sem_inc(sg_done, 2)
                    dve.sem_inc(ta_done, 2)
                    dve.sem_inc(res_done, 2)
                    wt.credit_vector(dve)
                    for slot in range(2):
                        wt.split_lo(dve, 0, slot, DC)
                    for n, (c, v) in enumerate(((0, oa), (4, ob))):
                        dve.wait_ge(oh_done, n + 1)
                        dve.tensor_tensor(olo[:, c:c + 4, :], v[:, :, :], ohi[:, c:c + 4, :].bitcast(F32), ALU.subtract).then_inc(ol_done, 1)
                    with dve.Fori(0, DC // 2) as m:
                        for q in range(2):
                            for kind in range(3):
                                tile = 3 * q + kind
                                wt.split_lo(dve, 3 * m + tile // 2 + 1, tile % 2, DC)
                            dve.wait_ge(sg_done, 4 * m + (2 * q + 4))
                            dve.wait_ge(wt.mm_done, 6 * m + (3 * q + 5))
                            for kind in range(2):
                                dve.tensor_tensor(two(tt[:, kind, :]), two(sg[:, kind, :]), (ppa, ppb)[kind][:, :, 0:HALF],
                                                  ALU.mult).then_inc(ta_done, 1)
                            dve.wait_ge(ta_done, 4 * m + (2 * q + 4))
                            dve.tensor_tensor(m32[:, :], tt[:, 0, :], tt[:, 1, :], ALU.add).then_inc(m_done, 1)
                            dve.wait_ge(mh_done, 2 * m + (q + 1))
                            dve.tensor_tensor(mlo[:, bass.ds(2 * m + q, 1), :], m32[:, :].unsqueeze(1),
                                              mhi[:, bass.ds(2 * m + q, 1), :].bitcast(F32), ALU.subtract).then_inc(ml_done, 1)

                    def chunks(c, last):
                        for slot in range(2):
                            if not last:
                                wt.split_lo(dve, c + (UO + 1), slot, DC)
                            dve.wait_ge(wt.mm_done, 2 * (c + UO) + (slot + 3))
                            residual(dve, (pma, pmb)[slot], 2 * c + slot, 5, rt[:, slot, :], x_done, res_done, 2 * c + (slot + 1))
                    peeled(dve, DC // 2, 1, chunks)

                @block.tensor
                def _(pe):
                    wt.credit_tensor(pe)
                    with pe.Fori(0, DC // 2) as m:
                        for q in range(2):
                            for kind in range(3):
                                tile = 3 * q + kind
                                u, slot = 3 * m + tile // 2, tile % 2
                                if kind == 0:
                                    pe.wait_ge(sg_done, 4 * m + (2 * q + 2))
                                if kind < 2:
                                    wt.product(pe, u, slot, (pma, pmb)[kind], nhi, nlo, DC)
                                else:
                                    pe.wait_ge(ol_done, 2)
                                    pe.wait_ge(ta_done, 4 * m + (2 * q + 2))
                                    wt.product(pe, u, slot, ppa, ohi, olo, R, last=False)
                                    wt.product(pe, u, slot, ppb, ohi[:, 4:8, :], olo[:, 4:8, :], HG, k0=4)
                    pe.wait_ge(ml_done, DC)
                    with pe.Fori(0, DC // 2) as c:
                        for slot in range(2):
                            pe.wait_ge(res_done, 2 * c + (slot + 1))
                            wt.product(pe, c + UO, slot, (pma, pmb)[slot], mhi, mlo, DC)

        def mixer(l):
            with ExitStack() as outer:
                nhi, nlo = (sb(n, [P, DC, T], F32R, at=outer) for n in ("nhi", "nlo"))
                oa = sb("oa", [P, R, T], at=outer)
                ob = sb("ob", [P, HG, T], at=outer)
                with ExitStack() as inner:
                    pj = sb("pj", [P, NPC, T], at=inner)
                    proj_stage(l, nhi, nlo, pj)
                    with ExitStack() as nsa:
                        kvn = sb("kvn", [P, 5, NKV * P], at=nsa)
                        gn = sb("gn", [P, 4, 24], at=nsa)
                        kct = sb("kct", [P, NSEQ * NCMP], at=nsa)
                        vcn = sb("vcn", [NCMP, NSEQ, P], at=nsa)
                        rows_stage(l, pj, kvn, gn)
                        compress_stage(l, pj, kct, vcn)
                        attention_stage(l, pj, kvn, gn, kct, vcn, oa)
                        sample_stage(l, pj, kvn, kct, vcn, oa)
                    hgrn_stage(l, pj, ob)
                merge_stage(l, nhi, nlo, oa, ob)
        with nc.Fori(0, DEPTH) as l:
            ada_stage(l)
            ffn_stage(l, 0, 0)
            mixer(l)
            ffn_stage(l, 1, 2)
        final_stage()


_INS = ["x_prompt", "x_sample", "cache_nsa_kv", "state_win_kv", "state_hgrn", "page_table", "c_prompt", "c_sample",
        "norm_g", "ada_w", "ada_b", "ffn_w_in", "ffn_w_out", "w_in", "cmp_w1", "cmp_b1", "cmp_w2", "cmp_b2",
        "rel_table", "hgrn_lb_logits", "hgrn_norm_g", "w_branch_nsa", "w_branch_hgrn", "w_out", "final_g"]
_OUTS = {
    "y_p": (1, SEQ, D), "y_s": (NB, NI, D), "kv_p": (DEPTH, 1, SEQ, 4, GROUPS, DH), "kv_s": (DEPTH, NB, NI, 4, GROUPS, DH),
    "win_p": (DEPTH, 1, SEQ, 2, GROUPS, DH), "win_s": (DEPTH, NB, PAST, 2, GROUPS, DH), "hg_p": (DEPTH, 1, HG, P, P),
    "hg_s": (DEPTH, NB, HG, P, P),
}


def kernel(**inputs):
    import concourse.bacc as bacc
    from concourse.bass_utils import run_bass_kernel_spmd

    nc = bacc.Bacc("TRN2", target_bir_lowering=False, num_devices=1)
    arrays = {f"in_{n}": np.ascontiguousarray(inputs[n]) for n in _INS}
    arrays.update({f"in_{n}": np.ascontiguousarray(v) for n, v in shape_constants().items()})
    a = {n[3:]: nc.dram_tensor(n, v.shape, mybir.dt.from_np(v.dtype), kind="ExternalInput").ap()
         for n, v in arrays.items()}
    o = {n: nc.dram_tensor(f"out_{n}", shape, F32, kind="ExternalOutput").ap() for n, shape in _OUTS.items()}
    trunk(nc, a, o)
    r = run_bass_kernel_spmd(nc, [arrays], core_ids=[0])
    return tuple(r.results[0][f"out_{n}"] for n in _OUTS)
```

```python
from contextlib import ExitStack, contextmanager
import math

import numpy as np
import concourse.bass as bass
from concourse import mybir

F32, F32R, I32, U32 = mybir.dt.float32, mybir.dt.float32r, mybir.dt.int32, mybir.dt.uint32
ALU, ACT = mybir.AluOpType, mybir.ActivationFunctionType

P = 128
D, DEPTH, D_FF = 1024, 2, 2816
SEQ, NB, NI, PAST, PAGE = 512, 8, 4, 512, 128
NSMP = NB * NI
T = SEQ + NSMP
HALF = T // 2
DC = D // P
NSEQ = 1 + NB
HEADS, GROUPS, R, DH = 8, 2, 4, 64
HG = 4
NKV = 6
CMP_STRIDE = 16
NPAGE = PAST // PAGE
NCMP = (PAST - 32) // 16 + 1
NSUB = NCMP + 1
BUCKETS, MAXDIST = 32, 128
EPS = 1e-6
NEG = -1e30
FLOOR = -1e29
FFN_PARTS = (12, 10)
KMAX = max(FFN_PARTS)
PIECES = 3
TOKT = [(t * P, P) for t in range(SEQ // P)] + [(SEQ, NSMP)]
LEVELS = [64, 32, 16, 8, 4, 2, 1, 0]
Q0, KV0, HQ0, HF0, HI0, HO0, GATE0 = 0, 4, 10, 14, 18, 22, 26
NPC = 27
NPOOL = NB * PAST // PAGE * 5 // 4
C_KV, C_GATE = 512, 1280
C_HG = C_GATE + 3 * HEADS
C_MA = C_HG + 4 * 512
C_MB = C_MA + D


def bucket(dist):
    exact = BUCKETS // 2
    if dist < exact:
        return dist
    return min(exact + int(math.log(dist / exact) / math.log(MAXDIST / exact) * exact), BUCKETS - 1)


def shape_constants():
    rev = np.zeros((BUCKETS + 1, 640), np.float32)
    for m in range(640):
        dist = 511 - m
        if dist >= 0:
            rev[bucket(dist), m] = 1.0
        else:
            rev[BUCKETS, m] = NEG
    old = np.zeros((BUCKETS + 1, 2, NI, PAST), np.float32)
    for i in range(NI):
        for c in range(PAST):
            tok = 4 * (c % P) + c // P
            old[bucket(PAST + i - tok), :, i, c] = 1.0
            if tok <= i:
                old[BUCKETS, 1, i, c] = NEG
    cmp = np.zeros((BUCKETS + 1, NI, NCMP), np.float32)
    for i in range(NI):
        for n in range(NCMP):
            cmp[bucket(PAST + i - 16 * n - 31), i, n] = 1.0
    new = np.zeros((BUCKETS + 1, 4, NI, 2, NSMP), np.float32)
    for j in range(4):
        for i in range(NI):
            for half in range(2):
                for key in range(NSMP):
                    b, k = key // NI, key % NI
                    if b == 4 * half + j and k <= i:
                        new[bucket(i - k), j, i, half, key] = 1.0
                    else:
                        new[BUCKETS, j, i, half, key] = NEG
    level = np.zeros((P, len(LEVELS), P), np.float32)
    for n, size in enumerate(LEVELS):
        for s in range(P):
            for t in range(P):
                if size == 0:
                    level[s, n, t] = s == t
                else:
                    level[s, n, t] = s // (2 * size) == t // (2 * size) and s % (2 * size) < size <= t % (2 * size)
    own = np.zeros((NSMP, NB), np.float32)
    for t in range(NSMP):
        own[t, t // NI] = 1.0
    return {
        "c_rev": rev, "c_old": old.reshape(BUCKETS + 1, -1), "c_cmp": cmp.reshape(BUCKETS + 1, -1),
        "c_new": new.reshape(BUCKETS + 1, -1), "c_level": level, "c_own": own, "c_ident": np.eye(P, dtype=np.float32),
    }


def strided(ap, *dims):
    return bass.AP(ap.tensor, ap.offset, [list(ap.ap[0])] + [list(d) for d in dims])


@contextmanager
def stage(nc, *names):
    with ExitStack() as ctx:
        sems = [ctx.enter_context(nc.semaphore(f"{n}_{nc.next_id()}")) for n in names]
        yield sems
        for s in sems:
            nc.sync.sem_clear(s)
        nc.all_engine_barrier(sem_only=True)


class Weights:

    NAMES = ("raw_full0", "raw_full1", "hi_done", "lo_done", "mm_done")

    def __init__(self, nc, ctx, sems, k):
        self.raw_full, (self.hi_done, self.lo_done, self.mm_done) = sems[0:2], sems[2:5]
        sb = lambda n, dt: ctx.enter_context(nc.sbuf_tensor(f"{n}_{nc.next_id()}", [P, k, P], dt))
        self.raw = [sb("w_raw", F32) for _ in range(2)]
        self.hi = [sb("w_hi", F32R) for _ in range(2)]
        self.lo = [sb("w_lo", F32R) for _ in range(2)]

    def credit_vector(self, dve):
        dve.sem_inc(self.lo_done, 2)

    def credit_tensor(self, pe):
        pe.sem_inc(self.mm_done, 2)

    def load(self, sp, u, slot, pieces):
        assert len(pieces) == PIECES
        sp.wait_ge(self.lo_done, 2 * u + slot + 1)
        for dst, src in pieces:
            sp.dma_start(dst, src).then_inc(self.raw_full[slot], 16)

    def columns(self, slot, k, src):
        v = src.rearrange("(k p) n -> p k n", p=P)
        cut = [0, (k + 2) // 3, (2 * k + 2) // 3, k]
        return [(self.raw[slot][:, a:b, :], v[:, a:b, :]) for a, b in zip(cut, cut[1:])]

    def split_hi(self, act, u, slot, k):
        act.wait_ge(self.raw_full[slot], 16 * PIECES * (u + 1))
        act.wait_ge(self.mm_done, 2 * u + slot + 1)
        act.activation(self.hi[slot][:, 0:k, :], self.raw[slot][:, 0:k, :], ACT.Copy).then_inc(self.hi_done, 1)

    def split_lo(self, dve, u, slot, k):
        dve.wait_ge(self.hi_done, 2 * u + slot + 1)
        dve.tensor_tensor(self.lo[slot][:, 0:k, :], self.raw[slot][:, 0:k, :],
                          self.hi[slot][:, 0:k, :].bitcast(F32), ALU.subtract).then_inc(self.lo_done, 1)

    def product(self, pe, u, slot, out, hi, lo, ks, k0=0, last=True, landed=None, count=0):
        pe.wait_ge(self.lo_done, 2 * u + slot + 3)
        for n in range(ks):
            if landed is not None and n >= ks - 2:
                pe.wait_ge(landed, count - ks + n + 1)
            for w, x, end in ((self.hi, hi, 0), (self.hi, lo, 0), (self.lo, hi, 1)):
                for half in range(2):
                    mm = pe.matmul(out[:, half, 0:HALF], w[slot][:, k0 + n, :], x[:, n, half * HALF:(half + 1) * HALF],
                                   start=(n == 0 and w is self.hi and x is hi), stop=(n == ks - 1 and end == 1))
        if last:
            mm.then_inc(self.mm_done, 1)
        return mm


    def first_products(self, pe, outs, hi, lo, ks, landed):
        pe.wait_ge(self.lo_done, 4)
        for n in range(ks):
            pe.wait_ge(landed, n + 1)
            for slot in range(2):
                for w, x, end in ((self.hi, hi, 0), (self.hi, lo, 0), (self.lo, hi, 1)):
                    for half in range(2):
                        mm = pe.matmul(outs[slot][:, half, 0:HALF], w[slot][:, n, :], x[:, n, half * HALF:(half + 1) * HALF],
                                       start=(n == 0 and w is self.hi and x is hi), stop=(n == ks - 1 and end == 1))
                if n == ks - 1:
                    mm.then_inc(self.mm_done, 1)


def norm_vector(dve, s, x, tmp, nf, rs, mods, w, nhi, nlo):
    dve.wait_ge(s.sd_done, 1)
    dve.reciprocal(rs[:, :], rs[:, :]).then_inc(s.rs_done, 1)
    dve.wait_ge(s.rs_done, 1)

    def lo(c):
        dve.wait_ge(s.nh_done, c + 1)
        dve.tensor_tensor(nlo[:, c, :], nf[:, c % 3, :], nhi[:, c, :].bitcast(F32), ALU.subtract).then_inc(s.nl_done, 1)

    for c in range(DC):
        if c >= 2:
            dve.wait_ge(s.af_done, c - 1)
        dve.tensor_tensor(tmp[:, c % 2, :], x[:, c, :], rs[:, :], ALU.mult).then_inc(s.xr_done, 1)
        if c >= 2:
            lo(c - 2)
        dve.wait_ge(s.xr_done, c + 1)
        smp = tmp[:, c % 2, SEQ:T]
        dve.tensor_tensor(strided(smp, [NI, NB], [1, NI]), strided(smp, [NI, NB], [1, NI]),
                          strided(mods[:, 3 * w + 1, c, 1:NSEQ], [1, NB], [0, NI]), ALU.mult).then_inc(s.sm_done, 1)
        dve.wait_ge(s.sm_done, c + 1)
        if c >= 3:
            dve.wait_ge(s.nl_done, c - 2)
        dve.tensor_tensor(strided(nf[:, c % 3, SEQ:T], [NI, NB], [1, NI]), strided(smp, [NI, NB], [1, NI]),
                          strided(mods[:, 3 * w, c, 1:NSEQ], [1, NB], [0, NI]), ALU.add).then_inc(s.sa_done, 1)
    lo(DC - 2)
    lo(DC - 1)


def norm_scalar(act, s, wt, x, sq, st, eps, tmp, nf, rs, mods, w, nhi):
    for c in range(DC):
        if c >= 2:
            act.wait_ge(s.st_done, c - 1)
        act.activation(sq[:, c % 2, :], x[:, c, :], ACT.Square).then_inc(s.sq_done, 1)
    for slot in range(2):
        wt.split_hi(act, 0, slot, DC)
    act.wait_ge(s.st_done, DC)
    act.activation(strided(rs[:, :], [HALF, 2], [1, HALF]), st[:, :, 0:HALF], ACT.Sqrt, bias=eps[:, 0:1],
                   scale=1.0 / D).then_inc(s.sd_done, 1)

    def hi(c):
        act.wait_ge(s.af_done, c + 1)
        act.wait_ge(s.sa_done, c + 1)
        act.activation(nhi[:, c, :], nf[:, c % 3, :], ACT.Copy).then_inc(s.nh_done, 1)

    for c in range(DC):
        act.wait_ge(s.xr_done, c + 1)
        if c >= 3:
            act.wait_ge(s.nl_done, c - 2)
        act.activation(nf[:, c % 3, 0:SEQ], tmp[:, c % 2, 0:SEQ], ACT.Identity, bias=mods[:, 3 * w, c, 0:1],
                       scale=mods[:, 3 * w + 1, c, 0:1]).then_inc(s.af_done, 1)
        if c >= 1:
            hi(c - 1)
    hi(DC - 1)


def norm_tensor(pe, s, sq, st, ones):
    for c in range(DC):
        pe.wait_ge(s.sq_done, c + 1)
        for half in range(2):
            mm = pe.matmul(st[:, half, 0:HALF], ones[:, :], sq[:, c % 2, half * HALF:(half + 1) * HALF],
                           start=(c == 0), stop=(c == DC - 1))
        mm.then_inc(s.st_done, 1)


class NormSems:
    NAMES = ("sq_done", "st_done", "sd_done", "rs_done", "xr_done", "sm_done", "sa_done", "af_done", "nh_done",
             "nl_done")

    def __init__(self, sems):
        (self.sq_done, self.st_done, self.sd_done, self.rs_done, self.xr_done, self.sm_done, self.sa_done,
         self.af_done, self.nh_done, self.nl_done) = sems


def peeled(engine, n, step, body):
    if n > step:
        with engine.Fori(0, n - step, step) as i:
            body(i, False)
    body(n - step, True)


def trunk(nc, a, o):
    ctx = ExitStack()
    with ctx:
        def sb(name, shape, dt=F32, at=ctx):
            return at.enter_context(nc.sbuf_tensor(f"{name}_{nc.next_id()}", shape, dt))

        def ps(name, banks, at):
            return at.enter_context(nc.psum_tensor(f"{name}_{nc.next_id()}", [P, banks, 512], F32))

        rv_dram = nc.dram_tensor("rel_rev", (HEADS, P, 640), F32, kind="Internal").ap()
        gate_dram = nc.dram_tensor("gate_rows", (NB, 3 * HEADS, NI), F32, kind="Internal").ap()

        n_dram = nc.dram_tensor("n_parts", (2, P, DC * T), F32, kind="Internal").ap()

        x = sb("x", [P, DC, T])
        mods = sb("mods", [P, 9, DC, NSEQ])
        cT = sb("cT", [P, DC, NSEQ])
        ident = sb("ident", [P, P])
        ones = sb("ones", [P, P])
        eps = sb("eps", [P, 1])
        vecs = sb("vecs", [P, 74])
        adab = sb("adab", [P, DEPTH, 72])
        lb = sb("lb", [P, DEPTH, HG])
        oml = sb("oml", [P, DEPTH, HG])
        own = sb("own", [NSMP, NB])
        b2row = sb("b2row", [32, DEPTH, DH])
        bias_old = sb("bias_old", [P, 2, PAST])
        bias_cmp = sb("bias_cmp", [P, NCMP])
        bias_new = sb("bias_new", [P, 2, NSMP])
        pages = sb("pages", [1, NB * PAST // PAGE], I32)

        with stage(nc, "loaded", "set_done", "dve_done", "tr_done", "ev_done", "sil_done", "la_done",
                                      "rev_done", "rev_ev", "rev_out", "bi_done", "bi_ev", "lb_done", "lbe_done") as (
                loaded, set_done, dve_done, tr_done, ev_done, sil_done, la_done, rev_done, rev_ev, rev_out, bi_done,
                bi_ev, lb_done, lbe_done), ExitStack() as st:
            xn = sb("xn", [P, 4, D], at=st)
            xs = sb("xs", [NSMP, D], at=st)
            cn = sb("cn", [NSEQ, D], at=st)
            vn = sb("vn", [74, P], at=st)
            an = sb("an", [72, DEPTH, P], at=st)
            rev = sb("rev", [33, 640], at=st)
            old = sb("old", [33, 2, NI, PAST], at=st)
            cmpc = sb("cmpc", [33, NI, NCMP], at=st)
            newc = sb("newc", [33, 16, 2 * NSMP], at=st)
            table = sb("table", [33, HEADS], at=st)
            la = sb("la", [33, NI, P], at=st)
            lj = sb("lj", [33, 16, P], at=st)
            revs = sb("revs", [HEADS, 640], at=st)
            sm = sb("sm", [P, 6, HG], at=st)
            pt = [ps(f"pt{i}", 1, st) for i in range(2)]
            pr = ps("pr", 2, st)
            pb = ps("pb", 4, st)
            block = st.enter_context(nc.Block())
            n_loads = 20
            jobs = []
            for c in range(DC):
                jobs.append(("x", c))
            for c in range(DC):
                jobs.append(("xs", c))
            jobs += [("c", 0), ("v", 0), ("a", 0)]

            @block.sync
            def _(sp):
                sp.wait_ge(set_done, 1)
                loads = [
                    (xn[:, :, :], a["x_prompt"][0].rearrange("(t p) d -> p t d", p=P)),
                    (xs[:, :], a["x_sample"].rearrange("b i d -> (b i) d")),
                    (cn[0:1, :], a["c_prompt"]), (cn[1:NSEQ, :], a["c_sample"]),
                    (vn[0:48, :], a["norm_g"].rearrange("l w (c p) -> (l w c) p", p=P)),
                    (vn[48:56, :], a["final_g"].rearrange("(c p) -> c p", p=P)),
                    (vn[56:60, :], a["cmp_b1"].rearrange("l k e -> (l k) e")),
                    (vn[60:64, 0:DH], a["cmp_b2"].rearrange("l k e -> (l k) e")),
                    (vn[60:64, DH:P], a["cmp_b2"].rearrange("l k e -> (l k) e")),
                    (vn[64:72, :], a["hgrn_lb_logits"].rearrange("l (h p) -> (l h) p", p=P)),
                    (vn[72:74, :], a["hgrn_norm_g"]),
                    (an[:, :, :], a["ada_b"].rearrange("l (n p) -> n l p", p=P)),
                    (rev[:, :], a["c_rev"]), (old[:, :, :, :], a["c_old"].rearrange("b (m i k) -> b m i k", m=2, i=NI)),
                    (cmpc[:, :, :], a["c_cmp"].rearrange("b (i k) -> b i k", i=NI)),
                    (newc[:, :, :], a["c_new"].rearrange("b (i k) -> b i k", i=16)),
                    (table[0:BUCKETS, :], a["rel_table"]), (own[:, :], a["c_own"]), (ident[:, :], a["c_ident"]),
                    (pages[:, :], a["page_table"].rearrange("(o b) n -> o (b n)", o=1)),
                ]
                assert len(loads) == n_loads
                for dst, src in loads:
                    sp.dma_start(dst, src).then_inc(loaded, 16)
                for l in range(DEPTH):
                    sp.dma_start(b2row[:, l, :], a["cmp_b2"][l, 1].partition_broadcast(32)).then_inc(loaded, 16)
                sp.wait_ge(rev_ev, 2)
                sp.dma_start(rv_dram, strided(revs[:, :], [0, P], [1, 640])).then_inc(rev_out, 16)
                sp.wait_ge(rev_out, 16)
                sp.wait_ge(loaded, 16 * (n_loads + DEPTH))

            @block.vector
            def _(dve):
                dve.memset(table[:, :], 1.0).then_inc(set_done, 1)
                dve.memset(ones[:, :], 1.0)
                dve.memset(eps[:, :], EPS)
                dve.memset(la[:, :, :], 0.0).then_inc(dve_done, 1)
                dve.memset(lj[:, :, :], 0.0).then_inc(dve_done, 1)
                dve.wait_ge(dve_done, 2)
                dve.wait_ge(loaded, 16 * (n_loads + DEPTH))
                for i in range(NI):
                    dve.tensor_copy(strided(la[:, i, i:], [32, 4], [NI, HEADS]),
                                    strided(table[:, :], [0, 4], [1, HEADS])).then_inc(la_done, 1)
                    dve.tensor_copy(strided(lj[:, i, i:], [NI * P + 32, 4], [NI, HEADS]),
                                    strided(table[:, :], [0, 4], [1, HEADS])).then_inc(la_done, 1)
                for n, (kind, c) in enumerate(jobs):
                    dve.wait_ge(tr_done, n + 1)
                    src = pt[n % 2][:, 0, :]
                    if kind == "x":
                        ins = dve.tensor_copy(x[:, c, 0:SEQ], src)
                    elif kind == "xs":
                        ins = dve.tensor_copy(x[:, c, SEQ:T], src[:, 0:NSMP])
                    elif kind == "c":
                        ins = dve.tensor_copy(strided(cT[:, :, :], [1, DC * NSEQ]), src[:, 0:DC * NSEQ])
                    elif kind == "v":
                        ins = dve.tensor_copy(vecs[:, :], src[:, 0:74])
                    else:
                        ins = dve.tensor_copy(strided(adab[:, :, :], [1, 144]), src[:, 0:144])
                    ins.then_inc(ev_done, 1)
                dve.wait_ge(ev_done, len(jobs))
                lg = vecs[:, 64:72]
                dve.tensor_tensor(sm[:, 0, :], lg[:, 0:4], lg[:, 4:8], ALU.max).then_inc(lb_done, 1)
                dve.wait_ge(lb_done, 1)
                dve.tensor_tensor(sm[:, 1, :], lg[:, 0:4], sm[:, 0, :], ALU.subtract).then_inc(lb_done, 1)
                dve.tensor_tensor(sm[:, 2, :], lg[:, 4:8], sm[:, 0, :], ALU.subtract).then_inc(lb_done, 1)
                dve.wait_ge(lbe_done, 1)
                dve.tensor_tensor(sm[:, 5, :], sm[:, 3, :], sm[:, 4, :], ALU.add).then_inc(lb_done, 1)
                dve.wait_ge(lb_done, 4)
                dve.reciprocal(sm[:, 5, :], sm[:, 5, :]).then_inc(lb_done, 1)
                dve.wait_ge(lb_done, 5)
                dve.tensor_tensor(sm[:, 3, :], sm[:, 3, :], sm[:, 5, :], ALU.mult).then_inc(lb_done, 1)
                dve.tensor_tensor(sm[:, 4, :], sm[:, 4, :], sm[:, 5, :], ALU.mult).then_inc(lb_done, 1)
                dve.wait_ge(lb_done, 7)
                dve.tensor_tensor(sm[:, 4, :], sm[:, 3, :], sm[:, 4, :], ALU.add).then_inc(lb_done, 1)
                dve.tensor_tensor(lb[:, 0, :], sm[:, 3, :], sm[:, 3, :], ALU.subtract).then_inc(lb_done, 1)
                dve.wait_ge(lb_done, 8)
                dve.tensor_tensor(lb[:, 1, :], sm[:, 4, :], sm[:, 3, :], ALU.subtract).then_inc(lb_done, 1)
                dve.wait_ge(lb_done, 10)
                dve.tensor_scalar(oml[:, :, :], lb[:, :, :], -1.0, 1.0, ALU.mult, ALU.add)
                dve.wait_ge(rev_done, 1)
                for h in range(2):
                    dve.tensor_copy(revs[:, 320 * h:320 * h + 320], pr[0:HEADS, h, 0:320]).then_inc(rev_ev, 1)
                dve.wait_ge(bi_done, 1)
                dve.tensor_copy(bias_old[:, :, :], pb[:, 0:2, :])
                dve.tensor_copy(bias_cmp[:, :], pb[:, 2, 0:NCMP])
                dve.tensor_copy(strided(bias_new[:, :, :], [1, 2 * NSMP]), pb[:, 3, 0:2 * NSMP]).then_inc(bi_ev, 1)

            @block.scalar
            def _(act):
                act.wait_ge(loaded, 16 * (n_loads + DEPTH))
                act.activation(cn[:, :], cn[:, :], ACT.Silu).then_inc(sil_done, 1)
                act.wait_ge(lb_done, 3)
                act.activation(strided(sm[:, 3:5, :], [1, 8]), strided(sm[:, 1:3, :], [1, 8]), ACT.Exp).then_inc(lbe_done, 1)

            @block.tensor
            def _(pe):
                pe.wait_ge(loaded, 16 * (n_loads + DEPTH))
                pe.wait_ge(sil_done, 1)
                for n, (kind, c) in enumerate(jobs):
                    out = pt[n % 2][:, 0, :]
                    if n >= 2:
                        pe.wait_ge(ev_done, n - 1)
                    if kind == "x":
                        for t in range(4):
                            mm = pe.transpose(out[:, t * P:(t + 1) * P], xn[:, t, c * P:(c + 1) * P], ident[:, :])
                    elif kind == "xs":
                        mm = pe.transpose(out[:, 0:NSMP], xs[:, c * P:(c + 1) * P], ident[0:NSMP, 0:NSMP])
                    elif kind == "c":
                        for k in range(DC):
                            mm = pe.transpose(out[:, k * NSEQ:(k + 1) * NSEQ], cn[:, k * P:(k + 1) * P],
                                              ident[0:NSEQ, 0:NSEQ])
                    elif kind == "v":
                        mm = pe.transpose(out[:, 0:74], vn[:, :], ident[0:74, 0:74])
                    else:
                        for l in range(DEPTH):
                            mm = pe.transpose(out[:, 72 * l:72 * l + 72], an[:, l, :], ident[0:72, 0:72])
                    mm.then_inc(tr_done, 1)
                for h in range(2):
                    mm = pe.matmul(pr[0:HEADS, h, 0:320], table[:, :], rev[:, 320 * h:320 * h + 320], start=True, stop=True)
                mm.then_inc(rev_done, 1)
                pe.wait_ge(la_done, 2 * NI)
                for m in range(2):
                    for i in range(NI):
                        pe.matmul(pb[:, m, :], la[:, i, :], old[:, m, i, :], start=(i == 0), stop=(i == NI - 1))
                for i in range(NI):
                    pe.matmul(pb[:, 2, 0:NCMP], la[:, i, :], cmpc[:, i, :], start=(i == 0), stop=(i == NI - 1))
                for i in range(16):
                    mm = pe.matmul(pb[:, 3, 0:2 * NSMP], lj[:, i, :], newc[:, i, :], start=(i == 0), stop=(i == 15))
                mm.then_inc(bi_done, 1)

        def ada_stage(l):
            NP = 4
            LO = 32
            with stage(nc, "full0", "full1", "full2", "full3", "c_done", "hi_done", "lo_done", "mm_done", "md_done",
                       "tp_done", "add_done", "mod_done") as (full0, full1, full2, full3, c_done, hi_done, lo_done,
                                                              mm_done, md_done, tp_done, add_done, mod_done), ExitStack() as st:
                full = [full0, full1, full2, full3]
                raw = [sb(f"ada_raw{i}", [P, DC // 2, 512], at=st) for i in range(NP)]
                hi = [sb(f"ada_hi{i}", [P, DC // 2, 512], F32R, at=st) for i in range(NP)]
                lo = [sb(f"ada_lo{i}", [P, DC // 2, 512], F32R, at=st) for i in range(NP)]
                cp = sb("cp", [P, DC, P], at=st)
                cs = sb("cs", [P, DC, P], F32R, at=st)
                ch = sb("ch", [P, DC, NSEQ], F32R, at=st)
                sel = sb("sel", [LO + NSEQ, NSEQ], at=st)
                md = sb("md", [LO + NSEQ, 2, 512], at=st)
                pm = [ps(f"pm{i}", 1, st) for i in range(2)]
                pt = [ps(f"pt{i}", 1, st) for i in range(2)]
                block = st.enter_context(nc.Block())
                src = a["ada_w"][l].rearrange("(k p) n -> p k n", p=P)

                @block.sync
                def _(sp):
                    with sp.Fori(0, 9) as u:
                        for i in range(NP):
                            s, h = divmod(i, 2)
                            sp.wait_ge(lo_done, NP * u + i + 1)
                            sp.dma_start(raw[i][:, :, :], src[:, 4 * h:4 * h + 4, bass.ds(u * 1024 + s * 512, 512)]).then_inc(full[i], 16)

                @block.scalar
                def _(act):
                    act.activation(ch[:, :, :], cT[:, :, :], ACT.Copy).then_inc(c_done, 1)
                    act.wait_ge(c_done, 4)
                    act.activation(cs[:, :, :], cp[:, :, :], ACT.Copy).then_inc(c_done, 1)

                    def split(u, i):
                        act.wait_ge(full[i], 16 * (u + 1))
                        act.wait_ge(mm_done, NP * u + i + 1)
                        act.activation(hi[i][:, :, :], raw[i][:, :, :], ACT.Copy).then_inc(hi_done, 1)

                    def evacuate(u, s):
                        act.wait_ge(mm_done, NP * u + (2 * s + 2 + NP))
                        act.wait_ge(tp_done, 2 * u + s + 1)
                        act.activation(md[:, s, :], pm[s][0:LO + NSEQ, 0, :], ACT.Copy).then_inc(md_done, 1)

                    split(0, 0)
                    split(0, 1)
                    with act.Fori(0, 8) as u:
                        split(u, 2)
                        split(u, 3)
                        evacuate(u, 0)
                        split(u + 1, 0)
                        split(u + 1, 1)
                        evacuate(u, 1)
                    split(8, 2)
                    split(8, 3)
                    evacuate(8, 0)
                    evacuate(8, 1)

                @block.tensor
                def _(pe):
                    pe.sem_inc(mm_done, NP)
                    pe.sem_inc(tp_done, 2)
                    pe.wait_ge(c_done, 5)

                    def products(u, i):
                        s, h = divmod(i, 2)
                        pe.wait_ge(lo_done, NP * u + (i + 1 + NP))
                        if h == 0:
                            pe.wait_ge(md_done, 2 * u + s + 1)
                        for n in range(DC // 2):
                            for w in (hi, lo):
                                mm = pe.matmul(pm[s][:, 0, :], cs[:, 4 * h + n, :], w[i][:, n, :],
                                               start=(h == 0 and n == 0 and w is hi), stop=(h == 1 and n == DC // 2 - 1 and w is lo))
                        mm.then_inc(mm_done, 1)

                    def turn(u, s):
                        pe.wait_ge(md_done, 2 * u + s + 3)
                        pe.wait_ge(add_done, 2 * u + s + 1)
                        for m in range(4):
                            mm = pe.matmul(pt[s][:, 0, m * NSEQ:(m + 1) * NSEQ], md[:, s, m * P:(m + 1) * P], sel[:, :],
                                           start=True, stop=True)
                        mm.then_inc(tp_done, 1)

                    products(0, 0)
                    products(0, 1)
                    with pe.Fori(0, 8) as u:
                        products(u, 2)
                        products(u, 3)
                        turn(u, 0)
                        products(u + 1, 0)
                        products(u + 1, 1)
                        turn(u, 1)
                    products(8, 2)
                    products(8, 3)
                    turn(8, 0)
                    turn(8, 1)

                @block.vector
                def _(dve):
                    dve.sem_inc(md_done, 2)
                    dve.sem_inc(add_done, 2)
                    dve.sem_inc(lo_done, NP)
                    dve.memset(cp[:, :, :], 0.0).then_inc(c_done, 1)
                    dve.tensor_tensor(sel[:, :], ident[0:LO + NSEQ, 0:NSEQ], ident[0:LO + NSEQ, LO:LO + NSEQ], ALU.add).then_inc(c_done, 1)
                    dve.wait_ge(c_done, 3)
                    dve.tensor_copy(cp[:, :, 0:NSEQ], cT[:, :, :])
                    dve.tensor_tensor(cp[:, :, LO:LO + NSEQ], cT[:, :, :], ch[:, :, :].bitcast(F32), ALU.subtract).then_inc(c_done, 1)
                    flat = mods[:, :, :, :].rearrange("p a c s -> p (a c s)")

                    def split(u, i):
                        dve.wait_ge(hi_done, NP * u + i + 1)
                        dve.tensor_tensor(lo[i][:, :, :], raw[i][:, :, :], hi[i][:, :, :].bitcast(F32), ALU.subtract).then_inc(lo_done, 1)

                    def add_bias(u, s):
                        dve.wait_ge(tp_done, 2 * u + s + 3)
                        dve.tensor_tensor(flat[:, bass.ds(u * 72 + s * 36, 36)].rearrange("p (m s) -> p m s", m=4),
                                          pt[s][:, 0, 0:36].rearrange("p (m s) -> p m s", m=4),
                                          bias_view(adab, l, u, s), ALU.add).then_inc(add_done, 1)

                    for i in range(3):
                        split(0, i)
                    with dve.Fori(0, 8) as u:
                        split(u, 3)
                        split(u + 1, 0)
                        add_bias(u, 0)
                        split(u + 1, 1)
                        split(u + 1, 2)
                        add_bias(u, 1)
                    split(8, 3)
                    add_bias(8, 0)
                    add_bias(8, 1)
                    dve.wait_ge(add_done, 20)
                    for w3 in range(3):
                        g = vecs[:, bass.ds(l * 24 + w3 * 8, 8)]
                        sc = mods[:, 3 * w3 + 1, :, :]
                        dve.scalar_tensor_tensor(sc, sc, 1.0, strided(g, [1, DC], [0, NSEQ]), ALU.add, ALU.mult).then_inc(mod_done, 1)
                        if w3 != 1:
                            gt = mods[:, 3 * w3 + 2, :, :]
                            dve.tensor_scalar(gt, gt, 0.5, None, ALU.mult).then_inc(mod_done, 1)

        def bias_view(t, l, u, s):
            v = t[:, :, :].rearrange("p l n -> p (l n)")[:, bass.ds(l * 72 + u * 8 + s * 4, 4)]
            return strided(v, [1, 4], [0, NSEQ])

        def norm_buffers(at):
            return (sb("sq", [P, 2, T], at=at), sb("tmp", [P, 2, T], at=at), sb("nf", [P, 3, T], at=at),
                    sb("rs", [P, T], at=at))

        def residual(dve, psum, c, comp, tmp, x_done, res_done, count):
            xc = x[:, bass.ds(c, 1), :]
            mc = mods[:, comp, bass.ds(c, 1), :]
            gate = mc[:, 0, 0:1]
            w = SEQ - HALF
            dve.tensor_tensor(strided(tmp, [NI, NB], [1, NI]), strided(psum[:, 1, w:w + NSMP], [NI, NB], [1, NI]),
                              strided(mc[:, 0, 1:NSEQ], [1, NB], [0, NI]), ALU.mult).then_inc(x_done, 1)
            dve.scalar_tensor_tensor(xc[:, 0, 0:HALF], psum[:, 0, 0:HALF], gate, xc[:, 0, 0:HALF], ALU.mult, ALU.add)
            dve.scalar_tensor_tensor(xc[:, 0, HALF:SEQ], psum[:, 1, 0:w], gate, xc[:, 0, HALF:SEQ], ALU.mult, ALU.add)
            dve.wait_ge(x_done, count)
            dve.tensor_tensor(xc[:, 0, SEQ:T], xc[:, 0, SEQ:T], tmp, ALU.add).then_inc(res_done, 1)

        def ffn_stage(l, which, w3):
            names = Weights.NAMES + NormSems.NAMES + ("silu_done", "prod_done", "gh_done", "gl_done", "res_done", "x_done")
            with stage(nc, *names) as sems, ExitStack() as st:
                s = NormSems(sems[5:15])
                silu_done, prod_done, gh_done, gl_done, res_done, x_done = sems[15:]
                wt = Weights(nc, st, sems[0:5], KMAX)
                nhi, nlo = (sb(n, [P, DC, T], F32R, at=st) for n in ("nhi", "nlo"))
                ghi, glo = (sb(n, [P, KMAX, T], F32R, at=st) for n in ("ghi", "glo"))
                sq, tmp, nf, rs = norm_buffers(st)
                sa, g32 = sq, tmp
                rt = sb("rt", [P, 2, NSMP], at=st)
                pa = [ps(f"pa{i}", 2, st) for i in range(2)]
                pg = [ps(f"pg{i}", 2, st) for i in range(2)]
                block = st.enter_context(nc.Block())
                w_in = a["ffn_w_in"][l, which]
                w_out = a["ffn_w_out"][l, which]
                n0, n1 = FFN_PARTS
                parts = [(n0, 0, 0, n0, DC), (n1, n0 + DC // 2, n0, n0 + DC // 2 + n1, None)]

                @block.sync
                def _(sp):
                    for n, u0, j0, uo, _ in parts:
                        with sp.Fori(0, n) as j:
                            for slot in range(2):
                                wt.load(sp, j + u0, slot, wt.columns(slot, DC, w_in[:, bass.ds((j + j0) * P + slot * D_FF, P)]))
                        rows = w_out[j0 * P:(j0 + n) * P, :]
                        with sp.Fori(0, DC // 2) as c:
                            for slot in range(2):
                                wt.load(sp, c + uo, slot, wt.columns(slot, n, rows[:, bass.ds((2 * c + slot) * P, P)]))

                @block.scalar
                def _(act):
                    norm_scalar(act, s, wt, x, sq, pg[1], eps, tmp, nf, rs, mods, w3, nhi)
                    for n, u0, j0, uo, k_after in parts:
                        def pair(j, last):
                            for q in range(2):
                                k = n if last and q == 1 else DC
                                wt.split_hi(act, j + (u0 + q + 1), 0, k)
                                act.wait_ge(prod_done, j + (j0 + q + 1))
                                act.activation(strided(sa[:, q, :], [HALF, 2], [1, HALF]), pa[q][:, :, 0:HALF],
                                               ACT.Silu).then_inc(silu_done, 1)
                                wt.split_hi(act, j + (u0 + q + 1), 1, k)
                                act.wait_ge(prod_done, j + (j0 + q + 3))
                                act.activation(ghi[:, bass.ds(j + q, 1), :], g32[:, q, :].unsqueeze(1), ACT.Copy).then_inc(gh_done, 1)

                        def chunks(c, last):
                            for slot in range(2):
                                if not last:
                                    wt.split_hi(act, c + (uo + 1), slot, n)
                                elif k_after:
                                    wt.split_hi(act, c + (uo + 1), slot, k_after)

                        peeled(act, n, 2, pair)
                        peeled(act, DC // 2, 1, chunks)

                @block.vector
                def _(dve):
                    dve.sem_inc(prod_done, 2)
                    dve.sem_inc(res_done, 2)
                    wt.credit_vector(dve)
                    for slot in range(2):
                        wt.split_lo(dve, 0, slot, DC)
                    norm_vector(dve, s, x, tmp, nf, rs, mods, w3, nhi, nlo)
                    for c0, (n, u0, j0, uo, k_after) in enumerate(parts):
                        def pair(j, last):
                            for q in range(2):
                                k = n if last and q == 1 else DC
                                for slot in range(2):
                                    wt.split_lo(dve, j + (u0 + q + 1), slot, k)
                                dve.wait_ge(silu_done, j + (j0 + q + 1))
                                dve.wait_ge(wt.mm_done, 2 * (j + (u0 + q)) + 4)
                                dve.tensor_tensor(strided(g32[:, q, :], [HALF, 2], [1, HALF]),
                                                  strided(sa[:, q, :], [HALF, 2], [1, HALF]), pg[q][:, :, 0:HALF],
                                                  ALU.mult).then_inc(prod_done, 1)
                                dve.wait_ge(gh_done, j + (j0 + q + 1))
                                dve.tensor_tensor(glo[:, bass.ds(j + q, 1), :], g32[:, q, :].unsqueeze(1),
                                                  ghi[:, bass.ds(j + q, 1), :].bitcast(F32), ALU.subtract).then_inc(gl_done, 1)

                        def chunks(c, last):
                            for slot in range(2):
                                if not last:
                                    wt.split_lo(dve, c + (uo + 1), slot, n)
                                elif k_after:
                                    wt.split_lo(dve, c + (uo + 1), slot, k_after)
                                dve.wait_ge(wt.mm_done, 2 * (c + uo) + (slot + 3))
                                residual(dve, pa[slot], 2 * c + slot, 3 * w3 + 2, rt[:, slot, :], x_done, res_done,
                                         2 * c + (DC * c0 + slot + 1))

                        peeled(dve, n, 2, pair)
                        peeled(dve, DC // 2, 1, chunks)

                @block.tensor
                def _(pe):
                    wt.credit_tensor(pe)
                    norm_tensor(pe, s, sq, pg[1], ones)

                    def pair(j, u0, j0, q, c0):
                        pe.wait_ge(prod_done, j + (j0 + q + 1))
                        pe.wait_ge(res_done, DC * c0 + q + 1)
                        for slot in range(2):
                            wt.product(pe, j + (u0 + q), slot, (pa, pg)[slot][q], nhi, nlo, DC)

                    wt.first_products(pe, (pa[0], pg[0]), nhi, nlo, DC, s.nl_done)
                    pair(0, 0, 0, 1, 0)
                    for c0, (n, u0, j0, uo, _) in enumerate(parts):
                        with pe.Fori(2 if c0 == 0 else 0, n, 2) as j:
                            for q in range(2):
                                pair(j, u0, j0, q, c0)
                        pe.wait_ge(gl_done, j0 + n - 2)
                        pe.wait_ge(prod_done, j0 + n + 1)
                        wt.product(pe, uo, 0, pa[0], ghi, glo, n, landed=gl_done, count=j0 + n)
                        pe.wait_ge(prod_done, j0 + n + 2)
                        wt.product(pe, uo, 1, pa[1], ghi, glo, n)
                        with pe.Fori(1, DC // 2) as c:
                            for slot in range(2):
                                pe.wait_ge(res_done, 2 * c + (DC * c0 + slot + 1))
                                wt.product(pe, c + uo, slot, pa[slot], ghi, glo, n)

        def final_stage():
            with stage(nc, *NormSems.NAMES, "tr_done", "ya_done", "out_done") as sems, ExitStack() as st:
                s = NormSems(sems[0:10])
                tr_done, ya_done, out_done = sems[10:]
                sq, tmp, nf, rs = norm_buffers(st)
                y = sb("y", [P, 5, D], at=st)
                pst = ps("pst", 2, st)
                pt = [ps(f"pt{i}", 2, st) for i in range(2)]
                block = st.enter_context(nc.Block())

                @block.sync
                def _(sp):
                    sp.wait_ge(ya_done, 10)
                    sp.dma_start(o["y_p"][0].rearrange("(t p) d -> p t d", p=P), y[:, 0:4, :]).then_inc(out_done, 16)
                    sp.dma_start(o["y_s"].rearrange("b i d -> (b i) d"), y[0:NSMP, 4, :]).then_inc(out_done, 16)
                    sp.wait_ge(out_done, 32)

                @block.scalar
                def _(act):
                    for c in range(DC):
                        if c >= 2:
                            act.wait_ge(s.st_done, c - 1)
                        act.activation(sq[:, c % 2, :], x[:, c, :], ACT.Square).then_inc(s.sq_done, 1)
                    act.wait_ge(s.st_done, DC)
                    act.activation(strided(rs[:, :], [HALF, 2], [1, HALF]), pst[:, :, 0:HALF], ACT.Sqrt,
                                   bias=eps[:, 0:1], scale=1.0 / D).then_inc(s.sd_done, 1)

                @block.vector
                def _(dve):
                    dve.wait_ge(s.sd_done, 1)
                    dve.reciprocal(rs[:, :], rs[:, :]).then_inc(s.rs_done, 1)
                    dve.wait_ge(s.rs_done, 1)
                    for c in range(DC):
                        dve.scalar_tensor_tensor(x[:, c, :], x[:, c, :], vecs[:, 48 + c:49 + c], rs[:, :], ALU.mult,
                                                 ALU.mult).then_inc(s.xr_done, 1)
                    for n in range(10):
                        t, h = divmod(n, 2)
                        r = TOKT[t][1]
                        dve.wait_ge(tr_done, n + 1)
                        dve.tensor_copy(y[0:r, t, h * 512:(h + 1) * 512], pt[n % 2][0:r, 0, :]).then_inc(ya_done, 1)

                @block.tensor
                def _(pe):
                    norm_tensor(pe, s, sq, pst, ones)
                    pe.wait_ge(s.xr_done, DC)
                    for n in range(10):
                        t, h = divmod(n, 2)
                        t0, r = TOKT[t]
                        if n >= 2:
                            pe.wait_ge(ya_done, n - 1)
                        for k in range(4):
                            mm = pe.transpose(pt[n % 2][0:r, 0, k * P:(k + 1) * P], x[:, 4 * h + k, t0:t0 + r], ident[:, :])
                        mm.then_inc(tr_done, 1)

        def proj_stage(l, pj):
            names = Weights.NAMES + NormSems.NAMES + ("ev_done", "n_out")
            with stage(nc, *names) as sems, ExitStack() as st:
                s = NormSems(sems[5:15])
                ev_done, n_out = sems[15:]
                wt = Weights(nc, st, sems[0:5], DC)
                nhi, nlo = (sb(n, [P, DC, T], F32R, at=st) for n in ("nhi", "nlo"))
                sq, tmp, nf, rs = norm_buffers(st)
                pp = [ps(f"pp{i}", 2, st) for i in range(2)]
                pst = ps("pst", 2, st)
                block = st.enter_context(nc.Block())
                w = a["w_in"][l]
                UQ, UK, UH, UG = 0, R // 2, (R + NKV) // 2, (R + NKV) // 2 + 8

                @block.sync
                def _(sp):
                    with sp.Fori(0, R // 2) as u:
                        for slot in range(2):
                            src = [w[:, bass.ds(u * 2 * DH + slot * DH + g * R * DH, DH)].rearrange("(k p) n -> p k n", p=P)
                                   for g in range(GROUPS)]
                            raw = wt.raw[slot]
                            wt.load(sp, u + UQ, slot, [(raw[:, :, 0:DH], src[0]), (raw[:, 0:4, DH:P], src[1][:, 0:4, :]),
                                                       (raw[:, 4:8, DH:P], src[1][:, 4:8, :])])
                    for n, u0, col in ((NKV // 2, UK, C_KV), (8, UH, C_HG)):
                        with sp.Fori(0, n) as u:
                            for slot in range(2):
                                wt.load(sp, u + u0, slot, wt.columns(slot, DC, w[:, bass.ds(u * 256 + (slot * P + col), P)]))
                    wt.load(sp, UG, 0, wt.columns(0, DC, w[:, C_GATE:C_GATE + P]))

                @block.scalar
                def _(act):
                    norm_scalar(act, s, wt, x, sq, pst, eps, tmp, nf, rs, mods, 1, nhi)
                    act.wait_ge(s.nl_done, DC)
                    for n, part in enumerate((nhi, nlo)):
                        act.dma_start(n_dram[n], part[:, :, :].rearrange("p c t -> p (c t)").bitcast(F32)).then_inc(n_out, 16)
                    with act.Fori(1, UG) as u:
                        for slot in range(2):
                            wt.split_hi(act, u, slot, DC)
                    wt.split_hi(act, UG, 0, DC)
                    act.wait_ge(n_out, 32)

                @block.vector
                def _(dve):
                    dve.sem_inc(ev_done, 2)
                    wt.credit_vector(dve)
                    for slot in range(2):
                        wt.split_lo(dve, 0, slot, DC)
                    norm_vector(dve, s, x, tmp, nf, rs, mods, 1, nhi, nlo)

                    def evacuate(u, slot, chunk, scale):
                        dve.wait_ge(wt.mm_done, 2 * u + (slot + 3))
                        dve.tensor_scalar(pj[:, bass.ds(chunk, 1), :].rearrange("p o (h t) -> p (o h) t", h=2),
                                          pp[slot][:, :, 0:HALF], scale, None, ALU.mult).then_inc(ev_done, 1)

                    for n, u0, chunk, scale in ((R // 2, UQ, Q0, DH ** -0.5), (NKV // 2, UK, KV0, 1.0), (8, UH, HQ0, 1.0)):
                        def pair(u, last):
                            for slot in range(2):
                                if not (last and u0 == UH and slot == 1):
                                    wt.split_lo(dve, u + (u0 + 1), slot, DC)
                                evacuate(u + u0, slot, 2 * u + (chunk + slot), scale)
                        peeled(dve, n, 1, pair)
                    evacuate(UG, 0, GATE0, 1.0)

                @block.tensor
                def _(pe):
                    wt.credit_tensor(pe)
                    norm_tensor(pe, s, sq, pst, ones)
                    wt.first_products(pe, pp, nhi, nlo, DC, s.nl_done)
                    with pe.Fori(1, UG) as u:
                        for slot in range(2):
                            pe.wait_ge(ev_done, 2 * u + (slot + 1))
                            wt.product(pe, u, slot, pp[slot], nhi, nlo, DC)
                    pe.wait_ge(ev_done, 2 * UG + 1)
                    wt.product(pe, UG, 0, pp[0], nhi, nlo, DC)

        def rows_stage(l, pj, kvn, gn, kct, vcn):
            NM = CMP_STRIDE // 2
            with stage(nc, "sig_done", "rt_done", "va_done", "sc_done", "out_done", "gate_out", "rows0", "rows1", "rows2",
                       "rows3", "w_in", "tr_done", "ca_done", "cb_done", "silu_done", "o_done", "oe_done", "x_done") as (
                    sig_done, rt_done, va_done, sc_done, out_done, gate_out, rows0, rows1, rows2, rows3, w_in, tr_done,
                    ca_done, cb_done, silu_done, o_done, oe_done, x_done), ExitStack() as st:
                rows_in = [rows0, rows1, rows2, rows3]
                cn = [sb(f"cn{i}", [P, NPAGE, 2, P], at=st) for i in range(4)]
                ct = sb("ct", [P, 2, GROUPS, NM, NSEQ, NSUB], at=st)
                w1 = sb("w1", [P, 2, 2, NM, P], at=st)
                w2 = sb("w2", [P, 2, DH], at=st)
                sh = sb("sh", [P, 2, NSEQ * NCMP], at=st)
                pt = [ps(f"pt{i}", 1, st) for i in range(2)]
                ph = [ps(f"ph{i}", 1, st) for i in range(2)]
                po = [ps(f"po{i}", 2, st) for i in range(2)]
                pa, pb = ph, po
                block = st.enter_context(nc.Block())

                def load_rows(sp, b):
                    if b >= 4:
                        sp.wait_ge(tr_done, 2 * (b - 3))
                    for n in range(NPAGE):
                        page = sp.value_load(pages[0:1, NPAGE * b + n:NPAGE * b + n + 1], min_val=0, max_val=NPOOL - 1)
                        sp.dma_start(cn[b % 4][:, n, :, :], a["cache_nsa_kv"][l][bass.ds(page, 1), :, 0:2].rearrange(
                            "o p k g d -> (o p) k (g d)")).then_inc(rows_in[b % 4], 16)

                @block.sync
                def _(sp):
                    load_rows(sp, 0)
                    sp.wait_ge(sig_done, 1)
                    sp.dma_start(gate_dram.rearrange("b g i -> g b i"), pj[0:3 * HEADS, GATE0, SEQ:T].rearrange("g (b i) -> g b i", i=NI)).then_inc(gate_out, 16)
                    for b in range(1, 4):
                        load_rows(sp, b)
                    for kv in range(2):
                        for j in range(2):
                            sp.dma_start(w1[j * DH:(j + 1) * DH, kv, :, :, :],
                                         a["cmp_w1"][l, kv, :, j::2].rearrange("r m d e -> d r m e")).then_inc(w_in, 16)
                        sp.dma_start(w2[:, kv, :], a["cmp_w2"][l, kv]).then_inc(w_in, 16)
                    for b in range(4, NB):
                        load_rows(sp, b)
                    sp.wait_ge(va_done, 5)
                    sp.wait_ge(sc_done, 5)
                    sp.dma_start(o["kv_p"][l, 0].rearrange("(t p) k g d -> p t (k g d)", p=P), kvn[:, 0:4, 0:512]).then_inc(out_done, 16)
                    sp.dma_start(o["win_p"][l, 0].rearrange("(t p) k g d -> p t (k g d)", p=P), kvn[:, 0:4, 512:768]).then_inc(out_done, 16)
                    sp.dma_start(o["kv_s"][l].rearrange("b i k g d -> (b i) (k g d)"), kvn[0:NSMP, 4, 0:512]).then_inc(out_done, 16)
                    for b in range(NB):
                        sp.dma_start(o["win_s"][l, b, PAST - NI:PAST].rearrange("i k g d -> i (k g d)"),
                                     kvn[NI * b:NI * b + NI, 4, 512:768]).then_inc(out_done, 16)
                    sp.wait_ge(out_done, 16 * (3 + NB))
                    sp.wait_ge(gate_out, 16)

                def gather(engine, g, done):
                    rows = slice(g * DH, (g + 1) * DH)
                    for s in (NSEQ - 1, *range(NB)):
                        for kv in range(2):
                            if s < NB:
                                engine.wait_ge(tr_done, 2 * s + kv + 1)
                                src = pt[kv][rows, 0, :]
                            else:
                                src = pj[rows, KV0 + kv, 0:SEQ]
                            for parity in range(2):
                                dst, v = ct[parity * DH:(parity + 1) * DH, kv, g, :, s, :], strided(src[:, parity:], [2, NM], [CMP_STRIDE, NSUB])
                                if g == 0:
                                    ins = engine.activation(dst, v, ACT.Copy)
                                else:
                                    ins = engine.tensor_copy(dst, v)
                            ins.then_inc(done, 1)

                @block.tensor
                def _(pe):
                    pe.wait_ge(sig_done, 1)
                    for t, (t0, r) in enumerate(TOKT):
                        if t >= 2:
                            pe.wait_ge(va_done, t - 1)
                            pe.wait_ge(sc_done, t)
                        for c in range(4):
                            pe.transpose(pa[t % 2][0:r, 0, c * P:(c + 1) * P], pj[:, KV0 + c, t0:t0 + r], ident[:, :])
                        for c in range(2):
                            mm = pe.transpose(pb[t % 2][0:r, 0, c * P:(c + 1) * P], pj[:, KV0 + 4 + c, t0:t0 + r], ident[:, :])
                        if t < 4:
                            mm = pe.transpose(pb[t % 2][0:r, 0, 256:280], pj[0:24, GATE0, t0:t0 + r], ident[0:24, 0:24])
                        mm.then_inc(rt_done, 1)

                    for b in range(NB):
                        pe.wait_ge(rows_in[b % 4], 64 * (b // 4 + 1))
                        for kv in range(2):
                            if b >= 1:
                                pe.wait_ge(ca_done, 2 * b + kv + 1)
                                pe.wait_ge(cb_done, 2 * b + kv + 1)
                            for n in range(NPAGE):
                                mm = pe.transpose(pt[kv][:, 0, n * P:(n + 1) * P], cn[b % 4][:, n, kv, :], ident[:, :])
                            mm.then_inc(tr_done, 1)

                    def hidden(q):
                        kv, g = divmod(q, 2)
                        if q >= 2:
                            pe.wait_ge(silu_done, q - 1)
                        for m in range(NM):
                            for r in range(2):
                                mm = pe.matmul(ph[q % 2][:, 0, 0:NSEQ * NCMP].rearrange("p (s n) -> p s n", n=NCMP),
                                               w1[:, kv, r, m, :], ct[:, kv, g, m, :, r:r + NCMP], start=(m == 0 and r == 0),
                                               stop=(m == NM - 1 and r == 1))
                        mm.then_inc(x_done, 1)

                    def output(q):
                        kv, g = divmod(q, 2)
                        pe.wait_ge(silu_done, q + 1)
                        if q >= 2:
                            pe.wait_ge(oe_done, q - 1)
                        if kv == 0:
                            mm = pe.matmul(po[q % 2][g * DH:(g + 1) * DH, 0, 0:NSEQ * NCMP], w2[:, 0, :], sh[:, q % 2, :],
                                           start=True, stop=True)
                        else:
                            for b in range(NSEQ):
                                mm = pe.matmul(po[q % 2][0:NCMP, b // NB, (b % NB) * DH:(b % NB) * DH + DH],
                                               sh[:, q % 2, b * NCMP:(b + 1) * NCMP], w2[:, 1, :], start=True, stop=True)
                        mm.then_inc(o_done, 1)

                    pe.wait_ge(w_in, 16 * 6)
                    pe.wait_ge(va_done, 5)
                    pe.wait_ge(sc_done, 5)
                    pe.wait_ge(ca_done, 2 * NSEQ)
                    hidden(0)
                    pe.wait_ge(cb_done, 2 * NSEQ)
                    hidden(1)
                    output(0)
                    hidden(2)
                    output(1)
                    hidden(3)
                    output(2)
                    output(3)

                @block.vector
                def _(dve):
                    for t, (t0, r) in enumerate(TOKT):
                        dve.wait_ge(rt_done, t + 1)
                        dve.tensor_copy(kvn[0:r, t, 0:512], pa[t % 2][0:r, 0, :]).then_inc(va_done, 1)
                    gather(dve, 1, cb_done)
                    for q in range(4):
                        kv, g = divmod(q, 2)
                        dve.wait_ge(o_done, q + 1)
                        if kv == 0:
                            src = po[q % 2][g * DH:(g + 1) * DH, 0, 0:NSEQ * NCMP]
                            b2 = vecs[g * DH:(g + 1) * DH, bass.ds(60 + l * 2, 1)]
                            dve.tensor_scalar(kct[g * DH:(g + 1) * DH, :], src, b2, None, ALU.add).then_inc(oe_done, 1)
                        else:
                            row = b2row[0:NCMP, bass.ds(l, 1), :]
                            dve.tensor_tensor(vcn[:, 0:NB, g * DH:(g + 1) * DH],
                                              po[q % 2][0:NCMP, 0, :].rearrange("p (b d) -> p b d", d=DH),
                                              strided(row, [0, NB], [1, DH]), ALU.add)
                            dve.tensor_tensor(vcn[:, NB, g * DH:(g + 1) * DH], po[q % 2][0:NCMP, 1, 0:DH], row[:, 0, :],
                                              ALU.add).then_inc(oe_done, 1)

                @block.scalar
                def _(act):
                    gate = pj[0:24, GATE0, :]
                    act.activation(gate, gate, ACT.Sigmoid).then_inc(sig_done, 1)
                    for t, (t0, r) in enumerate(TOKT):
                        act.wait_ge(rt_done, t + 1)
                        act.activation(kvn[0:r, t, 512:768], pb[t % 2][0:r, 0, 0:256], ACT.Copy).then_inc(sc_done, 1)
                        if t < 4:
                            act.activation(gn[0:r, t, :], pb[t % 2][0:r, 0, 256:280], ACT.Copy)
                    gather(act, 0, ca_done)
                    for q in range(4):
                        act.wait_ge(x_done, q + 1)
                        if q >= 2:
                            act.wait_ge(o_done, q - 1)
                        act.activation(sh[:, q % 2, :], ph[q % 2][:, 0, 0:NSEQ * NCMP], ACT.Silu,
                                       bias=vecs[:, bass.ds(56 + l * 2 + q // 2, 1)]).then_inc(silu_done, 1)

        def load_sequence(sp, l, b, kv, done):
            for n in range(NPAGE):
                page = sp.value_load(pages[0:1, NPAGE * b + n:NPAGE * b + n + 1], min_val=0, max_val=NPOOL - 1)
                src = a["cache_nsa_kv"][l][bass.ds(page, 1)].rearrange("o (p t) k g d -> (o p) t (k g d)", t=4)
                sp.dma_start(kv[32 * n:32 * n + 32, b % 4, 0, :, :], src[:, :, 2 * P:4 * P]).then_inc(done, 16)
            sp.dma_start(kv[:, b % 4, 1, :, :], a["state_win_kv"][l, b].rearrange("(p t) k g d -> p t (k g d)", t=4)).then_inc(done, 16)

        def attention_stage(l, pj, kvn, gn, kct, vcn, oa, kv):
            NU = 8
            with stage(nc, "kv_in", "q_done", "tz_in", "s_done", "max_done", "neg_done", "exp_done", "w_done", "p_done", "t_done", "pt_act",
                       "pt_dve", "pv_done", "o_done") as (kv_in, q_done, tz_in, s_done, max_done, neg_done, exp_done, w_done, p_done,
                                                          t_done, pt_act, pt_dve, pv_done, o_done), ExitStack() as st:
                tz = sb("tz", [P, HEADS, SEQ], at=st)
                qs = sb("qs", [P, 2, P], at=st)
                bs = sb("bs", [P, 2, SEQ], at=st)
                sc = sb("sc", [P, 4, 2 * SEQ + 32], at=st)
                pT = sb("pT", [P, 2, 2 * SEQ + P], at=st)
                mx = sb("mx", [P, 4, 3], at=st)
                start = sb("start", [P, 2], at=st)
                begun = sb("begun", [P, 2], at=st)
                neg = sb("neg", [P, 4, 3], at=st)
                rsum = sb("rsum", [P, 4, 3], at=st)
                wgt = sb("wgt", [P, 4, 3], at=st)
                ps_sel, ps_win, ps_cmp, pt_sel, pt_win, pt_cmp = (ps(n, 1, st) for n in ("ss", "sw", "sc", "ts", "tw", "tc"))
                po = [ps(f"po{i}", 1, st) for i in range(2)]
                block = st.enter_context(nc.Block())

                def unit(k):
                    g, qi = divmod(k % NU, 4)
                    return g, qi, P * (qi + 1), 7 + 8 * qi

                @block.sync
                def _(sp):
                    sp.dma_start(tz[:, :, :], bass.AP(rv_dram.tensor, rv_dram.offset + P - 1, [[639, P], [640 * P, HEADS], [1, SEQ]])).then_inc(tz_in, 16)
                    for b in range(NB // 2):
                        load_sequence(sp, l, b, kv, kv_in)
                    sp.wait_ge(kv_in, 80 * (NB // 2))

                @block.tensor
                def _(pe):
                    def scores(r, k):
                        g, qi, w, nc_ = unit(k)
                        rows = slice(g * DH, (g + 1) * DH)
                        q = qs[rows, k % 2, :]
                        pe.wait_ge(q_done, 2 * (NU * r + k) + 1)
                        pe.wait_ge(max_done, 3 * (NU * r + k) + 3)
                        pe.matmul(ps_cmp[:, 0, 0:nc_], q, kct[rows, NB * NCMP:NB * NCMP + nc_], start=True, stop=True)
                        pe.matmul(ps_sel[:, 0, 0:w], q, pj[rows, KV0 + 2, 0:w], start=True, stop=True)
                        pe.matmul(ps_win[:, 0, 0:w], q, pj[rows, KV0 + 4, 0:w], start=True, stop=True).then_inc(s_done, 1)

                    def turn(r, k):
                        g, qi, w, nc_ = unit(k)
                        u = NU * r + k
                        pe.wait_ge(p_done, 3 * u + 3)
                        pe.wait_ge(pt_act, u + 1)
                        pe.wait_ge(pt_dve, 2 * u + 2)
                        pe.transpose(pt_cmp[0:nc_, 0, 0:P], sc[:, k % 4, 2 * SEQ:2 * SEQ + nc_], ident[:, :])
                        for half, out in ((0, pt_sel), (1, pt_win)):
                            for t in range(qi + 1):
                                mm = pe.transpose(out[:, 0, t * P:(t + 1) * P], sc[:, k % 4, half * SEQ + t * P:half * SEQ + (t + 1) * P], ident[:, :])
                        mm.then_inc(t_done, 1)

                    def values(r, k):
                        g, qi, w, nc_ = unit(k)
                        u = NU * r + k
                        pe.wait_ge(pt_act, u + 2)
                        pe.wait_ge(pt_dve, 2 * u + 4)
                        pe.wait_ge(o_done, u + 1)
                        out = po[k % 2][g * DH:(g + 1) * DH, 0, 0:P]
                        pe.matmul(out, vcn[0:nc_, NB, g * DH:(g + 1) * DH], pT[0:nc_, k % 2, 2 * SEQ:], start=True, stop=False)
                        for half, col in ((0, 3 * P), (1, 5 * P)):
                            for t in range(qi + 1):
                                mm = pe.matmul(out, kvn[:, t, col + g * DH:col + (g + 1) * DH], pT[:, k % 2, half * SEQ + t * P:half * SEQ + (t + 1) * P],
                                               start=False, stop=(half == 1 and t == qi))
                        mm.then_inc(pv_done, 1)

                    def head(r, last):
                        for k in range(NU):
                            if k + 2 < NU or not last:
                                scores(r, k + 2)
                            if k >= 1:
                                values(r, k - 1)
                            turn(r, k)
                        values(r, NU - 1)

                    scores(0, 0)
                    scores(0, 1)
                    peeled(pe, R, 1, head)

                @block.vector
                def _(dve):
                    dve.sem_inc(max_done, 3)
                    dve.sem_inc(pt_dve, 2)
                    dve.sem_inc(w_done, 6)

                    def maxima(r, k):
                        g, qi, w, nc_ = unit(k)
                        u = NU * r + k
                        i = k % 4
                        dve.wait_ge(q_done, 2 * u + 2)
                        dve.wait_ge(s_done, u + 1)
                        dve.wait_ge(t_done, u + 1)
                        dve.memset(start[:, k % 2:k % 2 + 1], 0.0)
                        for n, (dst, src, b, lo, width) in enumerate((
                                (2 * SEQ, ps_cmp, bs[:, k % 2, 31:w:16], 2, nc_),
                                (0, ps_sel, bs[:, k % 2, 0:w], 0, w),
                                (SEQ, ps_win, bs[:, k % 2, 0:w], 1, w))):
                            dve.tensor_tensor_reduce(sc[:, i, dst:dst + width], src[:, 0, 0:width], b, 1.0, 3 * FLOOR, ALU.add,
                                                     ALU.max, mx[:, i, lo:lo + 1]).then_inc(max_done, 1)
                        dve.wait_ge(max_done, 3 * u + 6)
                        dve.tensor_scalar(neg[:, i, :], mx[:, i, :], FLOOR, -1.0, ALU.max, ALU.mult).then_inc(neg_done, 1)

                    def weigh(r, k):
                        g, qi, w, nc_ = unit(k)
                        u = NU * r + k
                        i = k % 4
                        dve.wait_ge(exp_done, 3 * u + 3)
                        dve.tensor_scalar(wgt[:, i, :], rsum[:, i, :], 1e-30, None, ALU.max).then_inc(w_done, 1)
                        dve.wait_ge(w_done, 3 * u + 7)
                        dve.reciprocal(wgt[:, i, :], wgt[:, i, :]).then_inc(w_done, 1)
                        dve.wait_ge(w_done, 3 * u + 8)
                        gate = gn[:, qi, bass.ds(r + g * R, 17)]
                        dve.tensor_tensor(wgt[:, i, :], wgt[:, i, :], strided(gate, [HEADS, 3]), ALU.mult).then_inc(w_done, 1)
                        dve.wait_ge(w_done, 3 * u + 9)
                        for dst, br, width in ((2 * SEQ, 0, nc_), (0, 1, w), (SEQ, 2, w)):
                            v = sc[:, i, dst:dst + width]
                            dve.tensor_scalar(v, v, wgt[:, i, br:br + 1], None, ALU.mult).then_inc(p_done, 1)

                    def copy_turned(r, k):
                        g, qi, w, nc_ = unit(k)
                        u = NU * r + k
                        dve.wait_ge(t_done, u + 5)
                        dve.wait_ge(pv_done, u + 1)
                        dve.tensor_copy(pT[0:nc_, k % 2, 2 * SEQ:], pt_cmp[0:nc_, 0, 0:P]).then_inc(pt_dve, 1)
                        dve.tensor_copy(pT[:, k % 2, SEQ:SEQ + w], pt_win[:, 0, 0:w]).then_inc(pt_dve, 1)

                    def head(r, last):
                        for k in range(NU):
                            weigh(r, k)
                            if k + 2 < NU or not last:
                                maxima(r, k + 2)
                            copy_turned(r, k)

                    maxima(0, 0)
                    maxima(0, 1)
                    peeled(dve, R, 1, head)

                @block.scalar
                def _(act):
                    act.sem_inc(pt_act, 1)
                    act.sem_inc(o_done, 2)

                    def exps(r, k):
                        g, qi, w, nc_ = unit(k)
                        u = NU * r + k
                        i = k % 4
                        act.wait_ge(neg_done, u + 1)
                        act.wait_ge(w_done, 3 * u + 1)
                        for dst, n, br, width in ((2 * SEQ, 2, 0, nc_), (0, 0, 1, w), (SEQ, 1, 2, w)):
                            v = sc[:, i, dst:dst + width]
                            act.activation(v, v, ACT.Exp, bias=neg[:, i, n:n + 1], accum_out=rsum[:, i, br:br + 1]).then_inc(exp_done, 1)

                    def copy_turned(r, k):
                        g, qi, w, nc_ = unit(k)
                        u = NU * r + k
                        act.wait_ge(t_done, u + 5)
                        act.wait_ge(pv_done, u + 1)
                        act.activation(pT[:, k % 2, 0:w], pt_sel[:, 0, 0:w], ACT.Copy).then_inc(pt_act, 1)

                    def outputs(r, k):
                        g, qi, w, nc_ = unit(k)
                        u = NU * r + k
                        rows = slice(g * DH, (g + 1) * DH)
                        act.wait_ge(pv_done, u + 3)
                        act.activation(oa[rows, bass.ds(r, 1), qi * P:(qi + 1) * P], po[k % 2][rows, 0, 0:P].unsqueeze(1),
                                       ACT.Copy).then_inc(o_done, 1)

                    def head(r, last):
                        for k in range(NU):
                            if k + 1 < NU or not last:
                                exps(r, k + 1)
                            if k >= 1:
                                outputs(r, k - 1)
                            copy_turned(r, k)
                        outputs(r, NU - 1)

                    exps(0, 0)
                    peeled(act, R, 1, head)

                @block.gpsimd
                def _(pool):
                    pool.sem_inc(t_done, 4)
                    pool.sem_inc(pv_done, 2)
                    pool.wait_ge(tz_in, 16)
                    with pool.Fori(0, R) as r:
                        for k in range(NU):
                            g, qi, w, nc_ = unit(k)
                            pool.wait_ge(max_done, 3 * (NU * r + k) + 1)
                            pool.tensor_tensor(begun[:, k % 2:k % 2 + 1], ones[:, 0:1], ones[:, 0:1], ALU.mult)
                            pool.tensor_copy(qs[:, k % 2, :].unsqueeze(1), pj[:, bass.ds(r, 1), qi * P:(qi + 1) * P]).then_inc(q_done, 1)
                            pool.tensor_copy(bs[:, k % 2, 0:w].unsqueeze(1), tz[:, bass.ds(r + g * R, 1), SEQ - w:SEQ]).then_inc(q_done, 1)

        def sample_stage(l, pj, kvn, kct, vcn, oa, kv):
            with stage(nc, "in0", "in1", "in2", "in3", "gs_in", "win_out", "qbd_done", "kt_done", "ka_done", "kb_done",
                       "s_done", "sa_done", "mx_done", "neg_done", "exp_done", "w_done", "p_done", "t_done", "ta_done",
                       "tb_done", "pv_done", "o_done", "sq_done") as (
                    in0, in1, in2, in3, gs_in, win_out, qbd_done, kt_done, ka_done, kb_done, s_done, sa_done, mx_done,
                    neg_done, exp_done, w_done, p_done, t_done, ta_done, tb_done, pv_done, o_done, sq_done), ExitStack() as st:
                rows_in = [in0, in1, in2, in3]
                kT = sb("kT", [P, 2, 2, PAST], at=st)
                qbd = sb("qbd", [P, NB, GROUPS, R, NI], at=st)
                gs = sb("gs", [P, 2, 3], at=st)
                sc = [sb("sc", [P, 2, PAST + NSMP], at=st), pj[:, Q0:Q0 + 2, :]]
                scc = sb("scc", [P, 2, 32], at=st)
                pT = sb("pT", [P, 2, 5, P], at=st)
                pTc = sb("pTc", [32, P], at=st)
                mx = sb("mx", [P, 2, 5], at=st)
                m3 = sb("m3", [P, 2, 3], at=st)
                rsum = sb("rsum", [P, 2, 3], at=st)
                wgt = sb("wgt", [P, 2, 3], at=st)
                pk = [ps(f"pk{i}", 1, st) for i in range(2)]
                pss = [ps(f"pss{i}", 1, st) for i in range(2)]
                psn = ps("psn", 1, st)
                ptn = ps("ptn", 1, st)
                po = ps("po", 1, st)
                block = st.enter_context(nc.Block())
                probs = [(scc[:, half, 0:NCMP], sc[half][:, 0, :], sc[half][:, 1, :]) for half in range(2)]

                def write_window(sp, b):
                    sp.dma_start(o["win_s"][l, b, 0:PAST - NI].rearrange("(p t) k g d -> p t (k g d)", t=4),
                                 kv[b // 4][1:P, b % 4, 1, :, :]).then_inc(win_out, 16)

                @block.sync
                def _(sp):
                    for b in range(4, NB):
                        load_sequence(sp, l, b, kv[1], rows_in[b % 4])
                        if b == 4:
                            for n in range(NB):
                                sp.dma_start(gs[32 * (n % 4):32 * (n % 4) + 32, n // 4, :],
                                             gate_dram[n].rearrange("(r h) i -> (h i) r", r=3),
                                             allow_slow_non_contiguous=True).then_inc(gs_in, 16)
                    for b in range(NB):
                        if b >= 4:
                            sp.wait_ge(rows_in[b % 4], 80)
                        write_window(sp, b)
                    sp.wait_ge(win_out, 16 * NB)

                @block.tensor
                def _(pe):
                    for half in range(2):
                        for j in range(4):
                            b = 4 * half + j
                            if half:
                                pe.wait_ge(rows_in[j], 80)
                            if half or j:
                                pe.wait_ge(ka_done, b)
                                pe.wait_ge(kb_done, b)
                            for br in range(2):
                                for t in range(4):
                                    mm = pe.transpose(pk[br][:, 0, t * P:(t + 1) * P], kv[half][:, j, br, t, 0:P], ident[:, :])
                            mm.then_inc(kt_done, 1)
                            pe.wait_ge(ka_done, b + 1)
                            pe.wait_ge(kb_done, b + 1)
                            pe.wait_ge(qbd_done, 2)
                            if half and j == 0:
                                pe.wait_ge(sa_done, 5)
                            rows = slice(32 * j, 32 * j + 32)
                            q = qbd[:, b, :, :, :]
                            for br in range(2):
                                pe.matmul(pss[br][rows, 0, :], q, kT[:, b % 2, br, :], start=True, stop=True)
                            for br in range(2):
                                pe.matmul(psn[rows, 0, br * NSMP:(br + 1) * NSMP], q, pj[:, KV0 + 2 + 2 * br, SEQ:T], start=True, stop=True)
                            mm = pe.matmul(psn[rows, 0, 64:64 + NCMP], q, kct[:, b * NCMP:(b + 1) * NCMP], start=True, stop=True)
                            mm.then_inc(s_done, 1)
                    for half in range(2):
                        pe.wait_ge(p_done, 3 * (half + 1))
                        if half:
                            pe.wait_ge(ta_done, 1)
                            pe.wait_ge(tb_done, 1)
                        for br in range(2):
                            for t in range(4):
                                pe.transpose(pk[br][:, 0, t * P:(t + 1) * P], sc[half][:, br, t * P:(t + 1) * P], ident[:, :])
                        for br in range(2):
                            pe.transpose(ptn[0:NSMP, 0, br * P:(br + 1) * P], sc[half][:, br, PAST:PAST + NSMP], ident[:, :])
                        mm = pe.transpose(ptn[0:NCMP, 0, 2 * P:3 * P], scc[:, half, 0:NCMP], ident[:, :])
                        mm.then_inc(t_done, 1)
                        pe.wait_ge(ta_done, half + 1)
                        pe.wait_ge(tb_done, half + 1)
                        if half:
                            pe.wait_ge(o_done, 2)
                        for j in range(4):
                            b = 4 * half + j
                            cols = slice(32 * j, 32 * j + 32)
                            out = po[:, 0, cols]
                            pe.matmul(out, vcn[0:NCMP, b, :], pTc[0:NCMP, cols], start=True, stop=False)
                            for br in range(2):
                                for t in range(4):
                                    pe.matmul(out, kv[half][:, j, br, t, P:2 * P], pT[:, br, t, cols], start=False, stop=False)
                                mm = pe.matmul(out, kvn[0:NSMP, 4, (3 + 2 * br) * P:(4 + 2 * br) * P], pT[0:NSMP, br, 4, cols],
                                               start=False, stop=(br == 1))
                        mm.then_inc(pv_done, 1)

                @block.vector
                def _(dve):
                    dve.memset(qbd[:, :, :, :, :], 0.0).then_inc(sq_done, 1)
                    dve.wait_ge(sq_done, 1)
                    for g in range(GROUPS):
                        rows = slice(g * DH, (g + 1) * DH)
                        dve.tensor_copy(qbd[rows, :, g, :, :], pj[rows, Q0:Q0 + R, SEQ:T].rearrange("p r (b i) -> p b r i", i=NI)).then_inc(qbd_done, 1)

                    def maxima(half):
                        for j in range(4):
                            b = 4 * half + j
                            dve.wait_ge(kt_done, b + 1)
                            if b >= 2:
                                dve.wait_ge(s_done, b - 1)
                            dve.tensor_copy(kT[:, b % 2, 1, :], pk[1][:, 0, :]).then_inc(kb_done, 1)
                        dve.wait_ge(s_done, 4 * half + 4)
                        for n, (out, src, bias) in enumerate((
                                (scc[:, half, 0:NCMP], psn[:, 0, 64:64 + NCMP], bias_cmp[:, :]),
                                (sc[half][:, 0, 0:PAST], pss[0][:, 0, :], bias_old[:, 0, :]),
                                (sc[half][:, 1, 0:PAST], pss[1][:, 0, :], bias_old[:, 1, :]),
                                (sc[half][:, 0, PAST:PAST + NSMP], psn[:, 0, 0:NSMP], bias_new[:, half, :]),
                                (sc[half][:, 1, PAST:PAST + NSMP], psn[:, 0, NSMP:2 * NSMP], bias_new[:, half, :]))):
                            dve.tensor_tensor_reduce(out, src, bias, 1.0, 3 * FLOOR, ALU.add, ALU.max, mx[:, half, n:n + 1]).then_inc(sa_done, 1)
                        dve.wait_ge(sa_done, 5 * half + 5)
                        dve.tensor_copy(m3[:, half, 0:1], mx[:, half, 0:1]).then_inc(mx_done, 1)
                        dve.tensor_tensor(m3[:, half, 1:3], mx[:, half, 1:3], mx[:, half, 3:5], ALU.max).then_inc(mx_done, 1)
                        dve.wait_ge(mx_done, 2 * half + 2)
                        dve.tensor_scalar(m3[:, half, :], m3[:, half, :], FLOOR, -1.0, ALU.max, ALU.mult).then_inc(neg_done, 1)

                    def weigh(half):
                        dve.wait_ge(exp_done, 3 * half + 3)
                        dve.tensor_scalar(wgt[:, half, :], rsum[:, half, :], 1e-30, None, ALU.max).then_inc(w_done, 1)
                        dve.wait_ge(w_done, 3 * half + 1)
                        dve.reciprocal(wgt[:, half, :], wgt[:, half, :]).then_inc(w_done, 1)
                        dve.wait_ge(w_done, 3 * half + 2)
                        dve.wait_ge(gs_in, 16 * NB)
                        dve.tensor_tensor(wgt[:, half, :], wgt[:, half, :], gs[:, half, :], ALU.mult).then_inc(w_done, 1)
                        dve.wait_ge(w_done, 3 * half + 3)
                        for br in range(3):
                            v = probs[half][br]
                            dve.tensor_scalar(v, v, wgt[:, half, br:br + 1], None, ALU.mult).then_inc(p_done, 1)

                    def copy_turned(half):
                        dve.wait_ge(t_done, half + 1)
                        if half:
                            dve.wait_ge(pv_done, 1)
                        dve.tensor_copy(pT[0:NSMP, :, 4, :], ptn[0:NSMP, 0, 0:2 * P].rearrange("p (b q) -> p b q", b=2))
                        dve.tensor_copy(pTc[0:NCMP, :], ptn[0:NCMP, 0, 2 * P:3 * P])
                        dve.tensor_copy(pT[:, 1, 0:4, :], pk[1][:, 0, :].rearrange("p (t q) -> p t q", t=4)).then_inc(tb_done, 1)

                    def outputs(half):
                        dve.wait_ge(pv_done, half + 1)
                        for g in range(GROUPS):
                            rows = slice(g * DH, (g + 1) * DH)
                            for j in range(4):
                                b = 4 * half + j
                                ins = dve.tensor_copy(oa[rows, 0:R, SEQ + NI * b:SEQ + NI * b + NI],
                                                      po[rows, 0, 32 * j + 16 * g:32 * j + 16 * g + 16].rearrange("p (r i) -> p r i", i=NI))
                            ins.then_inc(o_done, 1)

                    maxima(0)
                    weigh(0)
                    maxima(1)
                    weigh(1)
                    copy_turned(0)
                    outputs(0)
                    copy_turned(1)
                    outputs(1)

                @block.scalar
                def _(act):
                    for half in range(2):
                        for j in range(4):
                            b = 4 * half + j
                            act.wait_ge(kt_done, b + 1)
                            if b >= 2:
                                act.wait_ge(s_done, b - 1)
                            act.activation(kT[:, b % 2, 0, :], pk[0][:, 0, :], ACT.Copy).then_inc(ka_done, 1)
                        act.wait_ge(neg_done, half + 1)
                        for br in range(3):
                            v = probs[half][br]
                            act.activation(v, v, ACT.Exp, bias=m3[:, half, br:br + 1], accum_out=rsum[:, half, br:br + 1]).then_inc(exp_done, 1)
                    for half in range(2):
                        act.wait_ge(t_done, half + 1)
                        if half:
                            act.wait_ge(pv_done, 1)
                        act.activation(pT[:, 0, 0:4, :], pk[0][:, 0, :].rearrange("p (t q) -> p t q", t=4), ACT.Copy).then_inc(ta_done, 1)

        def hgrn_stage(l, pj, ob, nhi, nlo):
            NL = len(LEVELS) - 1
            W = HG * T
            with stage(nc, "sin", "mask_in", "sig_done", "aff_done", "ln_done", "set_done", "b_done", "d_done", "e_done",
                       "g_done", "a_done", "cp_done", "tr_done", "ie_done", "qe_done", "kt_done", "ke_done", "po_done",
                       "oe_done", "st_done", "su_done", "kd_done", "sp_done", "ss_done", "out_done", "sq_done", "n_done",
                       "r_done", "mul_done", "hv_done", "n_in", "l_done") as (
                    sin, mask_in, sig_done, aff_done, ln_done, set_done, b_done, d_done, e_done, g_done, a_done, cp_done,
                    tr_done, ie_done, qe_done, kt_done, ke_done, po_done, oe_done, st_done, su_done, kd_done, sp_done,
                    ss_done, out_done, sq_done, n_done, r_done, mul_done, hv_done, n_in, l_done), ExitStack() as st:
                q, k, g = (pj[:, c:c + HG, :] for c in (HQ0, HF0, HO0))
                f1 = sb("f1", [P, HG, T], at=st)
                bc = sb("bc", [P, HG, T], at=st)
                g1 = sb("g1", [P, HG, T], at=st)
                dd = [f1[:, :, :], pj[:, 0:4, :]]
                gg = [pj[:, 4:8, :], g1[:, :, :]]
                rows = sb("rows", [P, 5, HG * P], at=st)
                at = sb("at", [P, 4, HG, P], at=st)
                ats = sb("ats", [NSMP, HG, NSMP], at=st)
                keep = sb("keep", [P, T], at=st)
                state = sb("state", [P, HG, P], at=st)
                ss = sb("ss", [P, NB, HG, P], at=st)
                level = sb("level", [P, len(LEVELS), P], at=st)
                flat = pj[:, :, :].rearrange("p c t -> p (c t)")
                kn = [flat[:, t * HG * P:(t + 1) * HG * P] for t in range(4)] + [flat[0:NSMP, 8 * T:8 * T + HG * P]]
                kd = [flat[0:NSMP, 8 * T - (i + 1) * 512:8 * T - i * 512] for i in range(2)]
                inv = sb("inv", [P, 5, HG], at=st)
                bank = [ps(f"b{i}", 1, st) for i in range(8)]
                SPREAD = (0, 1, 5, 6, 7)
                block = st.enter_context(nc.Block())

                def tiles(n):
                    return 4 if n < NL and LEVELS[n] > 2 else 5

                def before(n, t=0):
                    return sum(tiles(i) for i in range(n)) + t

                def halves(n):
                    size = LEVELS[n]
                    blocks = (SEQ if size > 2 else T) // (2 * size)
                    return size, [T, HG], [2 * size, blocks], [1, size]

                @block.sync
                def _(sp):
                    sp.dma_start(level[:, :, :], a["c_level"]).then_inc(mask_in, 16)
                    for rows_ in (slice(0, P // 2), slice(P // 2, P)):
                        sp.dma_start(ss[rows_, :, :, :], a["state_hgrn"][l, :, :, rows_].rearrange("b h k v -> k b h v")).then_inc(sin, 16)
                    for n, part in enumerate((nhi, nlo)):
                        sp.dma_start(part[:, :, :].rearrange("p c t -> p (c t)").bitcast(F32), n_dram[n]).then_inc(n_in, 16)
                    sp.wait_ge(su_done, 16)
                    sp.dma_start(o["hg_p"][l, 0].rearrange("h k v -> k h v"), state[:, :, :]).then_inc(out_done, 16)
                    sp.wait_ge(ss_done, 2 * NB)
                    sp.dma_start(o["hg_s"][l].rearrange("b h k v -> k b h v"), ss[:, :, :, :]).then_inc(out_done, 16)
                    sp.wait_ge(out_done, 32)
                    sp.wait_ge(n_in, 32)

                @block.scalar
                def _(act):
                    act.activation(f1[:, :, :], k, ACT.Sigmoid).then_inc(sig_done, 1)
                    act.wait_ge(sig_done, 1)
                    act.activation(k, k, ACT.Sigmoid, scale=-1.0).then_inc(sig_done, 1)
                    for t in range(5):
                        r = TOKT[t][1]
                        act.wait_ge(tr_done, t + 1)
                        act.activation(rows[0:r, t, :], bank[5 + t % 2][0:r, 0, :], ACT.Copy).then_inc(ie_done, 1)
                    act.wait_ge(aff_done, 5)
                    act.activation(f1[:, :, :], f1[:, :, :], ACT.Ln).then_inc(ln_done, 1)
                    act.activation(q, q, ACT.Silu).then_inc(sig_done, 1)
                    act.activation(g, g, ACT.Silu).then_inc(sig_done, 1)
                    for n in range(NL + 2):
                        if n == NL:
                            act.wait_ge(g_done, 2 * NL)
                        else:
                            act.wait_ge(d_done, 2 * min(n, NL) + 2)
                        d = dd[n % 2] if n <= NL else pj[:, 0:4, :]
                        d = f1[:, :, :] if n == NL else d
                        if n < NL and LEVELS[n] > 2:
                            d = d[:, :, 0:SEQ]
                        act.activation(d, bc[:, :, :] if n == NL else d, ACT.Exp).then_inc(e_done, 1)
                    for t in range(5):
                        t0, r = TOKT[t]
                        act.wait_ge(po_done, t + 1)
                        act.activation(ob[:, :, t0:t0 + r], bank[t % 2][:, 0, 0:HG * r].rearrange("p (h t) -> p h t", h=HG),
                                       ACT.Copy).then_inc(oe_done, 1)
                    act.wait_ge(oe_done, 5)
                    act.activation(g1[:, :, :], ob[:, :, :], ACT.Square).then_inc(sq_done, 1)
                    act.wait_ge(n_done, 1)
                    act.activation(inv[:, 0:4, :], bank[2][:, 0, 0:4 * HG].rearrange("p (t h) -> p t h", h=HG), ACT.Sqrt,
                                   bias=eps[:, 0:1], scale=1.0 / P).then_inc(r_done, 1)
                    act.activation(inv[0:NSMP, 4, :], bank[2][0:NSMP, 0, 4 * HG:5 * HG], ACT.Sqrt, bias=eps[0:NSMP, 0:1],
                                   scale=1.0 / P).then_inc(r_done, 1)

                @block.gpsimd
                def _(pool):
                    def differences(n):
                        size, hd, bd, td = halves(n)
                        d = dd[n % 2]
                        last = strided(bc[:, 0, size - 1:], hd, bd, [0, size])
                        if n >= 2:
                            pool.wait_ge(g_done, 2 * n - 2)
                        pool.tensor_tensor(strided(d, hd, bd, td), last, strided(bc[:, :, :], hd, bd, td), ALU.subtract).then_inc(d_done, 1)
                        pool.tensor_tensor(strided(d[:, 0, size:], hd, bd, td), strided(bc[:, 0, size:], hd, bd, td), last, ALU.subtract).then_inc(d_done, 1)

                    pool.wait_ge(b_done, HG)
                    for n in range(NL):
                        differences(n)

                @block.vector
                def _(dve):
                    dve.memset(at[:, :, :, :], 0.0).then_inc(set_done, 1)
                    dve.memset(ats[:, :, :], 0.0).then_inc(set_done, 1)
                    dve.memset(keep[:, :], 1.0).then_inc(set_done, 1)
                    dve.wait_ge(set_done, 3)
                    dve.memset(keep[:, 0:SEQ:P], 0.0).then_inc(set_done, 1)
                    dve.memset(keep[:, SEQ:T:NI], 0.0).then_inc(set_done, 1)
                    dve.wait_ge(sig_done, 1)
                    lbl = lb[:, bass.ds(l, 1), :]
                    oml_l = oml[:, bass.ds(l, 1), :]
                    for h in range(HG):
                        dve.tensor_scalar(f1[:, h, :], f1[:, h, :], oml_l[:, 0, h:h + 1], lbl[:, 0, h:h + 1], ALU.mult, ALU.add).then_inc(aff_done, 1)
                    dve.wait_ge(aff_done, 4)
                    dve.tensor_scalar(f1[:, :, :], f1[:, :, :], 2.0 ** -64, None, ALU.max).then_inc(aff_done, 1)
                    dve.wait_ge(sig_done, 2)
                    for h in range(HG):
                        dve.tensor_scalar(k[:, h, :], k[:, h, :], oml_l[:, 0, h:h + 1], None, ALU.mult).then_inc(aff_done, 1)
                    dve.wait_ge(ln_done, 1)
                    dve.wait_ge(set_done, 5)
                    for h in range(HG):
                        dve.tensor_tensor_scan(bc[:, h, :], keep[:, :], f1[:, h, :], 0.0, ALU.mult, ALU.add).then_inc(b_done, 1)
                    dve.wait_ge(b_done, HG)
                    dve.wait_ge(mask_in, 16)

                    def operands(n):
                        size, hd, bd, td = halves(n)
                        d, out = dd[n % 2], gg[n % 2]
                        dve.wait_ge(e_done, n + 1)
                        if n >= 2:
                            dve.wait_ge(a_done, before(n - 1))
                        dve.tensor_tensor(strided(out, hd, bd, td), strided(d, hd, bd, td), strided(k, hd, bd, td), ALU.mult).then_inc(g_done, 1)
                        dve.wait_ge(sig_done, 4)
                        dve.tensor_tensor(strided(out[:, 0, size:], hd, bd, td), strided(d[:, 0, size:], hd, bd, td),
                                          strided(q[:, 0, size:], hd, bd, td), ALU.mult).then_inc(g_done, 1)

                    def select(n):
                        for t in range(tiles(n)):
                            t0, r = TOKT[t]
                            dve.wait_ge(a_done, before(n, t) + 1)
                            dst = at[:, t, :, :] if t < 4 else ats[:, :, :]
                            dve.copy_predicated(dst, strided(level[0:r, n, :].bitcast(U32), [0, HG], [1, r]),
                                                bank[t][0:r, 0, 0:HG * r].rearrange("p (h t) -> p h t", h=HG)).then_inc(cp_done, 1)

                    for n in range(NL):
                        operands(n)
                        if n >= 1:
                            select(n - 1)
                    select(NL - 1)
                    dve.wait_ge(g_done, 2 * NL)
                    for t0, n, c in ((0, SEQ // P, P), (SEQ, NB, NI)):
                        hd, bd, td = [T, HG], [c, n], [1, c]
                        dve.tensor_tensor(strided(pj[:, 0, t0:], hd, bd, td), strided(bc[:, 0, t0 + c - 1:], hd, bd, [0, c]),
                                          strided(bc[:, 0, t0:], hd, bd, td), ALU.subtract).then_inc(d_done, 1)
                    select(NL)
                    dve.wait_ge(e_done, NL + 1)
                    dve.tensor_tensor(g1[:, :, :], q, f1[:, :, :], ALU.mult).then_inc(qe_done, 1)
                    dve.wait_ge(e_done, NL + 2)
                    dve.tensor_tensor(pj[:, 4:8, :], k, pj[:, 0:4, :], ALU.mult).then_inc(qe_done, 1)
                    dve.wait_ge(qe_done, 2)
                    for t in range(5):
                        r = TOKT[t][1]
                        dve.wait_ge(kt_done, t + 1)
                        dve.tensor_copy(kn[t], bank[2 + t % 2][0:r, 0, :]).then_inc(ke_done, 1)
                    for t in range(4):
                        dve.wait_ge(st_done, t + 1)
                        dve.wait_ge(po_done, t + 1)
                        for h in range(HG):
                            new = bank[2 + t % 2][:, 0, h * P:(h + 1) * P]
                            if t == 0:
                                dve.tensor_copy(state[:, h, :], new).then_inc(su_done, 1)
                            else:
                                dve.scalar_tensor_tensor(state[:, h, :], state[:, h, :], f1[:, h, t * P + P - 1:t * P + P], new,
                                                         ALU.mult, ALU.add).then_inc(su_done, 1)
                    dve.wait_ge(sin, 32)
                    dve.wait_ge(po_done, 5)
                    dve.wait_ge(ke_done, 5)

                    def own_rows(b):
                        if b >= 2:
                            dve.wait_ge(sp_done, b - 1)
                        dve.tensor_scalar(kd[b % 2], kn[4], own[:, b:b + 1], None, ALU.mult).then_inc(kd_done, 1)

                    own_rows(0)
                    for b in range(NB):
                        if b + 1 < NB:
                            own_rows(b + 1)
                        decay = strided(f1[:, 0, SEQ + NI * b + NI - 1:], [T, HG], [0, P])
                        dve.tensor_tensor(ss[:, b, :, :], ss[:, b, :, :], decay, ALU.mult).then_inc(ss_done, 1)
                        dve.wait_ge(ss_done, 2 * b + 1)
                        dve.wait_ge(sp_done, b + 1)
                        dve.tensor_tensor(ss[:, b, :, :], ss[:, b, :, :], bank[5 + b % 2][:, 0, :].rearrange("p (h v) -> p h v", h=HG),
                                          ALU.add).then_inc(ss_done, 1)
                    dve.wait_ge(r_done, 2)
                    dve.reciprocal(inv[:, 0:4, :], inv[:, 0:4, :]).then_inc(l_done, 1)
                    dve.reciprocal(inv[0:NSMP, 4, :], inv[0:NSMP, 4, :]).then_inc(l_done, 1)
                    for t, (t0, r) in enumerate(TOKT):
                        dve.wait_ge(n_done, t + 2)
                        dve.tensor_tensor(ob[:, :, t0:t0 + r], ob[:, :, t0:t0 + r],
                                          bank[SPREAD[t]][:, 0, 0:HG * r].rearrange("p (h t) -> p h t", h=HG), ALU.mult).then_inc(mul_done, 1)
                    dve.wait_ge(mul_done, 5)
                    dve.scalar_tensor_tensor(ob[:, :, :], ob[:, :, :], vecs[:, bass.ds(72 + l, 1)], g, ALU.mult, ALU.mult).then_inc(hv_done, 1)

                @block.tensor
                def _(pe):
                    for t in range(5):
                        t0, r = TOKT[t]
                        if t >= 2:
                            pe.wait_ge(ie_done, t - 1)
                        for h in range(HG):
                            mm = pe.transpose(bank[5 + t % 2][0:r, 0, h * P:(h + 1) * P], pj[:, HI0 + h, t0:t0 + r], ident[:, :])
                        mm.then_inc(tr_done, 1)
                    for n in range(NL + 1):
                        if n < NL:
                            pe.wait_ge(g_done, 2 * n + 2)
                            ks, qs = gg[n % 2], gg[n % 2]
                        else:
                            ks, qs = k, q
                        for t in range(tiles(n)):
                            t0, r = TOKT[t]
                            if n >= 1 and t < tiles(n - 1):
                                pe.wait_ge(cp_done, before(n - 1, t) + 1)
                            for h in range(HG):
                                mm = pe.matmul(bank[t][0:r, 0, h * r:(h + 1) * r], ks[:, h, t0:t0 + r], qs[:, h, t0:t0 + r],
                                               start=True, stop=True)
                            mm.then_inc(a_done, 1)
                    pe.wait_ge(qe_done, 2)
                    pe.wait_ge(cp_done, before(NL + 1))
                    for t in range(5):
                        t0, r = TOKT[t]
                        if t >= 2:
                            pe.wait_ge(ke_done, t - 1)
                        for h in range(HG):
                            mm = pe.transpose(bank[2 + t % 2][0:r, 0, h * P:(h + 1) * P], pj[:, 4 + h, t0:t0 + r], ident[:, :])
                        mm.then_inc(kt_done, 1)
                    pe.wait_ge(ie_done, 5)
                    pe.wait_ge(ke_done, 5)
                    pe.wait_ge(sin, 32)
                    for t in range(5):
                        t0, r = TOKT[t]
                        if t >= 2:
                            pe.wait_ge(oe_done, t - 1)
                        if 1 <= t < 4:
                            pe.wait_ge(su_done, 4 * t)
                        for h in range(HG):
                            out = bank[t % 2][:, 0, h * r:(h + 1) * r]
                            if 1 <= t < 4:
                                pe.matmul(out, state[:, h, :], g1[:, h, t0:t0 + r], start=True, stop=False)
                            w = at[:, t, h, :] if t < 4 else ats[:, h, :]
                            mm = pe.matmul(out, rows[0:r, t, h * P:(h + 1) * P], w, start=(t in (0, 4)), stop=(t < 4))
                            if t == 4:
                                for b in range(NB):
                                    mm = pe.matmul(out[:, NI * b:NI * b + NI], ss[:, b, h, :], g1[:, h, SEQ + NI * b:SEQ + NI * b + NI],
                                                   start=False, stop=(b == NB - 1))
                        mm.then_inc(po_done, 1)
                        if t < 4:
                            if t >= 2:
                                pe.wait_ge(su_done, 4 * (t - 1))
                            for h in range(HG):
                                mm = pe.matmul(bank[2 + t % 2][:, 0, h * P:(h + 1) * P], kn[t][:, h * P:(h + 1) * P],
                                               rows[:, t, h * P:(h + 1) * P], start=True, stop=True)
                            mm.then_inc(st_done, 1)
                    for b in range(NB):
                        pe.wait_ge(kd_done, b + 1)
                        if b >= 2:
                            pe.wait_ge(ss_done, 2 * b - 2)
                        for h in range(HG):
                            mm = pe.matmul(bank[5 + b % 2][:, 0, h * P:(h + 1) * P], kd[b % 2][:, h * P:(h + 1) * P],
                                           rows[0:NSMP, 4, h * P:(h + 1) * P], start=True, stop=True)
                        mm.then_inc(sp_done, 1)
                    pe.wait_ge(sq_done, 1)
                    pe.wait_ge(ss_done, 2 * NB)
                    for t, (t0, r) in enumerate(TOKT):
                        for h in range(HG):
                            mm = pe.matmul(bank[2][0:r, 0, t * HG + h:t * HG + h + 1], g1[:, h, t0:t0 + r], ones[:, 0:1],
                                           start=True, stop=True)
                    mm.then_inc(n_done, 1)
                    pe.wait_ge(l_done, 2)
                    for t, (t0, r) in enumerate(TOKT):
                        for h in range(HG):
                            mm = pe.matmul(bank[SPREAD[t]][:, 0, h * r:(h + 1) * r], strided(inv[0:r, t, h:h + 1], [0, P]),
                                           ident[0:r, 0:r], start=True, stop=True)
                        mm.then_inc(n_done, 1)

        def merge_stage(l, oa, ob, nhi, nlo):
            names = Weights.NAMES + ("oh_done", "ol_done", "sg_done", "ta_done", "m_done", "mh_done", "ml_done", "x_done", "res_done")
            with stage(nc, *names) as sems, ExitStack() as st:
                oh_done, ol_done, sg_done, ta_done, m_done, mh_done, ml_done, x_done, res_done = sems[5:]
                wt = Weights(nc, st, sems[0:5], DC)
                ohi, olo, mhi, mlo = (sb(n, [P, DC, T], F32R, at=st) for n in ("ohi", "olo", "mhi", "mlo"))
                sg = sb("sg", [P, 2, T], at=st)
                tt = sb("tt", [P, 2, T], at=st)
                m32 = sb("m32", [P, T], at=st)
                rt = sb("rt", [P, 2, NSMP], at=st)
                pma, pmb, ppa, ppb = (ps(n, 2, st) for n in ("pma", "pmb", "ppa", "ppb"))
                block = st.enter_context(nc.Block())
                two = lambda v: v.rearrange("p (h t) -> p h t", h=2)
                UO = 3 * DC // 2

                @block.sync
                def _(sp):
                    w = a["w_in"][l]
                    with sp.Fori(0, DC // 2) as m:
                        for q in range(2):
                            for kind in range(3):
                                tile = 3 * q + kind
                                u, slot = 3 * m + tile // 2, tile % 2
                                if kind < 2:
                                    col = bass.ds(m * 256 + (q * P + (C_MA, C_MB)[kind]), P)
                                    wt.load(sp, u, slot, wt.columns(slot, DC, w[:, col]))
                                else:
                                    col = bass.ds(m * 256 + q * P, P)
                                    nsa = a["w_branch_nsa"][l].rearrange("(g r d) n -> g d r n", g=GROUPS, r=R)
                                    raw = wt.raw[slot]
                                    wt.load(sp, u, slot, [(raw[g * DH:(g + 1) * DH, 0:R, :], nsa[g][:, :, col]) for g in range(GROUPS)]
                                            + [(raw[:, 4:8, :], a["w_branch_hgrn"][l].rearrange("(k p) n -> p k n", p=P)[:, :, col])])
                    with sp.Fori(0, DC // 2) as c:
                        for slot in range(2):
                            wt.load(sp, c + UO, slot, wt.columns(slot, DC, a["w_out"][l][:, bass.ds(c * 256 + slot * P, P)]))

                @block.scalar
                def _(act):
                    for slot in range(2):
                        wt.split_hi(act, 0, slot, DC)
                    for c, v in ((0, oa), (4, ob)):
                        act.activation(ohi[:, c:c + 4, :], v[:, :, :], ACT.Copy).then_inc(oh_done, 1)
                    with act.Fori(0, DC // 2) as m:
                        for q in range(2):
                            for kind in range(3):
                                tile = 3 * q + kind
                                wt.split_hi(act, 3 * m + tile // 2 + 1, tile % 2, DC)
                                if kind < 2:
                                    act.wait_ge(ta_done, 4 * m + (2 * q + kind + 1))
                                    act.activation(two(sg[:, kind, :]), (pma, pmb)[kind][:, :, 0:HALF], ACT.Sigmoid).then_inc(sg_done, 1)
                            act.wait_ge(m_done, 2 * m + (q + 1))
                            act.activation(mhi[:, bass.ds(2 * m + q, 1), :], m32[:, :].unsqueeze(1), ACT.Copy).then_inc(mh_done, 1)
                    with act.Fori(1, DC // 2) as c:
                        for slot in range(2):
                            wt.split_hi(act, c + UO, slot, DC)

                @block.vector
                def _(dve):
                    dve.sem_inc(sg_done, 2)
                    dve.sem_inc(ta_done, 2)
                    dve.sem_inc(res_done, 2)
                    wt.credit_vector(dve)
                    for slot in range(2):
                        wt.split_lo(dve, 0, slot, DC)
                    for n, (c, v) in enumerate(((0, oa), (4, ob))):
                        dve.wait_ge(oh_done, n + 1)
                        dve.tensor_tensor(olo[:, c:c + 4, :], v[:, :, :], ohi[:, c:c + 4, :].bitcast(F32), ALU.subtract).then_inc(ol_done, 1)
                    with dve.Fori(0, DC // 2) as m:
                        for q in range(2):
                            for kind in range(3):
                                tile = 3 * q + kind
                                wt.split_lo(dve, 3 * m + tile // 2 + 1, tile % 2, DC)
                            dve.wait_ge(sg_done, 4 * m + (2 * q + 4))
                            dve.wait_ge(wt.mm_done, 6 * m + (3 * q + 5))
                            for kind in range(2):
                                dve.tensor_tensor(two(tt[:, kind, :]), two(sg[:, kind, :]), (ppa, ppb)[kind][:, :, 0:HALF],
                                                  ALU.mult).then_inc(ta_done, 1)
                            dve.wait_ge(ta_done, 4 * m + (2 * q + 4))
                            dve.tensor_tensor(m32[:, :], tt[:, 0, :], tt[:, 1, :], ALU.add).then_inc(m_done, 1)
                            dve.wait_ge(mh_done, 2 * m + (q + 1))
                            dve.tensor_tensor(mlo[:, bass.ds(2 * m + q, 1), :], m32[:, :].unsqueeze(1),
                                              mhi[:, bass.ds(2 * m + q, 1), :].bitcast(F32), ALU.subtract).then_inc(ml_done, 1)

                    def chunks(c, last):
                        for slot in range(2):
                            if not last:
                                wt.split_lo(dve, c + (UO + 1), slot, DC)
                            dve.wait_ge(wt.mm_done, 2 * (c + UO) + (slot + 3))
                            residual(dve, (pma, pmb)[slot], 2 * c + slot, 5, rt[:, slot, :], x_done, res_done, 2 * c + (slot + 1))
                    peeled(dve, DC // 2, 1, chunks)

                @block.tensor
                def _(pe):
                    wt.credit_tensor(pe)
                    with pe.Fori(0, DC // 2) as m:
                        for q in range(2):
                            for kind in range(3):
                                tile = 3 * q + kind
                                u, slot = 3 * m + tile // 2, tile % 2
                                if kind == 0:
                                    pe.wait_ge(sg_done, 4 * m + (2 * q + 2))
                                if kind < 2:
                                    wt.product(pe, u, slot, (pma, pmb)[kind], nhi, nlo, DC)
                                else:
                                    pe.wait_ge(ol_done, 2)
                                    pe.wait_ge(ta_done, 4 * m + (2 * q + 2))
                                    wt.product(pe, u, slot, ppa, ohi, olo, R, last=False)
                                    wt.product(pe, u, slot, ppb, ohi[:, 4:8, :], olo[:, 4:8, :], HG, k0=4)
                    pe.wait_ge(ml_done, DC - 2)
                    pe.wait_ge(sg_done, 2 * DC + 2)
                    wt.product(pe, UO, 0, pma, mhi, mlo, DC, landed=ml_done, count=DC)
                    wt.product(pe, UO, 1, pmb, mhi, mlo, DC)
                    with pe.Fori(1, DC // 2) as c:
                        for slot in range(2):
                            pe.wait_ge(res_done, 2 * c + (slot + 1))
                            wt.product(pe, c + UO, slot, (pma, pmb)[slot], mhi, mlo, DC)

        def mixer(l):
            with ExitStack() as outer:
                oa = sb("oa", [P, R, T], at=outer)
                ob = sb("ob", [P, HG, T], at=outer)
                with ExitStack() as inner:
                    pj = sb("pj", [P, NPC, T], at=inner)
                    proj_stage(l, pj)
                    with ExitStack() as nsa:
                        kvn = sb("kvn", [P, 5, NKV * P], at=nsa)
                        gn = sb("gn", [P, 4, 24], at=nsa)
                        kct = sb("kct", [P, NSEQ * NCMP], at=nsa)
                        vcn = sb("vcn", [NCMP, NSEQ, P], at=nsa)
                        rows_stage(l, pj, kvn, gn, kct, vcn)
                        kv = [sb("kv", [P, NB // 2, 2, 4, 2 * P], at=nsa)]
                        attention_stage(l, pj, kvn, gn, kct, vcn, oa, kv[0])
                        kv.append(sb("kv", [P, NB // 2, 2, 4, 2 * P], at=nsa))
                        sample_stage(l, pj, kvn, kct, vcn, oa, kv)
                    nhi, nlo = (outer.enter_context(nc.sbuf_tensor(f"{n}_{nc.next_id()}", [P, DC, T], F32R, side="right"))
                                for n in ("nhi", "nlo"))
                    hgrn_stage(l, pj, ob, nhi, nlo)
                merge_stage(l, oa, ob, nhi, nlo)
        with nc.Fori(0, DEPTH) as l:
            ada_stage(l)
            ffn_stage(l, 0, 0)
            mixer(l)
            ffn_stage(l, 1, 2)
        final_stage()


_INS = ["x_prompt", "x_sample", "cache_nsa_kv", "state_win_kv", "state_hgrn", "page_table", "c_prompt", "c_sample",
        "norm_g", "ada_w", "ada_b", "ffn_w_in", "ffn_w_out", "w_in", "cmp_w1", "cmp_b1", "cmp_w2", "cmp_b2",
        "rel_table", "hgrn_lb_logits", "hgrn_norm_g", "w_branch_nsa", "w_branch_hgrn", "w_out", "final_g"]
_OUTS = {
    "y_p": (1, SEQ, D), "y_s": (NB, NI, D), "kv_p": (DEPTH, 1, SEQ, 4, GROUPS, DH), "kv_s": (DEPTH, NB, NI, 4, GROUPS, DH),
    "win_p": (DEPTH, 1, SEQ, 2, GROUPS, DH), "win_s": (DEPTH, NB, PAST, 2, GROUPS, DH), "hg_p": (DEPTH, 1, HG, P, P),
    "hg_s": (DEPTH, NB, HG, P, P),
}


def kernel(**inputs):
    import concourse.bacc as bacc
    from concourse.bass_utils import run_bass_kernel_spmd

    nc = bacc.Bacc("TRN2", target_bir_lowering=False, num_devices=1)
    arrays = {f"in_{n}": np.ascontiguousarray(inputs[n]) for n in _INS}
    arrays.update({f"in_{n}": np.ascontiguousarray(v) for n, v in shape_constants().items()})
    a = {n[3:]: nc.dram_tensor(n, v.shape, mybir.dt.from_np(v.dtype), kind="ExternalInput").ap()
         for n, v in arrays.items()}
    o = {n: nc.dram_tensor(f"out_{n}", shape, F32, kind="ExternalOutput").ap() for n, shape in _OUTS.items()}
    trunk(nc, a, o)
    r = run_bass_kernel_spmd(nc, [arrays], core_ids=[0])
    return tuple(r.results[0][f"out_{n}"] for n in _OUTS)
```
